# Optimizing a Trainium2 kernel written in Bass

```python
import math
import jax
import jax.numpy as jnp
from jax import lax
import numpy as np

D_MODEL = 1024
BATCH = 1
SEQ = 256
DEPTH = 2

GRID_W = 64
CTX_LEN = 256
N_EVEN = (DEPTH + 1) // 2
N_ODD = DEPTH // 2
N_MOD = 6
NORM_EPS = 1e-6
ROPE_BASE = 10000.0
Q_BLOCK = 128
NEG_INF = -1e30

A_GROUPS = 4
A_GROUP_DIM = 128
A_WIDTH = A_GROUPS * A_GROUP_DIM
CHUNK = 128
B_HEADS = 4
B_HEAD_DIM = 64
B_WIDTH = B_HEADS * 2 * B_HEAD_DIM
EVEN_IN = 2 * A_WIDTH + 3 * B_WIDTH
C_HEADS = 8
C_HEAD_DIM = 64
C_WIDTH = C_HEADS * C_HEAD_DIM
WIN_H = 8
WIN_W = 16
D_HEADS = 4
D_NOPE = 64
D_ROPE = 32
D_VDIM = 128
Q_LORA = 256
KV_LORA = 128
D_WIDTH = D_HEADS * D_VDIM
ODD_IN = 3 * C_WIDTH + Q_LORA + KV_LORA + D_ROPE
MIX_WIDTH = A_WIDTH + B_WIDTH
D_FF = 2816
N_EXPERTS = 8
TOP_K = 2
D_FF_EXPERT = 3584

kernel_name = 'hybrid_diffusion_trunk'

def rmsnorm(x, g):
    xf = x.astype(jnp.float32)
    y = xf * lax.rsqrt(jnp.mean(xf * xf, axis=-1, keepdims=True) + NORM_EPS)
    return (y * g.astype(jnp.float32)).astype(x.dtype)

def layernorm(x, g):
    xf = x.astype(jnp.float32)
    xc = xf - jnp.mean(xf, axis=-1, keepdims=True)
    y = xc * lax.rsqrt(jnp.mean(xc * xc, axis=-1, keepdims=True) + NORM_EPS)
    return (y * g.astype(jnp.float32)).astype(x.dtype)

def modulate(h, shift, scale):
    return h * (1 + scale) + shift

def axial_rope_tables(row, col, dim):
    n_freq = dim // 4
    inv = 1.0 / (ROPE_BASE ** (jnp.arange(n_freq, dtype=jnp.float32) / n_freq))
    ang = jnp.concatenate([row.astype(jnp.float32)[:, None] * inv, col.astype(jnp.float32)[:, None] * inv], axis=-1)
    return jnp.cos(ang), jnp.sin(ang)

def apply_rope(x, cos, sin):
    xf = x.astype(jnp.float32)
    x1, x2 = jnp.split(xf, 2, axis=-1)
    cs, sn = cos[None, :, None, :], sin[None, :, None, :]
    return jnp.concatenate([x1 * cs - x2 * sn, x2 * cs + x1 * sn], axis=-1).astype(x.dtype)

def blocked_attention(q, k, v, map_w, scale):
    bsz, s_len, heads, n_maps, dk = q.shape
    qb = jnp.moveaxis(q.reshape(bsz, s_len // Q_BLOCK, Q_BLOCK, heads, n_maps, dk), 1, 0)
    w = map_w.astype(jnp.float32)

    def one_block(qi):
        s = jnp.einsum('bqhmd,bkhmd->bhmqk', qi, k).astype(jnp.float32) * scale
        p = jnp.einsum('bhmqk,m->bhqk', jax.nn.softmax(s, axis=-1), w)
        return jnp.einsum('bhqk,bkhd->bqhd', p.astype(v.dtype), v)

    out = lax.map(one_block, qb)
    return jnp.moveaxis(out, 0, 1).reshape(bsz, s_len, heads, v.shape[-1])

def chunk_spatial_gating(a, w_s, b_s, g_v):
    u, v = jnp.split(a, 2, axis=-1)
    v = layernorm(v, g_v)
    bsz, s_len, _ = v.shape
    vc = v.reshape(bsz, s_len // CHUNK, CHUNK, A_GROUPS, A_GROUP_DIM)
    mixed = jnp.einsum('gpq,bcqgd->bcpgd', w_s, vc) + b_s.T[None, None, :, :, None]
    return u * mixed.reshape(bsz, s_len, A_WIDTH)

def neighbourhood_attention(q, k, v, k_ctx, v_ctx, rpb, scale):
    bsz, s_len, heads, d = q.shape
    rows = s_len // GRID_W
    kh = min(WIN_H, rows)
    r = jnp.arange(rows)
    row_start = jnp.clip(r - WIN_H // 2, 0, rows - kh)
    ridx = row_start[:, None] + jnp.arange(kh)[None, :]
    qg = q.reshape(bsz, rows, GRID_W, heads, d)
    kg = k.reshape(bsz, rows, GRID_W, heads, d)[:, ridx].reshape(bsz, rows, kh * GRID_W, heads, d)
    vg = v.reshape(bsz, rows, GRID_W, heads, d)[:, ridx].reshape(bsz, rows, kh * GRID_W, heads, d)
    cq = jnp.arange(GRID_W)
    col_start = jnp.clip(cq - WIN_W // 2, 0, GRID_W - WIN_W)
    in_win = (cq[None, :] >= col_start[:, None]) & (cq[None, :] < col_start[:, None] + WIN_W)
    ro = ridx - r[:, None] + (WIN_H - 1)
    co = jnp.clip(cq[None, :] - cq[:, None] + (WIN_W - 1), 0, 2 * WIN_W - 2)
    bias = rpb[:, ro[:, None, :, None], co[None, :, None, :]]
    bias = bias.astype(jnp.float32).reshape(heads, rows, GRID_W, kh * GRID_W)
    mask = jnp.broadcast_to(in_win[:, None, :], (GRID_W, kh, GRID_W)).reshape(GRID_W, kh * GRID_W)
    bias = jnp.where(mask, bias, NEG_INF)
    s_loc = jnp.einsum('brqhd,brkhd->bhrqk', qg, kg).astype(jnp.float32) * scale + bias[None]
    s_ctx = jnp.einsum('brqhd,bkhd->bhrqk', qg, k_ctx).astype(jnp.float32) * scale
    p = jax.nn.softmax(jnp.concatenate([s_loc, s_ctx], axis=-1), axis=-1)
    n_loc = kh * GRID_W
    o = (jnp.einsum('bhrqk,brkhd->brqhd', p[..., :n_loc].astype(v.dtype), vg)
         + jnp.einsum('bhrqk,bkhd->brqhd', p[..., n_loc:].astype(v.dtype), v_ctx))
    return o.reshape(bsz, s_len, heads, d)

def swiglu(h, w1, w3, w2):
    return (jax.nn.silu(h @ w1) * (h @ w3)) @ w2

def moe_swiglu(h, router_w, w1, w3, w2):
    logits = (h @ router_w).astype(jnp.float32)
    top_val, top_idx = lax.top_k(logits, TOP_K)
    gates = jax.nn.softmax(top_val, axis=-1)
    dense_gate = jnp.sum(jax.nn.one_hot(top_idx, N_EXPERTS, dtype=jnp.float32) * gates[..., None], axis=-2).astype(h.dtype)
    out = jnp.zeros_like(h)
    for e in range(N_EXPERTS):
        out = out + dense_gate[..., e:e + 1] * swiglu(h, w1[e], w3[e], w2[e])
    return out

def even_mixer(h, hc, layer, w_in, w_out, sgu_w, sgu_b, sgu_g, lq1, lk1, lq2, lk2, subln_g, rope, need_ctx):
    lam_init = 0.8 - 0.6 * math.exp(-0.3 * layer)
    lam = (jnp.exp(jnp.sum(lq1.astype(jnp.float32) * lk1.astype(jnp.float32)))
           - jnp.exp(jnp.sum(lq2.astype(jnp.float32) * lk2.astype(jnp.float32))) + lam_init)
    map_w = jnp.stack([jnp.ones_like(lam), -lam])
    scale = 1.0 / math.sqrt(B_HEAD_DIM)

    def qkv(p):
        bsz, s_len = p.shape[:2]
        q, k, v = jnp.split(p[..., 2 * A_WIDTH:], 3, axis=-1)
        return (q.reshape(bsz, s_len, 2 * B_HEADS, B_HEAD_DIM),
                k.reshape(bsz, s_len, 2 * B_HEADS, B_HEAD_DIM),
                v.reshape(bsz, s_len, B_HEADS, 2 * B_HEAD_DIM))

    def maps(t):
        return t.reshape(t.shape[0], t.shape[1], B_HEADS, 2, B_HEAD_DIM)

    def merge(p, q, k, v):
        o = rmsnorm(blocked_attention(maps(q), k, v, map_w, scale), subln_g) * (1 - lam_init)
        y_a = chunk_spatial_gating(jax.nn.gelu(p[..., :2 * A_WIDTH]), sgu_w, sgu_b, sgu_g)
        return jnp.concatenate([y_a, o.reshape(p.shape[0], p.shape[1], B_WIDTH)], axis=-1) @ w_out

    p, pc = h @ w_in, hc @ w_in
    q, k, v = qkv(p)
    qc, kc, vc = qkv(pc)
    cos, sin = rope
    q, k = apply_rope(q, cos, sin), apply_rope(k, cos, sin)
    k_all = jnp.concatenate([maps(kc), maps(k)], axis=1)
    v_all = jnp.concatenate([vc, v], axis=1)
    y = merge(p, q, k_all, v_all)
    yc = merge(pc, qc, maps(kc), vc) if need_ctx else None
    return y, yc

def odd_mixer(h, hc, w_in, w_out, rpb, gq, w_uq, gkv, w_ukv, rope, need_ctx):
    scale_c = 1.0 / math.sqrt(C_HEAD_DIM)
    scale_d = 1.0 / math.sqrt(D_NOPE + D_ROPE)
    one_map = jnp.ones((1,), jnp.float32)
    o_cq = 3 * C_WIDTH
    o_ckv = o_cq + Q_LORA
    o_kr = o_ckv + KV_LORA

    def na_qkv(p):
        bsz, s_len = p.shape[:2]
        q, k, v = jnp.split(p[..., :3 * C_WIDTH], 3, axis=-1)
        return (q.reshape(bsz, s_len, C_HEADS, C_HEAD_DIM), k.reshape(bsz, s_len, C_HEADS, C_HEAD_DIM),
                v.reshape(bsz, s_len, C_HEADS, C_HEAD_DIM))

    def mla_q(p):
        bsz, s_len = p.shape[:2]
        return (rmsnorm(p[..., o_cq:o_ckv], gq) @ w_uq).reshape(bsz, s_len, D_HEADS, D_NOPE + D_ROPE)

    def mla_kv(p):
        bsz, s_len = p.shape[:2]
        kv = (rmsnorm(p[..., o_ckv:o_kr], gkv) @ w_ukv).reshape(bsz, s_len, D_HEADS, D_NOPE + D_VDIM)
        return kv[..., :D_NOPE], kv[..., D_NOPE:], p[..., o_kr:][:, :, None, :]

    def mla_key(k_nope, k_rope):
        return jnp.concatenate([k_nope, jnp.broadcast_to(k_rope, k_nope.shape[:3] + (D_ROPE,))], axis=-1)

    def merge(o_c, o_d):
        bsz, s_len = o_c.shape[:2]
        return jnp.concatenate([o_c.reshape(bsz, s_len, C_WIDTH), o_d.reshape(bsz, s_len, D_WIDTH)], axis=-1) @ w_out

    p, pc = h @ w_in, hc @ w_in
    cos, sin = rope
    q_c, k_c, v_c = na_qkv(p)
    q_cc, k_cc, v_cc = na_qkv(pc)
    q_d = mla_q(p)
    q_d = jnp.concatenate([q_d[..., :D_NOPE], apply_rope(q_d[..., D_NOPE:], cos, sin)], axis=-1)
    kn, v_d, kr = mla_kv(p)
    k_d = mla_key(kn, apply_rope(kr, cos, sin))
    kn_c, v_dc, kr_c = mla_kv(pc)
    k_dc = mla_key(kn_c, kr_c)
    o_c = neighbourhood_attention(q_c, k_c, v_c, k_cc, v_cc, rpb, scale_c)
    o_d = blocked_attention(q_d[:, :, :, None], jnp.concatenate([k_dc, k_d], axis=1)[:, :, :, None],
                            jnp.concatenate([v_dc, v_d], axis=1), one_map, scale_d)
    y = merge(o_c, o_d)
    if need_ctx:
        oc_c = blocked_attention(q_cc[:, :, :, None], k_cc[:, :, :, None], v_cc, one_map, scale_c)
        od_c = blocked_attention(mla_q(pc)[:, :, :, None], k_dc[:, :, :, None], v_dc, one_map, scale_d)
        yc = merge(oc_c, od_c)
    else:
        yc = None
    return y, yc

def setup_inputs(seed: int = 0) -> dict:
    key = jax.random.key(seed)
    ks = jax.random.split(key, 31)
    f32 = jnp.float32

    def nrm(k, shape, scale):
        return jax.random.normal(k, shape, f32) * scale

    def gain(k, shape):
        return 1.0 + 0.05 * jax.random.normal(k, shape, f32)

    return {
        'x': nrm(ks[0], (BATCH, SEQ, D_MODEL), 1.0),
        'c': nrm(ks[1], (BATCH, D_MODEL), 1.0),
        'ctx': nrm(ks[2], (BATCH, CTX_LEN, D_MODEL), 1.0),
        'c_ctx': nrm(ks[3], (D_MODEL,), 1.0),
        'w_mod': nrm(ks[4], (DEPTH, D_MODEL, N_MOD * D_MODEL), 0.5 * D_MODEL ** -0.5),
        'b_mod': nrm(ks[5], (DEPTH, N_MOD * D_MODEL), 0.01),
        'norm_g': gain(ks[6], (DEPTH, 4, D_MODEL)),
        'ev_w_in': nrm(ks[7], (N_EVEN, D_MODEL, EVEN_IN), D_MODEL ** -0.5),
        'ev_w_out': nrm(ks[8], (N_EVEN, MIX_WIDTH, D_MODEL), MIX_WIDTH ** -0.5),
        'sgu_w': nrm(ks[9], (N_EVEN, A_GROUPS, CHUNK, CHUNK), CHUNK ** -0.5),
        'sgu_b': gain(ks[10], (N_EVEN, A_GROUPS, CHUNK)),
        'sgu_g': gain(ks[11], (N_EVEN, A_WIDTH)),
        'diff_lq1': nrm(ks[12], (N_EVEN, B_HEAD_DIM), 0.1),
        'diff_lk1': nrm(ks[13], (N_EVEN, B_HEAD_DIM), 0.1),
        'diff_lq2': nrm(ks[14], (N_EVEN, B_HEAD_DIM), 0.1),
        'diff_lk2': nrm(ks[15], (N_EVEN, B_HEAD_DIM), 0.1),
        'diff_subln_g': gain(ks[16], (N_EVEN, 2 * B_HEAD_DIM)),
        'ffn_w1': nrm(ks[17], (N_EVEN, D_MODEL, D_FF), D_MODEL ** -0.5),
        'ffn_w3': nrm(ks[18], (N_EVEN, D_MODEL, D_FF), D_MODEL ** -0.5),
        'ffn_w2': nrm(ks[19], (N_EVEN, D_FF, D_MODEL), D_FF ** -0.5),
        'od_w_in': nrm(ks[20], (N_ODD, D_MODEL, ODD_IN), D_MODEL ** -0.5),
        'od_w_out': nrm(ks[21], (N_ODD, MIX_WIDTH, D_MODEL), MIX_WIDTH ** -0.5),
        'na_rpb': nrm(ks[22], (N_ODD, C_HEADS, 2 * WIN_H - 1, 2 * WIN_W - 1), 0.2),
        'mla_gq': gain(ks[23], (N_ODD, Q_LORA)),
        'mla_w_uq': nrm(ks[24], (N_ODD, Q_LORA, D_HEADS * (D_NOPE + D_ROPE)), Q_LORA ** -0.5),
        'mla_gkv': gain(ks[25], (N_ODD, KV_LORA)),
        'mla_w_ukv': nrm(ks[26], (N_ODD, KV_LORA, D_HEADS * (D_NOPE + D_VDIM)), KV_LORA ** -0.5),
        'router_w': nrm(ks[27], (N_ODD, D_MODEL, N_EXPERTS), D_MODEL ** -0.5),
        'moe_w1': nrm(ks[28], (N_ODD, N_EXPERTS, D_MODEL, D_FF_EXPERT), D_MODEL ** -0.5),
        'moe_w3': nrm(ks[29], (N_ODD, N_EXPERTS, D_MODEL, D_FF_EXPERT), D_MODEL ** -0.5),
        'moe_w2': nrm(ks[30], (N_ODD, N_EXPERTS, D_FF_EXPERT, D_MODEL), D_FF_EXPERT ** -0.5),
    }

def reference(x, c, ctx, c_ctx, w_mod, b_mod, norm_g, ev_w_in, ev_w_out, sgu_w, sgu_b, sgu_g,
              diff_lq1, diff_lk1, diff_lq2, diff_lk2, diff_subln_g, ffn_w1, ffn_w3, ffn_w2,
              od_w_in, od_w_out, na_rpb, mla_gq, mla_w_uq, mla_gkv, mla_w_ukv,
              router_w, moe_w1, moe_w3, moe_w2):
    bsz, s_len, _ = x.shape
    t = jnp.arange(s_len, dtype=jnp.int32)
    row, col = t // GRID_W, t % GRID_W
    rope_b = axial_rope_tables(row, col, B_HEAD_DIM)
    rope_d = axial_rope_tables(row, col, D_ROPE)
    silu_c = jax.nn.silu(c)
    silu_cc = jax.nn.silu(c_ctx)
    for l in range(DEPTH):
        i = l // 2
        need_ctx = l < DEPTH - 1
        mod = (silu_c @ w_mod[l] + b_mod[l]).reshape(bsz, N_MOD, 1, D_MODEL)
        mod_c = (silu_cc @ w_mod[l] + b_mod[l]).reshape(N_MOD, D_MODEL)
        sh1, sc1, g1, sh2, sc2, g2 = [mod[:, j] for j in range(N_MOD)]
        ch1, cs1, cg1, ch2, cs2, cg2 = [mod_c[j] for j in range(N_MOD)]
        h = modulate(rmsnorm(x, norm_g[l, 0]), sh1, sc1)
        hc = modulate(rmsnorm(ctx, norm_g[l, 0]), ch1, cs1)
        if l % 2 == 0:
            y, yc = even_mixer(h, hc, l, ev_w_in[i], ev_w_out[i], sgu_w[i], sgu_b[i], sgu_g[i],
                               diff_lq1[i], diff_lk1[i], diff_lq2[i], diff_lk2[i], diff_subln_g[i],
                               rope_b, need_ctx)

            def ffn(z):
                return swiglu(z, ffn_w1[i], ffn_w3[i], ffn_w2[i])
        else:
            y, yc = odd_mixer(h, hc, od_w_in[i], od_w_out[i], na_rpb[i], mla_gq[i], mla_w_uq[i],
                              mla_gkv[i], mla_w_ukv[i], rope_d, need_ctx)

            def ffn(z):
                return moe_swiglu(z, router_w[i], moe_w1[i], moe_w3[i], moe_w2[i])
        x = x + g1 * rmsnorm(y, norm_g[l, 1])
        h = modulate(rmsnorm(x, norm_g[l, 2]), sh2, sc2)
        x = x + g2 * rmsnorm(ffn(h), norm_g[l, 3])
        if need_ctx:
            ctx = ctx + cg1 * rmsnorm(yc, norm_g[l, 1])
            hc = modulate(rmsnorm(ctx, norm_g[l, 2]), ch2, cs2)
            ctx = ctx + cg2 * rmsnorm(ffn(hc), norm_g[l, 3])
    return x


_drawn_inputs = setup_inputs


def setup_inputs(seed=0):
    import zlib

    import numpy as np

    out = dict(_drawn_inputs(seed))
    spreads = {}
    factors = {'diff_lq1': 3.274,
     'diff_lq2': 187.608,
     'diff_lk2': 3.116,
     'na_rpb': 7.415,
     'mla_gq': 8.0,
     'sgu_b': 2.808,
     'sgu_g': 3.195}
    for name, (base, spread) in spreads.items():
        noise = np.random.default_rng([zlib.crc32(name.encode()), seed]).standard_normal(out[name].shape)
        drawn = base * np.exp(spread * noise) if base else spread * noise
        out[name] = jnp.asarray(drawn.astype(out[name].dtype))
    for name, factor in factors.items():
        out[name] = (out[name] * factor).astype(out[name].dtype)
    return out
```

```python
import math

import numpy as np

import concourse.bass as bass
from concourse import mybir
from contextlib import ExitStack

F32 = mybir.dt.float32
F32R = mybir.dt.float32r
I32 = mybir.dt.int32
U32 = mybir.dt.uint32
ALU = mybir.AluOpType
ACT = mybir.ActivationFunctionType
AX = mybir.AxisListType.X

P = 128
D = 1024
KT = D // P
CTX = 256
TOK = 512
SEQ = 256
TT = TOK // P
EPS = 1e-6
GRID = 64
WIN_W = 16
RPB_W = 31
ROWS = SEQ // GRID
REPEAT = GRID + 1
A_W = 512
EV_IN = 2560
OD_IN = 1952
FF = 2816
FT = FF // P
NE = 8
FFE = 3584
JE = FFE // 512
UNIT = 2048
NRAW = 6
NSPLIT = 2
NSP_E = 3
CAP = 128
LAM_INIT = 0.8 - 0.6 * math.exp(-0.3 * 0)

C_ID, C_ONE, C_R0, C_R1, C_TRI, C_IOTA, C_MASK, C_NEG = 0, 128, 256, 384, 480, 608, 736, 800
C_ALL = 864
V_NG, V_C, V_GQ, V_GKV, V_SUB, V_SG, V_ALL = 0, 64, 80, 82, 83, 84, 88


def constants():
    c = np.zeros((P, C_ALL), np.float32)
    i = np.arange(P)
    c[:, C_ID:C_ID + P] = np.eye(P)
    c[:, C_ONE:C_ONE + P] = 1.0
    for k in range(P):
        m = k % 64
        c[k, C_R0 + (k - 32 if m >= 32 else k + 32)] = -1.0 if m >= 32 else 1.0
    for k in range(64, 96):
        m = k - 64
        c[k, C_R1 + (k - 16 if m >= 16 else k + 16)] = -1.0 if m >= 16 else 1.0
    c[:, C_TRI:C_TRI + P] = (i[:, None] < i[None, :])
    c[:, C_IOTA:C_IOTA + P] = i[None, :]
    q, k = i % GRID, np.arange(GRID)
    start = np.clip(q - WIN_W // 2, 0, GRID - WIN_W)
    inside = (k[None, :] >= start[:, None]) & (k[None, :] < start[:, None] + WIN_W)
    c[:, C_MASK:C_MASK + GRID] = inside
    c[:, C_NEG:C_NEG + GRID] = np.where(inside, 0.0, -1e30)
    t = np.arange(SEQ)

    def angles(dim):
        n = dim // 4
        inv = (1.0 / (np.float32(10000.0) ** (np.arange(n, dtype=np.float32) / np.float32(n)))).astype(np.float32)
        row, col = (t // GRID).astype(np.float32), (t % GRID).astype(np.float32)
        return np.concatenate([row[:, None] * inv, col[:, None] * inv], axis=-1).astype(np.float32)

    tab = np.zeros((P, 4, SEQ), np.float32)
    a = angles(64)
    tab[:, 0], tab[:, 1] = np.cos(a).T[i % 32], np.sin(a).T[i % 32]
    a = angles(32)
    tab[:, 2] = 1.0
    tab[64:96, 2], tab[64:96, 3] = np.cos(a).T[np.arange(32) % 16], np.sin(a).T[np.arange(32) % 16]
    return c, tab.reshape(P, 4 * SEQ)


def weight_units(w):
    def cols(m, c0, n=256):
        return [(0, (KT, n), m.rearrange("(k p) n -> p k n", p=P)[:, :, c0:c0 + n])]

    def mod(l, m):
        return "direct", cols(w["w_mod"][l], 256 * m)

    units = [("direct", [(0, (4, P), w["sgu_w"][0].rearrange("g p q -> p g q"))])]
    units += [mod(0, m) for m in range(8)]
    for s in range(10):
        units.append(("split", cols(w["ev_w_in"][0], 256 * s)))
        if s < 8:
            units += [mod(0, 8 + 2 * s), mod(0, 9 + 2 * s)]
    units += [mod(1, m) for m in range(24)]
    units += [("split", cols(w["ev_w_out"][0], 256 * s)) for s in range(4)]
    for s in range(FT // 2):
        units += [("split", cols(w["ffn_w1"][0], 256 * s)), ("split", cols(w["ffn_w3"][0], 256 * s))]
    down = w["ffn_w2"][0].rearrange("(k p) n -> p k n", p=P)
    units += [("split", [(0, (2, D), down[:, 2 * s:2 * s + 2, :])]) for s in range(FT // 2)]
    od = w["od_w_in"][0]
    units += [("split", cols(od, 256 * s)) for s in range(7)]
    units.append(("split", cols(od, OD_IN - 256)))
    units.append(("latent", [(0, (2, 384), w["mla_w_uq"][0].rearrange("(k p) n -> p k n", p=P)),
                             (768, (768,), w["mla_w_ukv"][0])]))
    units += [("split", cols(w["od_w_out"][0], 256 * s)) for s in range(4)]
    units.append(("direct", [(0, (KT, NE), w["router_w"][0].rearrange("(k p) n -> p k n", p=P))]))
    return units


S_EV, S_EVO = 0, 10
S_UP, S_DOWN = S_EVO + 4, S_EVO + 4 + FT
S_OD = S_DOWN + FT // 2
S_ODO = S_OD + 8
S_END = S_ODO + 4


NORMS = ["n0", "sub0", "sub1", "sub2", "sub3", "n1", "n2", "n3", "n4", "cq", "ckv", "n5", "n6", "n7"]


def expert_order():
    order = [("a", 0), ("b", 0)]
    for j in range(1, JE):
        order += [("a", j), ("b", j), ("d", j - 1)]
    return order + [("d", JE - 1)]


ORDER = expert_order()
NU = 2 * len(ORDER)


def trunk(nc, w, out):
    ctx = ExitStack()
    with ctx:
        def sb(name, shape, dt=F32):
            return ctx.enter_context(nc.sbuf_tensor(name, shape, dt))

        sems = {}

        def S(name):
            if name not in sems:
                sems[name] = ctx.enter_context(nc.semaphore(name))
            return sems[name]

        RAW = sb("raw_weights", [P, NRAW, UNIT])
        SPH = sb("split_high", [P, NSPLIT, UNIT], F32R)
        SPL = sb("split_low", [P, NSPLIT, UNIT], F32R)
        X = sb("residual", [P, KT, TOK])
        HH = sb("h_high", [P, KT, TOK], F32R)
        HL = sb("h_low", [P, KT, TOK], F32R)
        Y = sb("y", [P, KT, TOK])
        CON = sb("constants", [P, C_ALL])
        TAB = sb("angles", [P, 4, SEQ])
        IDR = sb("ident_r", [P, P], F32R)
        BM = sb("b_mod_cols", [P, 96])
        VC = sb("vector_cols", [P, V_ALL])
        SC = sb("silu_c", [P, KT, 2])
        MOD = sb("modulation", [P, 2, 48, 2])
        VEC = sb("affine", [P, 2, 4, KT, 2])
        SM = sb("small", [P, 64])
        OVS = ExitStack()
        OV = OVS.enter_context(nc.sbuf_tensor("overlay", [P, 12288], F32))
        OVS.close()
        MP = sb("expert_onehot", [P, 2, NE + 1, CAP], F32R)
        MPT = sb("expert_onehot_t", [P, NE, SEQ], F32R)
        XEH, XEL = sb("xe_high", [P, KT, CAP], F32R), sb("xe_low", [P, KT, CAP], F32R)
        GTH, GTL = sb("gt_high", [P, 2, 512], F32R), sb("gt_low", [P, 2, 512], F32R)
        YEH, YEL = sb("ye_high", [P, D], F32R), sb("ye_low", [P, D], F32R)
        PS = [ctx.enter_context(nc.psum_tensor(f"bank{i}", [P, 512], F32)) for i in range(8)]

        ident, ones = CON[:, C_ID:C_ID + P], CON[:, C_ONE:C_ONE + P]
        tri = CON[:, C_TRI:C_TRI + P]

        def ov(a, n, *shape):
            v = OV[:, a:a + n]
            if len(shape) == 2:
                return v.rearrange("p (a b) -> p a b", a=shape[0])
            return v

        SQ, TMP, HF, RS = ov(0, 1024, 2, 512), ov(1024, 1024, 2, 512), ov(2048, 1024, 2, 512), ov(3072, 512)
        QK, V, U = ov(0, 4096, 8, 512), ov(4096, 2048, 4, 512), ov(6144, 2048, 4, 512)
        SV, OUN = ov(8192, 2048, 4, 512), ov(10240, 2048, 4, 512)
        WST, SBB = Y[:, 7, :], Y[:, 6, :]
        PB = Y[:, 0:4, :]
        PT = Y[:, 4:6, :]
        QC, KC, VCT = ov(0, 1024, 4, 256), ov(1024, 2048, 4, 512), ov(3072, 2048, 4, 512)
        CQ, CKV = ov(5120, 512, 2, 256), ov(5632, 512)
        KD, VD, QD = ov(6144, 2048, 4, 512), ov(8192, 2048, 4, 512), ov(10240, 1024, 4, 256)
        BT = ov(11264, 512, 2, 256)
        G = ov(0, FT * 512, FT, 512)
        HFULL = Y[:, :, 256:512]
        YACC = Y[:, :, 0:256]
        HTH = HH[:, 0:4, :].rearrange("p (t f) n -> p t (f n)", t=2)
        HTL = HL[:, 0:4, :].rearrange("p (t f) n -> p t (f n)", t=2)
        YG, GE, SIL = X[:, 0:4, 0:256], X[:, 4:6, 0:256], X[:, 6:8, 0:256]
        RT = ov(10752, 512)
        OUTT = ov(4096, 2048, 2, 1024)

        UNITS = weight_units(w)
        need, count = [], [0] * NRAW
        release, ns, nd = [], 0, 0
        split_at, direct_at = [], []
        for r, (kind, parts) in enumerate(UNITS):
            count[r % NRAW] += 16 * len(parts)
            need.append(count[r % NRAW])
            if kind == "split":
                ns += 1
                split_at.append(r)
                release.append(("split_low_done", ns))
            elif kind == "latent":
                latent_at = r
                release.append(("mla_full", 12))
            else:
                nd += 1
                direct_at.append(r)
                release.append(("direct_used", nd))
        assert ns == S_END
        raw_base = list(count)

        def raw_of(r):
            return RAW[:, r % NRAW, :]

        def esplit(u):
            g = u % NSP_E
            if g < NSPLIT:
                return SPH[:, g, :], SPL[:, g, :]
            return (HH[:, 4:8, :].rearrange("p a b -> p (a b)"), HL[:, 4:8, :].rearrange("p a b -> p (a b)"))

        def item_used(b, e, i):
            return S("e_slots"), e * NU + (b * NE * NU + NSP_E + 2 * i + 2)

        def halves(c0):
            return [(0, 0, 256), (1, 256, 512)] if c0 == 0 else [(1, 0, 256)]

        def norm(name, nt, src, width, dim, ready, scratch=(SQ, RS)):
            return dict(name=name, nt=nt, src=src, width=width, dim=dim, ready=ready, sq=scratch[0], rs=scratch[1])

        def xs(c0):
            return lambda t: X[:, t, c0:TOK]

        def ys(c0):
            return lambda t: Y[:, t, c0:TOK]

        N = {
            "n0": norm("n0", KT, xs(0), TOK, D, ("x_in", lambda t: t + 1)),
            "n1": norm("n1", KT, ys(0), TOK, D, ("y_evac0", lambda t: t + 1)),
            "n2": norm("n2", KT, xs(0), TOK, D, ("n1_res", lambda t: t + 1)),
            "n3": norm("n3", KT, ys(0), TOK, D, ("ffn_evac", lambda t: KT)),
            "n4": norm("n4", KT, xs(0), TOK, D, ("n3_res", lambda t: t + 1)),
            "n5": norm("n5", KT, ys(256), SEQ, D, ("y_evac1", lambda t: t + 1)),
            "n6": norm("n6", KT, xs(256), SEQ, D, ("n5_res", lambda t: t + 1)),
            "n7": norm("n7", KT, lambda t: YACC[:, t, :], SEQ, D, ("moe_done", lambda t: 1)),
            "cq": norm("cq", 2, lambda t: CQ[:, t, :], SEQ, 256, ("od_evac", lambda t: 13 + t),
                       (Y[:, 0:2, :], Y[:, 2, :])),
            "ckv": norm("ckv", 1, lambda t: CKV, TOK, P, ("od_evac", lambda t: 15),
                        (Y[:, 3:5, :], Y[:, 5, :])),
        }
        for h in range(4):
            N[f"sub{h}"] = norm(f"sub{h}", 1, lambda t, h=h: OUN[:, h, :], TOK, P, ("o_evac0", lambda t: 16),
                                (SQ[:, h % 2:h % 2 + 1, :], ov(3072 + 512 * h, 512)))

        tiles = 0
        for i, name in enumerate(NORMS):
            N[name]["tiles_before"], N[name]["index"] = tiles, i
            tiles += N[name]["nt"]

        def norm_root(name):
            return S("norm_root"), N[name]["index"] + 1

        def act_squares(act, n):
            for t in range(n["nt"]):
                act.wait_ge(S(n["ready"][0]), n["ready"][1](t))
                if t >= 2:
                    act.wait_ge(S("squares_used"), n["tiles_before"] + t - 1)
                act.activation(n["sq"][:, t % 2, :n["width"]], n["src"](t), ACT.Square)\
                   .then_inc(S("squares"), 1)

        def act_root(act, n):
            act.wait_ge(S("squares_used"), n["tiles_before"] + n["nt"])
            act.activation(n["rs"][:, :n["width"]], PS[6][:, :n["width"]], ACT.Sqrt,
                           bias=SM[:, 0:1], scale=1.0 / n["dim"]).then_inc(S("norm_root"), 1)

        def pe_sums(pe, n):
            for t in range(n["nt"]):
                pe.wait_ge(S("squares"), n["tiles_before"] + t + 1)
                pe.matmul(PS[6][:, :n["width"]], ones, n["sq"][:, t % 2, :n["width"]],
                          start=(t == 0), stop=(t == n["nt"] - 1)).then_inc(S("squares_used"), 1)

        own_steps = [0]

        def link(dve, ins):
            own_steps[0] += 1
            ins.then_inc(S("vector_step"), 1)
            dve.wait_ge(S("vector_step"), own_steps[0])

        def dve_rstd(dve, n):
            dve.wait_ge(*norm_root(n["name"]))
            r = n["rs"][:, :n["width"]]
            link(dve, dve.reciprocal(r, r))

        def mod_vectors(l, which):
            return VEC[:, l, 2 * which], MOD[:, l, 24 * which:24 * which + 8]

        def dve_modulate(dve, n, c0, full=False):
            nt, wd = n["nt"], n["width"]

            def tmp(t):
                if t >= 2:
                    dve.wait_ge(S(n["name"] + "_h"), t - 1)
                dve.tensor_tensor(TMP[:, t % 2, :wd], n["src"](t), RS[:, :wd], ALU.mult)\
                   .then_inc(S(n["name"] + "_tmp"), 1)

            tmp(0)
            tmp(1)
            for t in range(nt):
                if not full:
                    dve.wait_ge(S(n["name"] + "_hh"), t + 1)
                    dve.tensor_tensor(HL[:, t, c0:TOK], HF[:, t % 2, :wd], HH[:, t, c0:TOK].bitcast(F32),
                                      ALU.subtract).then_inc(S(n["name"] + "_hl"), 1)
                if t + 2 < nt:
                    tmp(t + 2)

        def act_modulate(act, n, l, which, c0, full=False):
            a, sh = mod_vectors(l, which)
            nt, wd = n["nt"], n["width"]
            for t in range(nt):
                act.wait_ge(S(n["name"] + "_tmp"), t + 1)
                if not full and t >= 2:
                    act.wait_ge(S(n["name"] + "_hl"), t - 1)
                dst = HFULL[:, t, :] if full else HF[:, t % 2, :wd]
                for v, a0, a1 in halves(c0):
                    last = act.activation(dst[:, a0:a1], TMP[:, t % 2, a0:a1], ACT.Identity,
                                          bias=sh[:, t, v:v + 1], scale=a[:, t, v:v + 1])
                last.then_inc(S(n["name"] + "_h"), 1)
                if not full:
                    act.wait_ge(S(n["name"] + "_h"), t + 1)
                    act.activation(HH[:, t, c0:TOK], HF[:, t % 2, :wd], ACT.Copy).then_inc(S(n["name"] + "_hh"), 1)

        def dve_residual(dve, n, l, which, c0):
            gg = VEC[:, l, 2 * which + 1]
            nt, wd = n["nt"], n["width"]

            def tmp(t):
                dve.tensor_tensor(TMP[:, t % 2, :wd], n["src"](t), RS[:, :wd], ALU.mult)\
                   .then_inc(S(n["name"] + "_tmp"), 1)

            tmp(0)
            for t in range(nt):
                if t + 1 < nt:
                    if t >= 1:
                        dve.wait_ge(S(n["name"] + "_res"), t)
                    tmp(t + 1)
                dve.wait_ge(S(n["name"] + "_tmp"), t + 1)
                for v, a0, a1 in halves(c0):
                    xt = X[:, t, c0 + a0:c0 + a1]
                    last = dve.scalar_tensor_tensor(xt, TMP[:, t % 2, a0:a1], gg[:, t, v:v + 1], xt,
                                                    ALU.mult, ALU.add)
                last.then_inc(S(n["name"] + "_res"), 1)

        def act_split(act, s):
            r = split_at[s]
            act.wait_ge(S(f"raw{r % NRAW}"), need[r])
            if s >= NSPLIT:
                act.wait_ge(*unit_used(s - NSPLIT))
            act.activation(SPH[:, s % NSPLIT, :], raw_of(r), ACT.Copy).then_inc(S("split_high_done"), 1)

        def dve_split(dve, s):
            dve.wait_ge(S("split_high_done"), s + 1)
            dve.tensor_tensor(SPL[:, s % NSPLIT, :], raw_of(split_at[s]), SPH[:, s % NSPLIT, :].bitcast(F32),
                              ALU.subtract).then_inc(S("split_low_done"), 1)

        def three(pe, ps, wh, wl, xh, xl, first, last):
            pe.matmul(ps, wh, xh, start=first, stop=False)
            pe.matmul(ps, wh, xl, start=False, stop=False)
            return pe.matmul(ps, wl, xh, start=False, stop=last)

        def bank_full(s, j):
            return S("bank_full"), 2 * (s if s < S_DOWN else s - FT // 2) + j + 1

        def unit_used(s):
            if S_DOWN <= s < S_OD:
                return S("gk_used"), 2 * (s - S_DOWN) + 2
            return bank_full(s, 1)

        def gemm_unit(pe, s, kind, c0, banks, free, hready=None, offs=(0, 128)):
            hi, lo = SPH[:, s % NSPLIT, :], SPL[:, s % NSPLIT, :]
            pe.wait_ge(S("split_low_done"), s + 1)
            for j in range(2):
                if free[j] is not None:
                    pe.wait_ge(*free[j])
                parts = 1 if kind == "f" else 2
                for q in range(parts):
                    for k in range(KT):
                        if hready is not None and j == 0 and q == 0:
                            pe.wait_ge(S(hready), k + 1)
                        if kind == "f":
                            a = slice(256 * k + offs[j], 256 * k + offs[j] + P)
                            m = three(pe, banks[j][:, :TOK - c0], hi[:, a], lo[:, a], HH[:, k, c0:TOK],
                                      HL[:, k, c0:TOK], k == 0, k == KT - 1)
                        else:
                            tt = 2 * j + q
                            a, b = slice(P * tt, P * tt + P), slice(256 * k, 256 * k + 256)
                            m = three(pe, banks[j][:, 256 * q:256 * q + 256], HH[:, k, a], HL[:, k, a],
                                      hi[:, b], lo[:, b], k == 0, k == KT - 1)
                if j == 0:
                    m.then_inc(S("bank_full"), 1)
            m.then_inc(S("bank_full"), 1)

        def mod_unit(pe, d, l, m):
            r = direct_at[d]
            pe.wait_ge(S(f"raw{r % NRAW}"), need[r])
            for j in range(2):
                c = 96 * l + 4 * m + 2 * j
                for k in range(KT):
                    a = 256 * k + 128 * j
                    last = pe.matmul(PS[7][:, c:c + 2], raw_of(r)[:, a:a + P], SC[:, k, :],
                                     start=(k == 0), stop=(k == KT - 1))
            last.then_inc(S("direct_used"), 1)

        def dve_mod(dve, step, l, m0, m1):
            n = m1 - m0
            dve.tensor_tensor(MOD[:, l, m0:m1, :],
                              PS[7][:, 96 * l + 2 * m0:96 * l + 2 * m1].rearrange("p (m v) -> p m v", v=2),
                              BM[:, 48 * l + m0:48 * l + m1].rearrange("p (m o) -> p m o", o=1)
                              .to_broadcast([P, n, 2]),
                              ALU.add).then_inc(S("mod_evac"), 1)
            dve.wait_ge(S("mod_evac"), step)

        def dve_affine(dve, l, which, plus_one, m):
            g = VC[:, V_NG + 8 * (4 * l + which):V_NG + 8 * (4 * l + which) + 8]\
                .rearrange("p (m o) -> p m o", o=1).to_broadcast([P, KT, 2])
            return dve.scalar_tensor_tensor(VEC[:, l, which], MOD[:, l, m:m + 8, :], plus_one, g, ALU.add, ALU.mult)

        att0 = []
        for h in range(4):
            for qb in range(4):
                nk = 2 if qb < 2 else 4
                att0.append(dict(
                    q=[QK[64 * m:64 * m + 64, h, P * qb:P * qb + P] for m in range(2)],
                    k=[QK[64 * m:64 * m + 64, 4 + h, 0:P * nk] for m in range(2)],
                    nk=nk, scale=1.0 / math.sqrt(64), bias=None, v=[V[:, kt, P * h:P * h + P] for kt in range(nk)],
                    o=slice(0, P), dst=(h, P * qb)))
        att1 = []
        for h in range(8):
            for qb in range(2):
                p0 = 64 * (h % 2)
                att1.append(dict(
                    q=[QC[p0:p0 + 64, h // 2, P * qb:P * qb + P]], k=[KC[p0:p0 + 64, h // 2, :]],
                    nk=4, scale=1.0 / math.sqrt(64), bias=(h, qb), v=[VCT[:, kt, 64 * h:64 * h + 64] for kt in range(4)],
                    o=slice(p0, p0 + 64), dst=(h // 2, 256 + P * qb)))
        for h in range(4):
            for qb in range(2):
                att1.append(dict(
                    q=[QD[0:96, h, P * qb:P * qb + P]], k=[KD[0:96, h, :]],
                    nk=4, scale=1.0 / math.sqrt(96), bias=None, v=[VD[:, kt, P * h:P * h + P] for kt in range(4)],
                    o=slice(0, P), dst=(4 + h, 256 + P * qb)))
        NB_ = len(att1) - 8

        def pe_attention(pe, a, units, between=None):
            for i in range(len(units) + 2):
                if i < len(units):
                    u = units[i]
                    if i >= 2:
                        pe.wait_ge(S(f"exp{a}"), i - 1)
                    for m in range(len(u["q"])):
                        last = pe.matmul(PS[2 * (i % 2) + m][:, :P * u["nk"]], u["q"][m], u["k"][m],
                                         start=True, stop=True)
                    last.then_inc(S(f"scores{a}"), 1)
                if between is not None:
                    between(i)
                if 1 <= i <= len(units):
                    u = units[i - 1]
                    pe.wait_ge(S(f"prob{a}"), i)
                    if i >= 2:
                        pe.wait_ge(S(f"pt{a}"), i - 1)
                    for kt in range(u["nk"]):
                        last = pe.transpose(PS[4][:, P * kt:P * kt + P], PB[:, 2 * ((i - 1) % 2), P * kt:P * kt + P],
                                            ident)
                    last.then_inc(S(f"ptrans{a}"), 1)
                if i >= 2:
                    u = units[i - 2]
                    pe.wait_ge(S(f"pt{a}"), i - 1)
                    if i >= 3:
                        pe.wait_ge(S(f"o_evac{a}"), i - 2)
                    for kt in range(u["nk"]):
                        last = pe.matmul(PS[5][u["o"], :P], u["v"][kt], PT[:, i % 2, P * kt:P * kt + P],
                                         start=(kt == 0), stop=(kt == u["nk"] - 1))
                    last.then_inc(S(f"o{a}"), 1)

        def act_attention(act, a, units):
            for i in range(len(units) + 2):
                if i < len(units):
                    u = units[i]
                    act.wait_ge(S(f"negmax{a}"), i + 1)
                    if i >= 2:
                        act.wait_ge(S(f"ptrans{a}"), i - 1)
                    n = P * u["nk"]
                    for m in range(len(u["q"])):
                        src = PB[:, 2 * (i % 2), :n] if u["bias"] else PS[2 * (i % 2) + m][:, :n]
                        c = 8 + 8 * (i % 2) + m
                        last = act.activation(PB[:, 2 * (i % 2) + m, :n], src, ACT.Exp, bias=SM[:, c:c + 1],
                                              scale=1.0 if u["bias"] else u["scale"],
                                              accum_out=SM[:, c + 2:c + 3])
                    last.then_inc(S(f"exp{a}"), 1)
                if 1 <= i <= len(units):
                    u = units[i - 1]
                    act.wait_ge(S(f"ptrans{a}"), i)
                    if i >= 3:
                        act.wait_ge(S(f"o{a}"), i - 2)
                    act.activation(PT[:, (i - 1) % 2, :P * u["nk"]], PS[4][:, :P * u["nk"]], ACT.Copy)\
                       .then_inc(S(f"pt{a}"), 1)
                if i >= 2 and a == 1:
                    u = units[i - 2]
                    t, c = u["dst"]
                    act.wait_ge(S("o1"), i - 1)
                    act.activation(HH[u["o"], t, c:c + P], PS[5][u["o"], :P], ACT.Copy).then_inc(S("o_high"), 1)

        def dve_attention(dve, a, units):
            for i in range(len(units) + 2):
                if i < len(units):
                    u = units[i]
                    n = P * u["nk"]
                    dve.wait_ge(S(f"scores{a}"), i + 1)
                    if i >= 2:
                        dve.wait_ge(S(f"exp{a}"), i - 1)
                        dve.wait_ge(S(f"prob{a}"), i - 1)
                    c = 8 + 8 * (i % 2)
                    if u["bias"]:
                        if i >= 2:
                            dve.wait_ge(S(f"ptrans{a}"), i - 1)
                        dve.wait_ge(S("bias_ready"), i + 1)
                        b = PB[:, 2 * (i % 2), :]
                        dve.tensor_scalar(b[:, :CTX], PS[2 * (i % 2)][:, :CTX], u["scale"], None, ALU.mult)\
                           .then_inc(S("biased"), 1)
                        dve.scalar_tensor_tensor(b[:, CTX:], PS[2 * (i % 2)][:, CTX:], u["scale"], BT[:, i % 2, :],
                                                 ALU.mult, ALU.add).then_inc(S("biased"), 1)
                        dve.wait_ge(S("biased"), 2 * i + 2)
                        dve.tensor_reduce(SM[:, c:c + 1], b[:, :], AX, ALU.max, negate=True)\
                           .then_inc(S(f"negmax{a}"), 1)
                    else:
                        for m in range(len(u["q"])):
                            last = dve.tensor_reduce(SM[:, c + 6 + m:c + 7 + m], PS[2 * (i % 2) + m][:, :n], AX,
                                                     ALU.max, negate=True)
                        link(dve, last)
                        dve.tensor_scalar(SM[:, c:c + 2], SM[:, c + 6:c + 8], u["scale"], None, ALU.mult)\
                           .then_inc(S(f"negmax{a}"), 1)
                if 1 <= i <= len(units):
                    u = units[i - 1]
                    n = P * u["nk"]
                    b, c = 2 * ((i - 1) % 2), 8 + 8 * ((i - 1) % 2)
                    dve.wait_ge(S(f"exp{a}"), i)
                    nm = len(u["q"])
                    link(dve, dve.reciprocal(SM[:, c + 4:c + 4 + nm], SM[:, c + 2:c + 2 + nm]))
                    if nm == 2:
                        link(dve, dve.tensor_scalar(PB[:, b + 1, :n], PB[:, b + 1, :n], SM[:, c + 5:c + 6],
                                                    SM[:, 1:2], ALU.mult, ALU.mult))
                        dve.scalar_tensor_tensor(PB[:, b, :n], PB[:, b, :n], SM[:, c + 4:c + 5], PB[:, b + 1, :n],
                                                 ALU.mult, ALU.add).then_inc(S(f"prob{a}"), 1)
                    else:
                        dve.tensor_scalar(PB[:, b, :n], PB[:, b, :n], SM[:, c + 4:c + 5], None, ALU.mult)\
                           .then_inc(S(f"prob{a}"), 1)
                if i >= 2:
                    u = units[i - 2]
                    t, c = u["dst"]
                    if a == 0:
                        dve.wait_ge(S("o0"), i - 1)
                        dve.tensor_copy(OUN[:, t, c:c + P], PS[5][:, :P]).then_inc(S("o_evac0"), 1)
                    else:
                        dve.wait_ge(S("o_high"), i - 1)
                        dve.tensor_tensor(HL[u["o"], t, c:c + P], PS[5][u["o"], :P],
                                          HH[u["o"], t, c:c + P].bitcast(F32), ALU.subtract)\
                           .then_inc(S("o_evac1"), 1)

        def ropes(l):
            if l == 0:
                return [(QK[:, t, CTX:TOK], CON[:, C_R0:C_R0 + P], TAB[:, 0, :], TAB[:, 1, :]) for t in range(8)]
            r, c, s = CON[0:96, C_R1:C_R1 + 96], TAB[0:96, 2, :], TAB[0:96, 3, :]
            return [(QD[0:96, h, :], r, c, s) for h in range(4)] + [(KD[0:96, h, CTX:TOK], r, c, s) for h in range(4)]

        def pe_rope(pe, l, ready):
            for i, (x, r, c, s) in enumerate(ropes(l)):
                pe.wait_ge(*ready(i))
                if i >= 2:
                    pe.wait_ge(S(f"rot_sin{l}"), i - 1)
                pe.matmul(PS[2 + i % 2][0:x.shape[0], :SEQ], r, x, start=True, stop=True).then_inc(S(f"rot{l}"), 1)

        def dve_rope(dve, l):
            for i, (x, r, c, s) in enumerate(ropes(l)):
                n = x.shape[0]
                t1, t2 = Y[0:n, i % 2, 0:256], Y[0:n, i % 2, 256:512]
                dve.wait_ge(S(f"rot{l}"), i + 1)
                if i >= 2:
                    dve.wait_ge(S(f"roped{l}"), i - 1)
                dve.tensor_tensor(t1, PS[2 + i % 2][0:n, :SEQ], s, ALU.mult).then_inc(S(f"rot_sin{l}"), 1)
                link(dve, dve.tensor_tensor(t2, x, c, ALU.mult))
                dve.wait_ge(S(f"rot_sin{l}"), i + 1)
                dve.tensor_tensor(x, t1, t2, ALU.add).then_inc(S(f"roped{l}"), 1)

        block = ctx.enter_context(nc.Block())

        @block.sync
        def _(sp):
            sp.dma_start(CON[:, :], w["consts"]).then_inc(S("consts_in"), 16)
            rows1 = OV[0:96, 0:P]
            sp.dma_start(rows1, w["b_mod"].rearrange("l (m p) -> (l m) p", p=P)).then_inc(S("rows_in"), 16)
            sp.dma_start(OV[V_NG:V_NG + 64, P:2 * P], w["norm_g"].rearrange("l g (m p) -> (l g m) p", p=P))\
              .then_inc(S("rows_in"), 16)
            sp.dma_start(OV[V_C:V_C + 8, P:2 * P], w["c_ctx"].rearrange("(m p) -> m p", p=P)).then_inc(S("rows_in"), 16)
            sp.dma_start(OV[V_C + 8:V_C + 16, P:2 * P], w["c"][0].rearrange("(m p) -> m p", p=P))\
              .then_inc(S("rows_in"), 16)
            sp.dma_start(OV[V_GQ:V_GQ + 2, P:2 * P], w["mla_gq"][0].rearrange("(m p) -> m p", p=P))\
              .then_inc(S("rows_in"), 16)
            sp.dma_start(OV[V_GKV:V_GKV + 1, P:2 * P], w["mla_gkv"]).then_inc(S("rows_in"), 16)
            sp.dma_start(OV[V_SUB:V_SUB + 1, P:2 * P], w["diff_subln_g"]).then_inc(S("rows_in"), 16)
            sp.dma_start(OV[V_SG:V_SG + 4, P:2 * P], w["sgu_g"][0].rearrange("(m p) -> m p", p=P))\
              .then_inc(S("rows_in"), 16)

            def load(r):
                for off, shape, src in UNITS[r][1]:
                    n = int(np.prod(shape))
                    dst = raw_of(r)[:, off:off + n]
                    if len(shape) == 2:
                        dst = dst.rearrange("p (k n) -> p k n", k=shape[0])
                    sp.dma_start(dst, src).then_inc(S(f"raw{r % NRAW}"), 16)

            def expert_load(b, e, u):
                kind, j = ORDER[u // 2]
                i = u % 2
                if kind == "d":
                    src = w["moe_w2"][0][e].rearrange("(k p) n -> p k n", p=P)[:, 4 * j + 2 * i:4 * j + 2 * i + 2, :]
                    dst = RAW[:, u % NRAW, :].rearrange("p (k n) -> p k n", k=2)
                else:
                    m = w["moe_w1" if kind == "a" else "moe_w3"][0][e].rearrange("(k p) n -> p k n", p=P)
                    src = m[:, 4 * i:4 * i + 4, 512 * j:512 * j + 512]
                    dst = RAW[:, u % NRAW, :].rearrange("p (k n) -> p k n", k=4)
                sp.dma_start(dst, src).then_inc(S(f"eraw{u % NRAW}"), 16)

            def experts(b):
                g0 = b * NE * NU
                for u in range(NRAW):
                    if b == 0:
                        sem, v = release[len(UNITS) - NRAW + (u - len(UNITS)) % NRAW]
                        sp.wait_ge(S(sem), v)
                    else:
                        sp.wait_ge(S("e_low"), g0 - NRAW + u + 1)
                    expert_load(b, 0, u)
                with sp.Fori(0, NE - 1) as e:
                    for u in range(NU):
                        sp.wait_ge(S("e_low"), e * NU + (g0 + u + 1))
                        sp.sem_inc(S("loads_let"), 1)
                        n = u + NRAW
                        expert_load(b, e + n // NU, n % NU)
                for u in range(NU - NRAW):
                    sp.wait_ge(S("e_low"), g0 + (NE - 1) * NU + u + 1)
                    expert_load(b, NE - 1, u + NRAW)

            for r in range(len(UNITS)):
                if r >= NRAW:
                    sem, v = release[r - NRAW]
                    sp.wait_ge(S(sem), v)
                load(r)
            experts(0)
            sp.wait_ge(S("flag_ready"), 1)
            more = sp.value_load(SM[0:1, 60:61].bitcast(I32))
            with sp.If(more > 0):
                experts(1)
            for c in range(2):
                sp.wait_ge(S("out_ready"), 2 * c + 2)
                sp.dma_start(out[0, P * c:P * c + P, :], OUTT[:, c, :]).then_inc(S("stored"), 16)
            sp.wait_ge(S("stored"), 32)

        @block.gpsimd
        def _(pool):
            pool.dma_start(Y[:, 0:4, :].rearrange("p (t f) n -> p t (f n)", t=2),
                           w["ctx"][0].rearrange("(t p) d -> p t d", p=P)).then_inc(S("tokens_in"), 16)
            pool.dma_start(Y[:, 4:8, :].rearrange("p (t f) n -> p t (f n)", t=2),
                           w["x"][0].rearrange("(t p) d -> p t d", p=P)).then_inc(S("tokens_in"), 16)
            for i, k in enumerate(("diff_lq1", "diff_lk1", "diff_lq2", "diff_lk2")):
                pool.dma_start(OV[:, 256 + 64 * i:320 + 64 * i], bass.AP(w[k].tensor, 0, [[0, P], [1, 64]]))\
                    .then_inc(S("lambda_in"), 16)
            pool.dma_start(TAB[:, :, :].rearrange("p a b -> p (a b)"), w["angles"]).then_inc(S("angles_in"), 16)
            pool.wait_ge(S("x_in"), KT)
            pool.dma_start(SBB, bass.AP(w["sgu_b"].tensor, 0, [[0, P], [1, 512]])).then_inc(S("sgu_b_in"), 16)
            pool.wait_ge(S("n4_hl"), KT)
            for i in range(NB_):
                h, qb = att1[i]["bias"]
                if i >= 2:
                    pool.wait_ge(S("biased"), 2 * i - 2)
                for r in range(2):
                    q_row = 2 * qb + r
                    base = (h * (2 * ROWS - 1) + ROWS - 1 - q_row) * REPEAT * RPB_W + WIN_W - 1
                    pool.dma_start(BT[64 * r:64 * r + 64, i % 2, :].rearrange("p (k n) -> p k n", k=4),
                                   bass.AP(w["rpb"].tensor, base, [[RPB_W - 1, GRID], [REPEAT * RPB_W, ROWS], [1, GRID]]))\
                        .then_inc(S(f"toeplitz{i % 2}"), 16)
                pool.wait_ge(S(f"toeplitz{i % 2}"), 32 * (i // 2 + 1))
                b = BT[:, i % 2, :].rearrange("p (k n) -> p k n", k=4)
                mask = CON[:, C_MASK:C_MASK + GRID].rearrange("p (o n) -> p o n", o=1).to_broadcast([P, 4, GRID])
                neg = CON[:, C_NEG:C_NEG + GRID].rearrange("p (o n) -> p o n", o=1).to_broadcast([P, 4, GRID])
                pool.tensor_tensor(b, b, mask, ALU.mult).then_inc(S("masked"), 1)
                pool.wait_ge(S("masked"), i + 1)
                pool.tensor_tensor(b, b, neg, ALU.add).then_inc(S("bias_ready"), 1)

        @block.scalar
        def _(act):
            act.wait_ge(S("consts_in"), 16)
            act.activation(IDR[:, :], ident, ACT.Copy).then_inc(S("ident_r"), 1)
            act.wait_ge(S("cols_done"), 2)
            act.activation(SC[:, :, 0], VC[:, V_C:V_C + 8], ACT.Silu)
            act.activation(SC[:, :, 1], VC[:, V_C + 8:V_C + 16], ACT.Silu).then_inc(S("silu_c"), 1)
            act.wait_ge(S("lam_dots"), 1)
            act.activation(SM[:, 4:6], SM[:, 2:4], ACT.Exp).then_inc(S("lam_exp"), 1)
            act_split(act, S_EV)
            act.wait_ge(S("eps"), 1)
            act_squares(act, N["n0"])
            act_root(act, N["n0"])
            act.wait_ge(S("affine"), 1)
            act_modulate(act, N["n0"], 0, 0, 0)
            for s in range(10):
                if s + 1 < 10:
                    act_split(act, S_EV + s + 1)
                for j in range(2):
                    act.wait_ge(*bank_full(S_EV + s, j))
                    b = PS[j]
                    if s < 2:
                        act.activation(U[:, 2 * s + j, :], b[:, :], ACT.Gelu_apprx_tanh).then_inc(S("ev_evac"), 1)
                    elif s < 4:
                        dst = SV[:, 2 * j:2 * j + 2, 256 * (s - 2):256 * (s - 1)]
                        act.activation(dst, b[:, :].rearrange("p (t n) -> p t n", t=2), ACT.Gelu_apprx_tanh)\
                           .then_inc(S("ev_evac"), 1)
                    elif s < 8:
                        act.activation(QK[:, 2 * (s - 4) + j, :], b[:, :], ACT.Copy).then_inc(S("ev_evac"), 1)
                    else:
                        dst = V[:, 2 * j:2 * j + 2, 256 * (s - 8):256 * (s - 7)]
                        act.activation(dst, b[:, :].rearrange("p (t n) -> p t n", t=2), ACT.Copy)\
                           .then_inc(S("ev_evac"), 1)
                if s == 4:
                    act.wait_ge(S("sgu_var"), 1)
                    act.activation(SM[:, 36:40], SM[:, 32:40].rearrange("p (t c) -> p t c", c=2)[:, :, 1] if False
                                   else SM[:, 28:32], ACT.Sqrt, bias=SM[:, 0:1]).then_inc(S("sgu_std"), 1)
            for g in range(4):
                act.wait_ge(S("sgu_out"), g + 1)
                act.activation(HH[:, g, :], U[:, g, :], ACT.Copy).then_inc(S("sgu_high"), 1)
            act_attention(act, 0, att0)
            act_split(act, S_EVO)
            for h in range(4):
                n = N[f"sub{h}"]
                if h >= 2:
                    act.wait_ge(S("squares_used"), N[f"sub{h - 2}"]["tiles_before"] + 1)
                act_squares(act, n)
                act_root(act, n)
            for h in range(4):
                act.wait_ge(S("sub_out"), h + 1)
                act.activation(HH[:, 4 + h, :], OUN[:, h, :], ACT.Copy).then_inc(S("sub_high"), 1)
            for s in range(4):
                if s + 1 < 4:
                    act_split(act, S_EVO + s + 1)
                for j in range(2):
                    act.wait_ge(*bank_full(S_EVO + s, j))
                    act.activation(Y[:, 2 * s + j, :], PS[j][:, :], ACT.Copy).then_inc(S("y_evac0"), 1)
            act_split(act, S_UP)
            act_squares(act, N["n1"])
            act_root(act, N["n1"])
            act_squares(act, N["n2"])
            act_root(act, N["n2"])
            act_modulate(act, N["n2"], 0, 1, 0)
            for s in range(FT):
                if s + 1 < FT:
                    act_split(act, S_UP + s + 1)
                if s % 2 == 0:
                    p = s // 2
                    for j in range(2):
                        act.wait_ge(*bank_full(S_UP + s, j))
                        if p >= 2:
                            act.wait_ge(S("g_done"), 2 * (p - 2) + j + 1)
                        act.activation(Y[:, 2 * (p % 2) + j, :], PS[4 * (p % 2) + j][:, :], ACT.Silu)\
                           .then_inc(S("silu_done"), 1)
            act_split(act, S_DOWN)
            for k in range(FT):
                act.wait_ge(S("g_done"), k + 1)
                if k == 0:
                    act.wait_ge(*unit_used(S_DOWN - 1))
                if k >= 4:
                    act.wait_ge(S("gk_used"), k - 3)
                act.activation(HH[:, k % 4, :], G[:, k, :], ACT.Copy).then_inc(S("gk_high"), 1)
                if k % 2 == 1 and k // 2 + 1 < FT // 2:
                    act_split(act, S_DOWN + k // 2 + 1)
            act_split(act, S_OD)
            act.wait_ge(S("gk_used"), FT)
            for m in range(4):
                act.activation(Y[:, m, :], PS[m][:, :], ACT.Copy).then_inc(S("ffn_evac"), 1)
            act_squares(act, N["n3"])
            act_root(act, N["n3"])
            act_squares(act, N["n4"])
            act_root(act, N["n4"])
            act_modulate(act, N["n4"], 1, 0, 0)
            for s in range(8):
                if s + 1 < 8:
                    act_split(act, S_OD + s + 1)
                for j in range(2):
                    act.wait_ge(*bank_full(S_OD + s, j))
                    b = PS[j]
                    if s < 2:
                        act.activation(QC[:, 2 * s + j, :], b[:, :SEQ], ACT.Copy).then_inc(S("od_evac"), 1)
                    elif s < 4:
                        act.activation(KC[:, 2 * (s - 2) + j, :], b[:, :], ACT.Copy).then_inc(S("od_evac"), 1)
                    elif s < 6:
                        dst = VCT[:, 2 * j:2 * j + 2, 256 * (s - 4):256 * (s - 3)]
                        act.activation(dst, b[:, :].rearrange("p (t n) -> p t n", t=2), ACT.Copy)\
                           .then_inc(S("od_evac"), 1)
                    elif s == 6:
                        act.activation(CQ[:, j, :], b[:, :SEQ], ACT.Copy).then_inc(S("od_evac"), 1)
                    elif j == 0:
                        act.activation(CKV, b[:, :], ACT.Copy).then_inc(S("od_evac"), 1)
                    else:
                        for h in range(4):
                            last = act.activation(KD[64:96, h, :], b[96:128, :], ACT.Copy)
                        last.then_inc(S("od_evac"), 1)
            for n in ("cq", "ckv"):
                act_squares(act, N[n])
                act_root(act, N[n])
            for i in range(12):
                act.wait_ge(S("mla_full"), i + 1)
                b = PS[i % 2]
                if i < 4:
                    act.activation(QD[0:96, i, :], b[0:96, :SEQ], ACT.Copy).then_inc(S("mla_evac"), 1)
                elif i < 8:
                    act.activation(KD[0:64, i - 4, :], b[0:64, :], ACT.Copy).then_inc(S("mla_evac"), 1)
                else:
                    act.activation(VD[:, i - 8, :], b[:, :], ACT.Copy).then_inc(S("mla_evac"), 1)
            act.wait_ge(*unit_used(S_ODO - 1))
            act_attention(act, 1, att1)
            act_split(act, S_ODO)
            for s in range(4):
                if s + 1 < 4:
                    act_split(act, S_ODO + s + 1)
                for j in range(2):
                    act.wait_ge(*bank_full(S_ODO + s, j))
                    act.activation(Y[:, 2 * s + j, 256:512], PS[j][:, :SEQ], ACT.Copy).then_inc(S("y_evac1"), 1)
            act_squares(act, N["n5"])
            act_root(act, N["n5"])
            act_squares(act, N["n6"])
            act_root(act, N["n6"])
            act_modulate(act, N["n6"], 1, 1, 256, full=True)
            for i in range(4):
                act.wait_ge(S("htok_full"), i + 1)
                t, f = i // 2, i % 2
                act.activation(HTH[:, t, 512 * f:512 * f + 512], PS[i][:, :], ACT.Copy).then_inc(S("htok_high"), 1)
            act.wait_ge(S("top_diff"), 1)
            act.activation(RT[:, 64:66], RT[:, 66:68], ACT.Exp).then_inc(S("top_exp"), 1)

            def experts(b):
                g0 = b * NE * NU
                for i in range(4):
                    act.wait_ge(S("pt_full"), 4 * b + i + 1)
                    act.activation(MPT[:, 2 * i:2 * i + 2, :], PS[i][:, :].rearrange("p (e n) -> p e n", e=2),
                                   ACT.Copy).then_inc(S("mpt_done"), 1)

                def xe_high(e, r):
                    act.wait_ge(S("xe_full"), e * 2 + (2 * (NE + 1) * b + r + 1))
                    act.activation(XEH[:, 4 * r:4 * r + 4, :], PS[7][:, :].rearrange("p (f n) -> p f n", f=4),
                                   ACT.Copy).then_inc(S("xe_high"), 1)

                def gt_high(e, j):
                    act.wait_ge(S("gt_full"), e * JE + (JE * NE * b + j + 1))
                    act.activation(GTH[:, j % 2, :], PS[6][:, :], ACT.Copy).then_inc(S("gt_high"), 1)

                xe_high(0, 0)
                xe_high(0, 1)
                with act.Fori(0, NE) as e:
                    for i, (kind, j) in enumerate(ORDER):
                        for u in (2 * i, 2 * i + 1):
                            act.wait_ge(S(f"eraw{u % NRAW}"), e * (16 * NU // NRAW)
                                        + (16 * (NE * NU // NRAW) * b + 16 * (u // NRAW + 1)))
                            act.wait_ge(S("e_slots"), e * NU + (g0 + u + 1))
                            act.activation(esplit(u)[0], RAW[:, u % NRAW, :], ACT.Copy).then_inc(S("e_high"), 1)
                        if i == 0:
                            continue
                        kind, j = ORDER[i - 1]
                        if kind == "a":
                            act.wait_ge(*item_used(b, e, i - 1))
                            act.wait_ge(S("ge_free"), e * JE + (JE * NE * b + j + 1))
                            act.activation(SIL, PS[2 * (j % 2)][:, :].rearrange("p (a n) -> p a n", a=2), ACT.Silu)\
                               .then_inc(S("esilu"), 1)
                            if j >= 1:
                                gt_high(e, j - 1)
                        if kind == "d" and j == JE - 2:
                            xe_high(e + 1, 0)
                            gt_high(e, JE - 1)
                            xe_high(e + 1, 1)
                    for c in range(2):
                        act.wait_ge(S("yg"), e * 2 + (2 * NE * b + c + 1))
                        act.activation(YEH[:, 512 * c:512 * c + 512],
                                       YG[:, 2 * c:2 * c + 2, :].rearrange("p a n -> p a n") if False else
                                       YG[:, 2 * c:2 * c + 2, :], ACT.Copy).then_inc(S("ye_high"), 1)

            experts(0)
            more = act.value_load(SM[0:1, 60:61].bitcast(I32))
            with act.If(more > 0):
                experts(1)
            act_squares(act, N["n7"])
            act_root(act, N["n7"])
            for i in range(4):
                act.wait_ge(S("out_full"), i + 1)
                act.activation(OUTT[:, i // 2, 512 * (i % 2):512 * (i % 2) + 512], PS[i][:, :], ACT.Copy)\
                   .then_inc(S("out_ready"), 1)

        @block.vector
        def _(dve):
            link(dve, dve.memset(SM[:, :], 0.0))
            dve.memset(SM[:, 0:1], EPS).then_inc(S("eps"), 1)
            dve.wait_ge(S("cols_full"), 2)
            dve.tensor_copy(BM[:, :], PS[0][:, 0:96]).then_inc(S("cols_done"), 1)
            dve.tensor_copy(VC[:, :], PS[1][:, 0:V_ALL]).then_inc(S("cols_done"), 1)
            dve.wait_ge(S("lambda_in"), 64)
            lam = OV[:, 256:512].rearrange("p (a n) -> p a n", a=4)
            for i in range(2):
                last = dve.tensor_tensor(lam[:, 2 * i, :], lam[:, 2 * i, :], lam[:, 2 * i + 1, :], ALU.mult)
            link(dve, last)
            for i in range(2):
                last = dve.tensor_reduce(SM[:, 2 + i:3 + i], lam[:, 2 * i, :], AX, ALU.add)
            last.then_inc(S("lam_dots"), 1)
            dve.wait_ge(S("lam_exp"), 1)
            link(dve, dve.tensor_tensor(SM[:, 6:7], SM[:, 5:6], SM[:, 4:5], ALU.subtract))
            link(dve, dve.tensor_scalar(SM[:, 1:2], SM[:, 6:7], -LAM_INIT, None, ALU.add))
            dve.wait_ge(S("cols_done"), 2)
            link(dve, dve.tensor_scalar(SM[:, 24:25], VC[:, V_SUB:V_SUB + 1], 1.0 - LAM_INIT, None, ALU.mult))
            for f in range(KT):
                dve.wait_ge(S("x_full"), f + 1)
                dve.tensor_copy(X[:, f, :], PS[f % 2][:, :]).then_inc(S("x_in"), 1)
            dve.wait_ge(S("direct_used"), 1)
            dve.tensor_copy(WST, PS[2][:, :]).then_inc(S("wst"), 1)
            dve_split(dve, S_EV)
            dve.wait_ge(S("direct_used"), 9)
            dve_mod(dve, 1, 0, 0, 16)
            dve_affine(dve, 0, 0, 1.0, 8).then_inc(S("affine"), 1)
            dve_rstd(dve, N["n0"])
            dve_modulate(dve, N["n0"], 0)
            for s in range(10):
                if s + 1 < 10:
                    dve_split(dve, S_EV + s + 1)
                if s == 4:
                    dve.wait_ge(S("ev_evac"), 8)
                    for t in range(TT):
                        last = dve.bn_stats(Y[:, 5, 8 * t:8 * t + 6], SV[:, t, :])
                    link(dve, last)
                    for t in range(TT):
                        last = dve.bn_aggr(Y[:, 5, 64 + 2 * t:66 + 2 * t], Y[:, 5, 8 * t:8 * t + 6])
                    link(dve, last)
                    dve.tensor_copy(SM[:, 28:32], Y[:, 5, 64:72].rearrange("p (t c) -> p t c", c=2)[:, :, 1])\
                       .then_inc(S("sgu_var"), 1)
                if s == 5:
                    dve.wait_ge(S("sgu_std"), 1)
                    link(dve, dve.reciprocal(SM[:, 40:44], SM[:, 36:40]))
                    for t in range(TT):
                        last = dve.tensor_scalar(SV[:, t, :], SV[:, t, :], Y[:, 5, 64 + 2 * t:65 + 2 * t],
                                                 SM[:, 40 + t:41 + t], ALU.subtract, ALU.mult)
                    last.then_inc(S("sgu_v"), 1)
            dve.wait_ge(S("direct_used"), 25)
            dve_mod(dve, 2, 0, 16, 48)
            dve_affine(dve, 0, 1, 0.0, 16)
            dve_affine(dve, 0, 2, 1.0, 32)
            dve_affine(dve, 0, 3, 0.0, 40).then_inc(S("affine"), 1)
            dve.wait_ge(S("angles_in"), 16)
            dve_rope(dve, 0)
            dve.wait_ge(S("sgu_b_in"), 16)
            dve.wait_ge(*unit_used(S_EV + 9))
            for g in range(4):
                t1 = Y[:, 4 + g % 2, :]
                dve.wait_ge(S("sgu_full"), g + 1)
                if g >= 2:
                    dve.wait_ge(S("sgu_out"), g - 1)
                bias = SBB[:, P * g:P * g + P].rearrange("p (o n) -> p o n", o=1).to_broadcast([P, TT, P])
                dve.scalar_tensor_tensor(t1.rearrange("p (t n) -> p t n", t=TT),
                                         PS[g % 2][:, :].rearrange("p (t n) -> p t n", t=TT),
                                         VC[:, V_SG + g:V_SG + g + 1], bias, ALU.mult, ALU.add)\
                   .then_inc(S("sgu_mixed"), 1)
                dve.wait_ge(S("sgu_mixed"), g + 1)
                dve.tensor_tensor(U[:, g, :], t1, U[:, g, :], ALU.mult).then_inc(S("sgu_out"), 1)
                dve.wait_ge(S("sgu_high"), g + 1)
                dve.tensor_tensor(HL[:, g, :], U[:, g, :], HH[:, g, :].bitcast(F32), ALU.subtract)\
                   .then_inc(S("mix0"), 1)
            dve_attention(dve, 0, att0)
            dve_split(dve, S_EVO)
            for h in range(4):
                n = N[f"sub{h}"]
                dve_rstd(dve, n)
                dve.scalar_tensor_tensor(OUN[:, h, :], OUN[:, h, :], SM[:, 24:25], n["rs"], ALU.mult, ALU.mult)\
                   .then_inc(S("sub_out"), 1)
            for h in range(4):
                dve.wait_ge(S("sub_high"), h + 1)
                dve.tensor_tensor(HL[:, 4 + h, :], OUN[:, h, :], HH[:, 4 + h, :].bitcast(F32), ALU.subtract)\
                   .then_inc(S("mix0"), 1)
            dve.wait_ge(S("direct_used"), 49)
            dve_mod(dve, 3, 1, 0, 48)
            dve_affine(dve, 1, 0, 1.0, 8)
            dve_affine(dve, 1, 1, 0.0, 16)
            dve_affine(dve, 1, 2, 1.0, 32)
            dve_affine(dve, 1, 3, 0.0, 40).then_inc(S("affine"), 1)
            dve.wait_ge(S("affine"), 3)
            for s in range(3):
                dve_split(dve, S_EVO + s + 1)
            dve_split(dve, S_UP)
            dve_rstd(dve, N["n1"])
            dve_residual(dve, N["n1"], 0, 0, 0)
            dve.wait_ge(S("n1_res"), KT)
            dve_rstd(dve, N["n2"])
            dve_modulate(dve, N["n2"], 0)
            for s in range(FT):
                if s + 1 < FT:
                    dve_split(dve, S_UP + s + 1)
                if s % 2 == 1:
                    p = s // 2
                    for j in range(2):
                        dve.wait_ge(*bank_full(S_UP + s, j))
                        dve.wait_ge(S("silu_done"), 2 * p + j + 1)
                        dve.tensor_tensor(G[:, 2 * p + j, :], PS[4 * (p % 2) + 2 + j][:, :],
                                          Y[:, 2 * (p % 2) + j, :], ALU.mult).then_inc(S("g_done"), 1)
            dve_split(dve, S_DOWN)
            dve.wait_ge(S("g_done"), FT)
            for k in range(FT):
                dve.wait_ge(S("gk_high"), k + 1)
                dve.tensor_tensor(HL[:, k % 4, :], G[:, k, :], HH[:, k % 4, :].bitcast(F32), ALU.subtract)\
                   .then_inc(S("gk_low"), 1)
                if k % 2 == 1 and k // 2 + 1 < FT // 2:
                    dve_split(dve, S_DOWN + k // 2 + 1)
            dve_split(dve, S_OD)
            dve.wait_ge(S("gk_used"), FT)
            for m in range(4, 8):
                dve.tensor_copy(Y[:, m, :], PS[m][:, :]).then_inc(S("ffn_evac"), 1)
            dve_rstd(dve, N["n3"])
            dve.wait_ge(S("ffn_evac"), 8)
            dve_residual(dve, N["n3"], 0, 1, 0)
            dve.wait_ge(S("n3_res"), KT)
            dve_rstd(dve, N["n4"])
            dve_modulate(dve, N["n4"], 0)
            for s in range(7):
                dve_split(dve, S_OD + s + 1)
            for name, gain, tiles in (("cq", V_GQ, 2), ("ckv", V_GKV, 1)):
                n = N[name]
                dve_rstd(dve, n)
                for t in range(tiles):
                    last = dve.scalar_tensor_tensor(n["src"](t), n["src"](t), VC[:, gain + t:gain + t + 1],
                                                    n["rs"][:, :n["width"]], ALU.mult, ALU.mult)
                last.then_inc(S("latent"), 1)
            dve_rope(dve, 1)
            dve_attention(dve, 1, att1)
            for s in range(4):
                dve_split(dve, S_ODO + s)
            dve_rstd(dve, N["n5"])
            dve_residual(dve, N["n5"], 1, 0, 256)
            dve.wait_ge(S("n5_res"), KT)
            dve_rstd(dve, N["n6"])
            dve_modulate(dve, N["n6"], 256, full=True)
            LG, MX = RT[:, 0:16].rearrange("p (t e) -> p t e", t=2), RT[:, 16:32].rearrange("p (t e) -> p t e", t=2)
            IX = RT[:, 32:48].bitcast(U32).rearrange("p (t e) -> p t e", t=2)
            IF = RT[:, 48:64].rearrange("p (t e) -> p t e", t=2)
            EXP, DIF, G1, G2 = RT[:, 64:66], RT[:, 66:68], RT[:, 68:70], RT[:, 70:72]
            SEL = RT[:, 80:96].rearrange("p (t e) -> p t e", t=2)
            GATE = RT[:, 96:112].rearrange("p (t e) -> p t e", t=2)
            T1 = RT[:, 112:128].rearrange("p (t e) -> p t e", t=2)
            T2 = RT[:, 128:144].rearrange("p (t e) -> p t e", t=2)
            POS = RT[:, 144:160].rearrange("p (t e) -> p t e", t=2)
            CNT, GSL = RT[:, 160:168], RT[:, 176:184]
            dve.wait_ge(S("direct_used"), len(direct_at))
            link(dve, dve.tensor_copy(LG, PS[4][:, 0:16].rearrange("p (t e) -> p t e", t=2)))
            for t in range(2):
                last = dve.max(MX[:, t, :], LG[:, t, :])
            link(dve, last)
            for t in range(2):
                last = dve.max_index(IX[:, t, :], MX[:, t, :], LG[:, t, :])
            link(dve, last)
            dve.tensor_tensor(DIF, MX[:, :, 1], MX[:, :, 0], ALU.subtract).then_inc(S("top_diff"), 1)
            link(dve, dve.tensor_copy(IF, IX))
            iota8 = CON[:, C_IOTA:C_IOTA + NE]
            for t in range(2):
                dve.tensor_scalar(T1[:, t, :], iota8, IF[:, t, 0:1], None, ALU.is_equal)
                last = dve.tensor_scalar(T2[:, t, :], iota8, IF[:, t, 1:2], None, ALU.is_equal)
            link(dve, last)
            dve.tensor_tensor(SEL, T1, T2, ALU.add).then_inc(S("selected"), 1)
            for i in range(4):
                t, f = i // 2, i % 2
                dve.wait_ge(S("htok_high"), i + 1)
                dve.tensor_tensor(HTL[:, t, 512 * f:512 * f + 512], PS[i][:, :],
                                  HTH[:, t, 512 * f:512 * f + 512].bitcast(F32), ALU.subtract)\
                   .then_inc(S("htok_low"), 1)
            dve.wait_ge(S("top_exp"), 1)
            link(dve, dve.tensor_scalar(G1, EXP, 1.0, None, ALU.add))
            link(dve, dve.reciprocal(G1, G1))
            link(dve, dve.tensor_tensor(G2, G1, EXP, ALU.mult))
            for t in range(2):
                last = dve.tensor_scalar(T1[:, t, :], T1[:, t, :], G1[:, t:t + 1], None, ALU.mult)
            link(dve, last)
            for t in range(2):
                last = dve.scalar_tensor_tensor(GATE[:, t, :], T2[:, t, :], G2[:, t:t + 1], T1[:, t, :],
                                                ALU.mult, ALU.add)
            link(dve, last)
            dve.wait_ge(S("positions"), 1)
            link(dve, dve.scalar_tensor_tensor(POS, PS[5][:, 0:16].rearrange("p (t e) -> p t e", t=2), 1.0, SEL,
                                          ALU.add, ALU.mult))
            link(dve, dve.tensor_scalar(POS, POS, -1.0, None, ALU.add))
            link(dve, dve.tensor_reduce(SM[:, 56:57], PS[5][:, 16:24], AX, ALU.max))
            link(dve, dve.tensor_scalar(SM[:, 57:58], SM[:, 56:57], float(CAP), None, ALU.is_gt))
            dve.tensor_copy(SM[:, 60:61].bitcast(I32), SM[:, 57:58]).then_inc(S("flag_ready"), 1)
            link(dve, dve.memset(YACC, 0.0))

            def experts(b):
                g0 = b * NE * NU
                if b:
                    dve.tensor_scalar(POS, POS, -float(CAP), None, ALU.add).then_inc(S("later_slots"), 1)
                    dve.wait_ge(S("later_slots"), 1)
                for t in range(2):
                    for e in range(NE):
                        dve.tensor_scalar(MP[:, t, e, :], CON[:, C_IOTA:C_IOTA + P], POS[:, t, e:e + 1], None,
                                          ALU.is_equal)
                    last = dve.tensor_scalar(MP[:, t, NE, :], CON[:, C_IOTA:C_IOTA + P], 0.0, None, ALU.mult)
                last.then_inc(S("onehot"), 1)
                dve.wait_ge(S("gslot_full"), b + 1)
                dve.tensor_copy(GSL, PS[5][:, 32:40]).then_inc(S("gslot"), 1)
                dve.wait_ge(S("gslot"), b + 1)

                def xe_low(e, r):
                    dve.wait_ge(S("xe_high"), e * 2 + (2 * (NE + 1) * b + r + 1))
                    dve.tensor_tensor(XEL[:, 4 * r:4 * r + 4, :], PS[7][:, :].rearrange("p (f n) -> p f n", f=4),
                                      XEH[:, 4 * r:4 * r + 4, :].bitcast(F32), ALU.subtract)\
                       .then_inc(S("xe_low"), 1)

                def gt_low(e, j):
                    dve.wait_ge(S("gt_high"), e * JE + (JE * NE * b + j + 1))
                    dve.tensor_tensor(GTL[:, j % 2, :], PS[6][:, :], GTH[:, j % 2, :].bitcast(F32), ALU.subtract)\
                       .then_inc(S("gt_low"), 1)

                xe_low(0, 0)
                xe_low(0, 1)
                with dve.Fori(0, NE) as e:
                    for i, (kind, j) in enumerate(ORDER):
                        for u in (2 * i, 2 * i + 1):
                            dve.wait_ge(S("e_high"), e * NU + (g0 + u + 1))
                            hi, lo = esplit(u)
                            dve.tensor_tensor(lo, RAW[:, u % NRAW, :], hi.bitcast(F32), ALU.subtract)\
                               .then_inc(S("e_low"), 1)
                        if i == 0:
                            continue
                        kind, j = ORDER[i - 1]
                        if kind == "a" and j >= 1:
                            gt_low(e, j - 1)
                        if kind == "b":
                            dve.wait_ge(*item_used(b, e, i - 1))
                            dve.wait_ge(S("esilu"), e * JE + (JE * NE * b + j + 1))
                            if j >= 1:
                                dve.wait_ge(S("gt_full"), e * JE + (JE * NE * b + j))
                            dve.tensor_tensor(GE, PS[2 * (j % 2) + 1][:, :].rearrange("p (a n) -> p a n", a=2), SIL,
                                              ALU.mult).then_inc(S("ge_free"), 1)
                        if kind == "d" and j == JE - 2:
                            xe_low(e + 1, 0)
                            gt_low(e, JE - 1)
                            xe_low(e + 1, 1)
                    dve.wait_ge(*item_used(b, e, len(ORDER) - 1))
                    for c in range(2):
                        dve.tensor_scalar(YG[:, 2 * c:2 * c + 2, :],
                                          PS[4 + c][:, :].rearrange("p (a n) -> p a n", a=2),
                                          GSL[:, bass.ds(e, 1)], None, ALU.mult).then_inc(S("yg"), 1)
                    for c in range(2):
                        dve.wait_ge(S("ye_high"), e * 2 + (2 * NE * b + c + 1))
                        ysl = slice(512 * c, 512 * c + 512)
                        dve.tensor_tensor(YEL[:, ysl].rearrange("p (a n) -> p a n", a=2), YG[:, 2 * c:2 * c + 2, :],
                                          YEH[:, ysl].bitcast(F32).rearrange("p (a n) -> p a n", a=2), ALU.subtract)\
                           .then_inc(S("ye_low"), 1)
                    for r in range(4):
                        dve.wait_ge(S("comb_full"), e * 4 + (4 * NE * b + r + 1))
                        acc = YACC[:, 2 * r:2 * r + 2, :]
                        dve.tensor_tensor(acc, PS[6 + r % 2][:, :].rearrange("p (f n) -> p f n", f=2), acc, ALU.add)\
                           .then_inc(S("comb_done"), 1)

            experts(0)
            more = dve.value_load(SM[0:1, 60:61].bitcast(I32))
            with dve.If(more > 0):
                dve.wait_ge(S("comb_done"), 4 * NE)
                experts(1)
            dve.tensor_scalar(SM[:, 61:62], SM[:, 0:1], 1.0, None, ALU.mult).then_inc(S("moe_done"), 1)
            dve_rstd(dve, N["n7"])
            dve_residual(dve, N["n7"], 1, 1, 256)

        @block.tensor
        def _(pe):
            pe.wait_ge(S("consts_in"), 16)
            pe.wait_ge(S("rows_in"), 8 * 16)
            pe.transpose(PS[0][:, 0:96], OV[0:96, 0:P], CON[0:96, C_ID:C_ID + 96]).then_inc(S("cols_full"), 1)
            pe.transpose(PS[1][:, 0:V_ALL], OV[0:V_ALL, P:2 * P], CON[0:V_ALL, C_ID:C_ID + V_ALL])\
              .then_inc(S("cols_full"), 1)
            pe.wait_ge(S("tokens_in"), 32)
            pe.wait_ge(S("cols_done"), 2)
            for f in range(KT):
                if f >= 2:
                    pe.wait_ge(S("x_in"), f - 1)
                for t in range(TT):
                    c = f * P
                    src = Y[:, 2 * t:2 * t + 2, :].rearrange("p f n -> p (f n)")[:, c:c + P]
                    last = pe.transpose(PS[f % 2][:, P * t:P * t + P], src, ident)
                last.then_inc(S("x_full"), 1)
            pe.wait_ge(S("raw0"), need[0])
            for g in range(4):
                last = pe.transpose(PS[2][:, P * g:P * g + P], raw_of(0)[:, P * g:P * g + P], ident)
            last.then_inc(S("direct_used"), 1)
            pe.wait_ge(S("silu_c"), 1)
            for m in range(8):
                mod_unit(pe, 1 + m, 0, m)
            pe_sums(pe, N["n0"])
            pe.wait_ge(S("mod_evac"), 1)
            for s in range(10):
                kind = "t" if s in (2, 3, 8, 9) else "f"
                free = [(S("ev_evac"), 2 * s - 1 + j) if s else None for j in range(2)]
                gemm_unit(pe, S_EV + s, kind, 0, PS, free, "n0_hl" if s == 0 else None)
                if s < 8:
                    mod_unit(pe, 9 + 2 * s, 0, 8 + 2 * s)
                    mod_unit(pe, 10 + 2 * s, 0, 9 + 2 * s)
            pe_rope(pe, 0, lambda i: (S("ev_evac"), 9 + i))
            pe.wait_ge(S("sgu_v"), 1)
            pe.wait_ge(S("wst"), 1)
            pe.wait_ge(S("ev_evac"), 20)
            for g in range(4):
                if g >= 2:
                    pe.wait_ge(S("sgu_mixed"), g - 1)
                for t in range(TT):
                    last = pe.matmul(PS[g % 2][:, P * t:P * t + P], SV[:, t, P * g:P * g + P], WST[:, P * g:P * g + P],
                                     start=True, stop=True)
                last.then_inc(S("sgu_full"), 1)
            pe.wait_ge(S("roped0"), 8)
            pe.wait_ge(S("sgu_mixed"), 4)
            pe.wait_ge(S("mod_evac"), 2)

            def layer1_modulation(i):
                for m in range(2 * i, min(2 * i + 2, 24)):
                    mod_unit(pe, 25 + m, 1, m)

            pe_attention(pe, 0, att0, layer1_modulation)
            for h in range(4):
                if h >= 1:
                    pe.wait_ge(*norm_root(f"sub{h - 1}"))
                pe_sums(pe, N[f"sub{h}"])
            for s in range(4):
                free = [(S("y_evac0"), 2 * s - 1 + j) if s else None for j in range(2)]
                gemm_unit(pe, S_EVO + s, "f", 0, PS, free, "mix0" if s == 0 else None)
            pe_sums(pe, N["n1"])
            pe.wait_ge(*norm_root("n1"))
            pe_sums(pe, N["n2"])
            pe.wait_ge(S("mod_evac"), 3)
            for s in range(FT):
                p, v = s // 2, s % 2
                free = [None, None]
                if p >= 2:
                    free = [(S("g_done"), 2 * (p - 2) + j + 1) for j in range(2)]
                gemm_unit(pe, S_UP + s, "f", 0, PS[4 * (p % 2) + 2 * v:4 * (p % 2) + 2 * v + 2], free,
                          "n2_hl" if s == 0 else None)
            pe.wait_ge(S("g_done"), FT)
            for d in range(FT // 2):
                s = S_DOWN + d
                hi, lo = SPH[:, s % NSPLIT, :], SPL[:, s % NSPLIT, :]
                pe.wait_ge(S("split_low_done"), s + 1)
                for r in range(2):
                    k = 2 * d + r
                    pe.wait_ge(S("gk_low"), k + 1)
                    for m in range(8):
                        a = slice(D * r + P * m, D * r + P * m + P)
                        last = three(pe, PS[m][:, :], hi[:, a], lo[:, a], HH[:, k % 4, :], HL[:, k % 4, :],
                                     k == 0, k == FT - 1)
                    last.then_inc(S("gk_used"), 1)
            pe.wait_ge(S("ffn_evac"), 8)
            pe_sums(pe, N["n3"])
            pe.wait_ge(*norm_root("n3"))
            pe_sums(pe, N["n4"])
            for s in range(8):
                kind, c0 = ("t", 0) if s in (4, 5) else ("f", 256 if s in (0, 1, 6) else 0)
                free = [(S("od_evac"), 2 * s - 1 + j) if s else None for j in range(2)]
                gemm_unit(pe, S_OD + s, kind, c0, PS, free, "n4_hl" if s == 0 else None,
                          offs=(96, 128) if s == 7 else (0, 128))
            pe_sums(pe, N["cq"])
            pe.wait_ge(*norm_root("cq"))
            pe_sums(pe, N["ckv"])
            r = latent_at
            pe.wait_ge(S(f"raw{r % NRAW}"), need[r])
            uq, ukv = raw_of(r)[:, 0:768].rearrange("p (k n) -> p k n", k=2), raw_of(r)[:, 768:1536]
            for i in range(12):
                if i == 0:
                    pe.wait_ge(S("latent"), 1)
                if i == 4:
                    pe.wait_ge(S("latent"), 2)
                if i >= 2:
                    pe.wait_ge(S("mla_evac"), i - 1)
                else:
                    pe.wait_ge(S("od_evac"), 16)
                b = PS[i % 2]
                if i < 4:
                    for k in range(2):
                        last = pe.matmul(b[0:96, :SEQ], uq[:, k, 96 * i:96 * i + 96], CQ[:, k, :],
                                         start=(k == 0), stop=(k == 1))
                elif i < 8:
                    c = 192 * (i - 4)
                    last = pe.matmul(b[0:64, :], ukv[:, c:c + 64], CKV, start=True, stop=True)
                else:
                    last = pe.matmul(b[:, :], CKV[:, P * (i - 8):P * (i - 7)],
                                     ukv.rearrange("p (h n) -> p h n", h=4)[:, :, 64:192], start=True, stop=True)
                last.then_inc(S("mla_full"), 1)
            pe_rope(pe, 1, lambda i: (S("mla_evac"), 12))
            pe.wait_ge(S("roped1"), 8)
            pe_attention(pe, 1, att1)
            for s in range(4):
                free = [(S("y_evac1"), 2 * s - 1 + j) if s else None for j in range(2)]
                if s == 0:
                    pe.wait_ge(S("o_evac1"), len(att1))
                gemm_unit(pe, S_ODO + s, "f", 256, PS, free)
            pe_sums(pe, N["n5"])
            pe.wait_ge(*norm_root("n5"))
            pe_sums(pe, N["n6"])
            r = direct_at[-1]
            pe.wait_ge(S(f"raw{r % NRAW}"), need[r])
            rw = raw_of(r)[:, 0:64].rearrange("p (k n) -> p k n", k=KT)
            pe.wait_ge(S("n6_h"), KT)
            for t in range(2):
                for k in range(KT):
                    last = pe.matmul(PS[4][:, 8 * t:8 * t + 8], HFULL[:, k, P * t:P * t + P], rw[:, k, :],
                                     start=(k == 0), stop=(k == KT - 1))
            last.then_inc(S("direct_used"), 1)
            pe.wait_ge(S("y_evac1"), 8)
            for i in range(4):
                t, f = i // 2, i % 2
                for k in range(4):
                    last = pe.transpose(PS[i][:, P * k:P * k + P], HFULL[:, 4 * f + k, P * t:P * t + P], ident)
                last.then_inc(S("htok_full"), 1)
            pe.wait_ge(S("selected"), 1)
            SEL = RT[:, 80:96].rearrange("p (t e) -> p t e", t=2)
            GATE = RT[:, 96:112].rearrange("p (t e) -> p t e", t=2)
            pe.matmul(PS[5][:, 0:8], tri, SEL[:, 0, :], start=True, stop=True)
            pe.matmul(PS[5][:, 8:16], tri, SEL[:, 1, :], start=True, stop=False)
            pe.matmul(PS[5][:, 8:16], ones, SEL[:, 0, :], start=False, stop=True)
            pe.matmul(PS[5][:, 16:24], ones, SEL[:, 0, :], start=True, stop=False)
            pe.matmul(PS[5][:, 16:24], ones, SEL[:, 1, :], start=False, stop=True).then_inc(S("positions"), 1)
            pe.wait_ge(S("htok_low"), 4)
            pe.sem_inc(S("e_slots"), NSP_E)
            pe.wait_ge(S("ident_r"), 1)

            def experts(b):
                g0 = b * NE * NU
                pe.wait_ge(S("onehot"), b + 1)
                if b:
                    pe.wait_ge(S("comb_done"), 4 * NE * b)
                for e in range(NE):
                    for t in range(2):
                        last = pe.matmul(PS[5][:, 32 + e:33 + e], MP[:, t, e, :].bitcast(F32), GATE[:, t, e:e + 1],
                                         start=(t == 0), stop=(t == 1))
                last.then_inc(S("gslot_full"), 1)
                for i in range(4):
                    for e in range(2):
                        for t in range(2):
                            last = pe.matmul(PS[i][:, 256 * e + P * t:256 * e + P * t + P], MP[:, t, 2 * i + e, :],
                                             IDR[:, :], start=True, stop=True)
                    last.then_inc(S("pt_full"), 1)

                def dispatch(e, r):
                    for f in range(4):
                        n = 0
                        for t in range(2):
                            for half in (HTH, HTL):
                                k = P * (4 * r + f)
                                rhs = MP[:, t, e, :] if isinstance(e, int) else \
                                    MP[:, t, bass.ds(e, 1), :].rearrange("p a n -> p (a n)")
                                last = pe.matmul(PS[7][:, P * f:P * f + P], half[:, t, k:k + P], rhs,
                                                 start=(n == 0), stop=(n == 3))
                                n += 1
                    last.then_inc(S("xe_full"), 1)

                dispatch(0, 0)
                pe.wait_ge(S("xe_low"), 2 * (NE + 1) * b + 1)
                dispatch(0, 1)
                pe.wait_ge(S("mpt_done"), 4 * b + 4)
                pe.wait_ge(S("gslot"), b + 1)

                def up(e, i, xkind, j):
                    bank = PS[2 * (j % 2) + (xkind == "b")]
                    for q in range(2):
                        u = 2 * i + q
                        pe.wait_ge(S("e_low"), e * NU + (g0 + u + 1))
                        hi, lo = esplit(u)
                        for k in range(4):
                            a = slice(512 * k, 512 * k + 512)
                            kk = 4 * q + k
                            last = three(pe, bank[:, :], XEH[:, kk, :], XEL[:, kk, :], hi[:, a], lo[:, a],
                                         kk == 0, kk == KT - 1)
                        if q == 0:
                            last.then_inc(S("e_slots"), 1)
                    return last

                def turn(e, j):
                    pe.wait_ge(S("ge_free"), e * JE + (JE * NE * b + j + 2))
                    if j >= 1:
                        pe.wait_ge(S("gt_low"), e * JE + (JE * NE * b + j))
                    g = GE
                    for k in range(4):
                        src = g[:, k // 2, P * (k % 2):P * (k % 2) + P]
                        last = pe.transpose(PS[6][:, P * k:P * k + P], src, ident)
                    last.then_inc(S("gt_full"), 1)

                def down(e, i, j):
                    pe.wait_ge(S("gt_low"), e * JE + (JE * NE * b + j + 1))
                    for q in range(2):
                        u = 2 * i + q
                        pe.wait_ge(S("e_low"), e * NU + (g0 + u + 1))
                        hi, lo = esplit(u)
                        for k in range(2):
                            kk = 2 * q + k
                            gs = slice(P * kk, P * kk + P)
                            for c in range(2):
                                a = slice(D * k + 512 * c, D * k + 512 * c + 512)
                                last = three(pe, PS[4 + c][:, :], GTH[:, j % 2, gs], GTL[:, j % 2, gs], hi[:, a],
                                             lo[:, a], j == 0 and kk == 0, j == JE - 1 and kk == 3)
                        if q == 0:
                            last.then_inc(S("e_slots"), 1)
                    return last

                with pe.Fori(0, NE) as e:
                    pe.wait_ge(S("xe_low"), e * 2 + (2 * (NE + 1) * b + 2))
                    for i, (kind, j) in enumerate(ORDER):
                        if kind == "a":
                            if j >= 2:
                                pe.wait_ge(S("ge_free"), e * JE + (JE * NE * b + j))
                            up(e, i, "a", j).then_inc(S("e_slots"), 1)
                            if j >= 1:
                                turn(e, j - 1)
                        elif kind == "b":
                            up(e, i, "b", j).then_inc(S("e_slots"), 1)
                        elif j < JE - 1:
                            down(e, i, j).then_inc(S("e_slots"), 1)
                            if j == JE - 2:
                                dispatch(e + 1, 0)
                                turn(e, JE - 1)
                                pe.wait_ge(S("xe_low"), e * 2 + (2 * (NE + 1) * b + 3))
                                dispatch(e + 1, 1)
                        else:
                            down(e, i, j).then_inc(S("e_slots"), 1)
                    pe.wait_ge(S("xe_low"), e * 2 + (2 * (NE + 1) * b + 4))
                    for r in range(4):
                        pe.wait_ge(S("ye_low"), e * 2 + (2 * NE * b + r // 2 + 1))
                        if r >= 2:
                            pe.wait_ge(S("comb_done"), e * 4 + (4 * NE * b + r - 1))
                        for f in range(2):
                            k = P * (2 * r + f)
                            o = PS[6 + r % 2][:, 256 * f:256 * f + 256]
                            rhs = MPT[:, bass.ds(e, 1), :].rearrange("p a n -> p (a n)")
                            pe.matmul(o, YEH[:, k:k + P], rhs, start=True, stop=False)
                            last = pe.matmul(o, YEL[:, k:k + P], rhs, start=False, stop=True)
                        last.then_inc(S("comb_full"), 1)
                    pe.wait_ge(S("comb_done"), e * 4 + (4 * NE * b + 4))

            pe.sem_inc(S("ge_free"), 1)
            experts(0)
            more = pe.value_load(SM[0:1, 60:61].bitcast(I32))
            with pe.If(more > 0):
                experts(1)
            pe_sums(pe, N["n7"])
            for i in range(4):
                pe.wait_ge(S("n7_res"), 4 * (i % 2) + 4)
                for k in range(4):
                    src = X[:, 4 * (i % 2) + k, CTX + P * (i // 2):CTX + P * (i // 2) + P]
                    last = pe.transpose(PS[i][:, P * k:P * k + P], src, ident)
                last.then_inc(S("out_full"), 1)


_INS = ["x", "c", "ctx", "c_ctx", "w_mod", "b_mod", "norm_g", "ev_w_in", "ev_w_out", "sgu_w", "sgu_b", "sgu_g",
        "diff_lq1", "diff_lk1", "diff_lq2", "diff_lk2", "diff_subln_g", "ffn_w1", "ffn_w3", "ffn_w2",
        "od_w_in", "od_w_out", "mla_gq", "mla_w_uq", "mla_gkv", "mla_w_ukv", "router_w",
        "moe_w1", "moe_w3", "moe_w2"]


def kernel(**inputs):
    import concourse.bacc as bacc
    from concourse.bass_utils import run_bass_kernel_spmd

    nc = bacc.Bacc("TRN2", target_bir_lowering=False, num_devices=1)
    arrays = {n: np.ascontiguousarray(inputs[n]) for n in _INS}
    used = np.asarray(inputs["na_rpb"])[0, :, 8 - ROWS:8 + ROWS - 1]
    arrays["rpb"] = np.ascontiguousarray(np.tile(used, (1, 1, REPEAT)))
    arrays["consts"], arrays["angles"] = constants()
    w = {}
    for n, a in arrays.items():
        w[n] = nc.dram_tensor(f"in_{n}", a.shape, mybir.dt.from_np(a.dtype), kind="ExternalInput").ap()
    out = nc.dram_tensor("out_0", (1, SEQ, D), F32, kind="ExternalOutput").ap()
    trunk(nc, w, out)
    r = run_bass_kernel_spmd(nc, [{f"in_{n}": a for n, a in arrays.items()}], core_ids=[0])
    return r.results[0]["out_0"]
```

```python
import math

import numpy as np

import concourse.bass as bass
from concourse import mybir
from contextlib import ExitStack

F32 = mybir.dt.float32
F32R = mybir.dt.float32r
I32 = mybir.dt.int32
U32 = mybir.dt.uint32
ALU = mybir.AluOpType
ACT = mybir.ActivationFunctionType
AX = mybir.AxisListType.X

P = 128
D = 1024
KT = D // P
CTX = 256
TOK = 512
SEQ = 256
TT = TOK // P
EPS = 1e-6
GRID = 64
WIN_W = 16
RPB_W = 31
ROWS = SEQ // GRID
REPEAT = GRID + 1
A_W = 512
EV_IN = 2560
OD_IN = 1952
FF = 2816
FT = FF // P
NE = 8
FFE = 3584
JE = FFE // 512
UNIT = 2048
NRAW = 6
NSPLIT = 2
NSP_E = 3
CAP = 128
LAM_INIT = 0.8 - 0.6 * math.exp(-0.3 * 0)

C_ID, C_ONE, C_R0, C_R1, C_TRI, C_IOTA, C_MASK, C_NEG = 0, 128, 256, 384, 480, 608, 736, 800
C_SEL = 864
C_ALL = 896
V_NG, V_C, V_GQ, V_GKV, V_SUB, V_SG, V_ALL = 0, 64, 80, 82, 83, 84, 88


def constants():
    c = np.zeros((P, C_ALL), np.float32)
    i = np.arange(P)
    c[:, C_ID:C_ID + P] = np.eye(P)
    c[:, C_ONE:C_ONE + P] = 1.0
    for k in range(P):
        m = k % 64
        c[k, C_R0 + (k - 32 if m >= 32 else k + 32)] = -1.0 if m >= 32 else 1.0
    for k in range(64, 96):
        m = k - 64
        c[k, C_R1 + (k - 16 if m >= 16 else k + 16)] = -1.0 if m >= 16 else 1.0
    c[:, C_TRI:C_TRI + P] = (i[:, None] < i[None, :])
    c[:, C_IOTA:C_IOTA + P] = i[None, :]
    q, k = i % GRID, np.arange(GRID)
    start = np.clip(q - WIN_W // 2, 0, GRID - WIN_W)
    inside = (k[None, :] >= start[:, None]) & (k[None, :] < start[:, None] + WIN_W)
    c[:, C_MASK:C_MASK + GRID] = inside
    c[:, C_NEG:C_NEG + GRID] = np.where(inside, 0.0, -1e30)
    for r in range(64):
        c[r, C_SEL + 2 * (r % 16) + (r // 16) % 2] = 1.0
    t = np.arange(SEQ)

    def angles(dim):
        n = dim // 4
        inv = (1.0 / (np.float32(10000.0) ** (np.arange(n, dtype=np.float32) / np.float32(n)))).astype(np.float32)
        row, col = (t // GRID).astype(np.float32), (t % GRID).astype(np.float32)
        return np.concatenate([row[:, None] * inv, col[:, None] * inv], axis=-1).astype(np.float32)

    tab = np.zeros((P, 4, SEQ), np.float32)
    a = angles(64)
    tab[:, 0], tab[:, 1] = np.cos(a).T[i % 32], np.sin(a).T[i % 32]
    a = angles(32)
    tab[:, 2] = 1.0
    tab[64:96, 2], tab[64:96, 3] = np.cos(a).T[np.arange(32) % 16], np.sin(a).T[np.arange(32) % 16]
    return c, tab.reshape(P, 4 * SEQ)


def weight_units(w):
    def cols(m, c0, n=256):
        return [(0, (KT, n), m.rearrange("(k p) n -> p k n", p=P)[:, :, c0:c0 + n])]

    def mods(l, m0, m1):
        return [("split", f"mod{l}", cols(w["w_mod"][l], 256 * m)) for m in range(m0, m1)]

    units = [("direct", "sgu", [(0, (4, P), w["sgu_w"][0].rearrange("g p q -> p g q"))])]
    units += mods(0, 0, 8)
    for s in range(10):
        units.append(("split", "ev", cols(w["ev_w_in"][0], 256 * s)))
        units += mods(0, 8 + 2 * s, min(10 + 2 * s, 24))
    units += [("split", "evo", cols(w["ev_w_out"][0], 256 * s)) for s in range(4)]
    for s in range(FT // 2):
        units += [("split", "up", cols(w["ffn_w1"][0], 256 * s)), ("split", "up", cols(w["ffn_w3"][0], 256 * s))]
        units += mods(1, s, min(s + 1, 8))
    down = w["ffn_w2"][0].rearrange("(k p) n -> p k n", p=P)
    units += [("split", "down", [(0, (2, D), down[:, 2 * s:2 * s + 2, :])]) for s in range(FT // 2)]
    od = w["od_w_in"][0]
    for s in range(8):
        units.append(("split", "od", cols(od, min(256 * s, OD_IN - 256))))
        units += mods(1, 8 + 2 * s, 10 + 2 * s)
    units.append(("latent", "latent", [(0, (2, 384), w["mla_w_uq"][0].rearrange("(k p) n -> p k n", p=P)),
                                       (768, (768,), w["mla_w_ukv"][0])]))
    units += [("split", "odo", cols(w["od_w_out"][0], 256 * s)) for s in range(4)]
    units.append(("direct", "router", [(0, (KT, NE), w["router_w"][0].rearrange("(k p) n -> p k n", p=P))]))
    return units


NORMS = ["n0", "sub0", "sub1", "sub2", "sub3", "n1", "n2", "n3", "n4", "cq", "ckv", "n5", "n6", "n7"]


def expert_order():
    order = [("a", 0), ("b", 0)]
    for j in range(1, JE):
        order += [("a", j), ("b", j), ("d", j - 1)]
    return order + [("d", JE - 1)]


ORDER = expert_order()
NU = 2 * len(ORDER)


def trunk(nc, w, out):
    ctx = ExitStack()
    with ctx:
        def sb(name, shape, dt=F32):
            return ctx.enter_context(nc.sbuf_tensor(name, shape, dt))

        sems = {}

        def S(name):
            if name not in sems:
                sems[name] = ctx.enter_context(nc.semaphore(name))
            return sems[name]

        RAW = sb("raw_weights", [P, NRAW, UNIT])
        SPH = sb("split_high", [P, NSPLIT, UNIT], F32R)
        SPL = sb("split_low", [P, NSPLIT, UNIT], F32R)
        X = sb("residual", [P, KT, TOK])
        HH = sb("h_high", [P, KT, TOK], F32R)
        HL = sb("h_low", [P, KT, TOK], F32R)
        Y = sb("y", [P, KT, TOK])
        CON = sb("constants", [P, C_ALL])
        TAB = sb("angles", [P, 4, SEQ])
        IDR = sb("ident_r", [P, P], F32R)
        BM = sb("b_mod_cols", [P, 96])
        VC = sb("vector_cols", [P, V_ALL])
        SC = sb("silu_c", [P, KT, 2])
        SCR = sb("silu_c_halves", [P, 4 * KT + P], F32R)
        MROW = sb("mod_row_buffers", [36, 512])
        MT = sb("mod_tiles", [64, 2, P])
        MOD = sb("modulation", [P, 2, 48, 2])
        VEC = sb("affine", [P, 2, 4, KT, 2])
        SM = sb("small", [P, 64])
        OVS = ExitStack()
        OV = OVS.enter_context(nc.sbuf_tensor("overlay", [P, 12288], F32))
        OVS.close()
        MP = sb("expert_onehot", [P, 2, NE + 1, CAP], F32R)
        MPT = sb("expert_onehot_t", [P, NE, SEQ], F32R)
        XEH, XEL = sb("xe_high", [P, KT, CAP], F32R), sb("xe_low", [P, KT, CAP], F32R)
        GTH, GTL = sb("gt_high", [P, 2, 512], F32R), sb("gt_low", [P, 2, 512], F32R)
        YEH, YEL = sb("ye_high", [P, D], F32R), sb("ye_low", [P, D], F32R)
        PS = [ctx.enter_context(nc.psum_tensor(f"bank{i}", [P, 512], F32)) for i in range(8)]

        ident, ones = CON[:, C_ID:C_ID + P], CON[:, C_ONE:C_ONE + P]
        tri = CON[:, C_TRI:C_TRI + P]

        def ov(a, n, *shape):
            v = OV[:, a:a + n]
            if len(shape) == 2:
                return v.rearrange("p (a b) -> p a b", a=shape[0])
            return v

        SQ, TMP, HF, RS = ov(0, 1024, 2, 512), ov(1024, 1024, 2, 512), ov(2048, 1024, 2, 512), ov(3072, 512)
        QK, V, U = ov(0, 4096, 8, 512), ov(4096, 2048, 4, 512), ov(6144, 2048, 4, 512)
        SV, OUN = ov(8192, 2048, 4, 512), ov(10240, 2048, 4, 512)
        WST, SBB = Y[:, 7, :], Y[:, 6, :]
        PB = Y[:, 0:4, :]
        PT = Y[:, 4:6, :]
        QC, KC, VCT = ov(0, 1024, 4, 256), ov(1024, 2048, 4, 512), ov(3072, 2048, 4, 512)
        CQ, CKV = ov(5120, 512, 2, 256), ov(5632, 512)
        KD, VD, QD = ov(6144, 2048, 4, 512), ov(8192, 2048, 4, 512), ov(10240, 1024, 4, 256)
        BT = ov(11264, 512, 2, 256)
        G = ov(0, FT * 512, FT, 512)
        HFULL = Y[:, :, 256:512]
        YACC = Y[:, :, 0:256]
        HTH = HH[:, 0:4, :].rearrange("p (t f) n -> p t (f n)", t=2)
        HTL = HL[:, 0:4, :].rearrange("p (t f) n -> p t (f n)", t=2)
        YG, GE, SIL = X[:, 0:4, 0:256], X[:, 4:6, 0:256], X[:, 6:8, 0:256]
        RT = ov(10752, 512)
        OUTT = ov(4096, 2048, 2, 1024)

        UNITS = weight_units(w)
        need, count = [], [0] * NRAW
        release, ns, nd = [], 0, 0
        split_at, direct_at = [], []
        of = {}
        full_after = []
        for r, (kind, stage, parts) in enumerate(UNITS):
            count[r % NRAW] += 16 * len(parts)
            need.append(count[r % NRAW])
            if kind == "split":
                of.setdefault(stage, []).append(ns)
                full_after.append((full_after[-1] if ns else 0)
                                  + (0 if stage == "down" else 1 if stage[:3] == "mod" else 2))
                ns += 1
                split_at.append(r)
                release.append(("split_low_done", ns))
            elif kind == "latent":
                latent_at = r
                release.append(("mla_full", 12))
            else:
                nd += 1
                direct_at.append(r)
                release.append(("direct_used", nd))

        stage_of = [UNITS[r][1] for r in split_at]

        def run(stage):
            s, last, out_, i = of[stage][0], of[stage][-1], [], 0
            while s <= last or (s < ns and stage_of[s][:3] == "mod"):
                mod = stage_of[s][:3] == "mod"
                out_.append((s, None if mod else i))
                i += not mod
                s += 1
            return out_

        mod_index = {s: i for i, s in enumerate(of["mod0"] + of["mod1"])}

        def raw_of(r):
            return RAW[:, r % NRAW, :]

        def esplit(u):
            g = u % NSP_E
            if g < NSPLIT:
                return SPH[:, g, :], SPL[:, g, :]
            return (HH[:, 4:8, :].rearrange("p a b -> p (a b)"), HL[:, 4:8, :].rearrange("p a b -> p (a b)"))

        def item_used(b, e, i):
            return S("e_slots"), e * NU + (b * NE * NU + NSP_E + 2 * i + 2)

        def halves(c0):
            return [(0, 0, 256), (1, 256, 512)] if c0 == 0 else [(1, 0, 256)]

        def norm(name, nt, src, width, dim, ready, scratch=(SQ, RS)):
            return dict(name=name, nt=nt, src=src, width=width, dim=dim, ready=ready, sq=scratch[0], rs=scratch[1])

        def xs(c0):
            return lambda t: X[:, t, c0:TOK]

        def ys(c0):
            return lambda t: Y[:, t, c0:TOK]

        N = {
            "n0": norm("n0", KT, xs(0), TOK, D, ("x_in", lambda t: t + 1)),
            "n1": norm("n1", KT, ys(0), TOK, D, ("y_evac0", lambda t: t + 1)),
            "n2": norm("n2", KT, xs(0), TOK, D, ("n1_res", lambda t: t + 1)),
            "n3": norm("n3", KT, ys(0), TOK, D, ("ffn_evac", lambda t: KT)),
            "n4": norm("n4", KT, xs(0), TOK, D, ("n3_res", lambda t: t + 1)),
            "n5": norm("n5", KT, ys(256), SEQ, D, ("y_evac1", lambda t: t + 1)),
            "n6": norm("n6", KT, xs(256), SEQ, D, ("n5_res", lambda t: t + 1)),
            "n7": norm("n7", KT, lambda t: YACC[:, t, :], SEQ, D, ("moe_done", lambda t: 1)),
            "cq": norm("cq", 2, lambda t: CQ[:, t, :], SEQ, 256, ("od_evac", lambda t: 13 + t),
                       (Y[:, 0:2, :], Y[:, 2, :])),
            "ckv": norm("ckv", 1, lambda t: CKV, TOK, P, ("od_evac", lambda t: 15),
                        (Y[:, 3:5, :], Y[:, 5, :])),
        }
        for h in range(4):
            N[f"sub{h}"] = norm(f"sub{h}", 1, lambda t, h=h: OUN[:, h, :], TOK, P, ("o_evac0", lambda t: 16),
                                (SQ[:, h % 2:h % 2 + 1, :], ov(3072 + 512 * h, 512)))

        tiles = 0
        for i, name in enumerate(NORMS):
            N[name]["tiles_before"], N[name]["index"] = tiles, i
            tiles += N[name]["nt"]

        def norm_root(name):
            return S("norm_root"), N[name]["index"] + 1

        def act_square(act, n, t):
            act.wait_ge(S(n["ready"][0]), n["ready"][1](t))
            if t >= 2:
                act.wait_ge(S("squares_used"), n["tiles_before"] + t - 1)
            act.activation(n["sq"][:, t % 2, :n["width"]], n["src"](t), ACT.Square).then_inc(S("squares"), 1)

        def act_squares(act, n):
            for t in range(n["nt"]):
                act_square(act, n, t)

        def act_root(act, n):
            act.wait_ge(S("squares_used"), n["tiles_before"] + n["nt"])
            act.activation(n["rs"][:, :n["width"]], PS[6][:, :n["width"]], ACT.Sqrt,
                           bias=SM[:, 0:1], scale=1.0 / n["dim"]).then_inc(S("norm_root"), 1)

        def pe_sum(pe, n, t):
            pe.wait_ge(S("squares"), n["tiles_before"] + t + 1)
            pe.matmul(PS[6][:, :n["width"]], ones, n["sq"][:, t % 2, :n["width"]],
                      start=(t == 0), stop=(t == n["nt"] - 1)).then_inc(S("squares_used"), 1)

        def pe_sums(pe, n):
            for t in range(n["nt"]):
                pe_sum(pe, n, t)

        own_steps = [0]

        def link(dve, ins):
            own_steps[0] += 1
            ins.then_inc(S("vector_step"), 1)
            dve.wait_ge(S("vector_step"), own_steps[0])

        def dve_rstd(dve, n):
            dve.wait_ge(*norm_root(n["name"]))
            r = n["rs"][:, :n["width"]]
            link(dve, dve.reciprocal(r, r))

        def mod_vectors(l, which):
            return VEC[:, l, 2 * which], MOD[:, l, 24 * which:24 * which + 8]

        def dve_modulate(dve, n, c0, full=False):
            nt, wd = n["nt"], n["width"]

            def tmp(t):
                if t >= 2:
                    dve.wait_ge(S(n["name"] + "_h"), t - 1)
                dve.tensor_tensor(TMP[:, t % 2, :wd], n["src"](t), RS[:, :wd], ALU.mult)\
                   .then_inc(S(n["name"] + "_tmp"), 1)

            tmp(0)
            tmp(1)
            for t in range(nt):
                if not full:
                    dve.wait_ge(S(n["name"] + "_hh"), t + 1)
                    dve.tensor_tensor(HL[:, t, c0:TOK], HF[:, t % 2, :wd], HH[:, t, c0:TOK].bitcast(F32),
                                      ALU.subtract).then_inc(S(n["name"] + "_hl"), 1)
                if t + 2 < nt:
                    tmp(t + 2)

        def act_modulate(act, n, l, which, c0, full=False):
            a, sh = mod_vectors(l, which)
            nt, wd = n["nt"], n["width"]
            for t in range(nt):
                act.wait_ge(S(n["name"] + "_tmp"), t + 1)
                if not full and t >= 2:
                    act.wait_ge(S(n["name"] + "_hl"), t - 1)
                dst = HFULL[:, t, :] if full else HF[:, t % 2, :wd]
                for v, a0, a1 in halves(c0):
                    last = act.activation(dst[:, a0:a1], TMP[:, t % 2, a0:a1], ACT.Identity,
                                          bias=sh[:, t, v:v + 1], scale=a[:, t, v:v + 1])
                last.then_inc(S(n["name"] + "_h"), 1)
                if not full:
                    act.wait_ge(S(n["name"] + "_h"), t + 1)
                    act.activation(HH[:, t, c0:TOK], HF[:, t % 2, :wd], ACT.Copy).then_inc(S(n["name"] + "_hh"), 1)

        def dve_residual(dve, n, l, which, c0):
            gg = VEC[:, l, 2 * which + 1]
            nt, wd = n["nt"], n["width"]

            def tmp(t):
                dve.tensor_tensor(TMP[:, t % 2, :wd], n["src"](t), RS[:, :wd], ALU.mult)\
                   .then_inc(S(n["name"] + "_tmp"), 1)

            tmp(0)
            for t in range(nt):
                if t + 1 < nt:
                    if t >= 1:
                        dve.wait_ge(S(n["name"] + "_res"), t)
                    tmp(t + 1)
                dve.wait_ge(S(n["name"] + "_tmp"), t + 1)
                for v, a0, a1 in halves(c0):
                    xt = X[:, t, c0 + a0:c0 + a1]
                    last = dve.scalar_tensor_tensor(xt, TMP[:, t % 2, a0:a1], gg[:, t, v:v + 1], xt,
                                                    ALU.mult, ALU.add)
                last.then_inc(S(n["name"] + "_res"), 1)

        def act_split(act, s):
            r = split_at[s]
            act.wait_ge(S(f"raw{r % NRAW}"), need[r])
            if s >= NSPLIT:
                act.wait_ge(*unit_used(s - NSPLIT))
            act.activation(SPH[:, s % NSPLIT, :], raw_of(r), ACT.Copy).then_inc(S("split_high_done"), 1)

        def dve_split(dve, s):
            dve.wait_ge(S("split_high_done"), s + 1)
            dve.tensor_tensor(SPL[:, s % NSPLIT, :], raw_of(split_at[s]), SPH[:, s % NSPLIT, :].bitcast(F32),
                              ALU.subtract).then_inc(S("split_low_done"), 1)

        def upto(eng, one):
            at = [0]

            def to(s):
                while at[0] <= min(s, ns - 1):
                    one(eng, at[0])
                    at[0] += 1
            return to

        def three(pe, ps, wh, wl, xh, xl, first, last):
            pe.matmul(ps, wh, xh, start=first, stop=False)
            pe.matmul(ps, wh, xl, start=False, stop=False)
            return pe.matmul(ps, wl, xh, start=False, stop=last)

        def bank_full(s, j):
            return S("bank_full"), full_after[s] - 1 + j

        def unit_used(s):
            if s in of["down"]:
                return S("gk_used"), 2 * of["down"].index(s) + 2
            return S("bank_full"), full_after[s]

        def gemm_unit(pe, s, kind, c0, banks, free, hready=None, offs=(0, 128)):
            hi, lo = SPH[:, s % NSPLIT, :], SPL[:, s % NSPLIT, :]
            pe.wait_ge(S("split_low_done"), s + 1)
            for j in range(2):
                if free[j] is not None:
                    pe.wait_ge(*free[j])
                parts = 1 if kind == "f" else 2
                for q in range(parts):
                    for k in range(KT):
                        if hready is not None and j == 0 and q == 0:
                            pe.wait_ge(S(hready), k + 1)
                        if kind == "f":
                            a = slice(256 * k + offs[j], 256 * k + offs[j] + P)
                            m = three(pe, banks[j][:, :TOK - c0], hi[:, a], lo[:, a], HH[:, k, c0:TOK],
                                      HL[:, k, c0:TOK], k == 0, k == KT - 1)
                        else:
                            tt = 2 * j + q
                            a, b = slice(P * tt, P * tt + P), slice(256 * k, 256 * k + 256)
                            m = three(pe, banks[j][:, 256 * q:256 * q + 256], HH[:, k, a], HL[:, k, a],
                                      hi[:, b], lo[:, b], k == 0, k == KT - 1)
                if j == 0:
                    m.then_inc(S("bank_full"), 1)
            m.then_inc(S("bank_full"), 1)

        def pe_mod(pe, s):
            i = mod_index[s]
            if i % 2 == 0 and i >= 2:
                pe.wait_ge(S("mod_rows"), i // 2)
            pe.wait_ge(S("split_low_done"), s + 1)
            o = PS[7][:, 256 * (i % 2):256 * (i % 2) + 256]
            for k in range(KT):
                for half in (SPH, SPL):
                    last = pe.matmul(o, SCR[:, 4 * k:4 * k + P], half[:, s % NSPLIT, 256 * k:256 * k + 256],
                                     start=(k == 0 and half is SPH), stop=(k == KT - 1 and half is SPL))
            last.then_inc(S("bank_full"), 1)

        def act_mod(act, s):
            i = mod_index[s]
            if i % 2 == 0:
                return
            n = i // 2
            act.wait_ge(*unit_used(s))
            if n >= 2:
                act.wait_ge(S(f"mod_moved{n % 2}"), 64 * (n // 2))
            act.activation(MROW[32 * (n % 2):32 * (n % 2) + 4, :], PS[7][0:4, :], ACT.Copy).then_inc(S("mod_rows"), 1)

        def pool_mod(pool, n):
            pool.wait_ge(S("mod_rows"), n + 1)
            if n >= 8 and n % 4 == 0:
                pool.wait_ge(S("mod_full"), n // 4 - 1)
            for r in range(4):
                pool.dma_start(MT[16 * r + 4 * (n % 4):16 * r + 4 * (n % 4) + 4, (n // 4) % 2, :],
                               MROW[32 * (n % 2) + r:32 * (n % 2) + r + 1, :].rearrange("r (m c) -> r m c", m=4))\
                    .then_inc(S(f"mod_moved{n % 2}"), 16)

        def pe_mod_third(pe, t):
            for b in range(2):
                pe.wait_ge(S(f"mod_moved{b}"), 64 * 2 * (t + 1))
            pe.matmul(PS[6][:, 0:32], MT[0:64, t % 2, :], CON[0:64, C_SEL:C_SEL + 32],
                      start=True, stop=True).then_inc(S("mod_full"), 1)

        def dve_mod_third(dve, t):
            l, m0 = t // 3, 16 * (t % 3)
            dve.wait_ge(S("mod_full"), t + 1)
            dve.tensor_tensor(MOD[:, l, m0:m0 + 16, :], PS[6][:, 0:32].rearrange("p (m v) -> p m v", v=2),
                              BM[:, 48 * l + m0:48 * l + m0 + 16].rearrange("p (m o) -> p m o", o=1)
                              .to_broadcast([P, 16, 2]), ALU.add).then_inc(S("mod_evac"), 1)
            dve.wait_ge(S("mod_evac"), t + 1)

        def dve_affine(dve, l, which, plus_one, m):
            g = VC[:, V_NG + 8 * (4 * l + which):V_NG + 8 * (4 * l + which) + 8]\
                .rearrange("p (m o) -> p m o", o=1).to_broadcast([P, KT, 2])
            return dve.scalar_tensor_tensor(VEC[:, l, which], MOD[:, l, m:m + 8, :], plus_one, g, ALU.add, ALU.mult)

        att0 = []
        for h in range(4):
            for qb in range(4):
                nk = 2 if qb < 2 else 4
                att0.append(dict(
                    q=[QK[64 * m:64 * m + 64, h, P * qb:P * qb + P] for m in range(2)],
                    k=[QK[64 * m:64 * m + 64, 4 + h, 0:P * nk] for m in range(2)],
                    nk=nk, scale=1.0 / math.sqrt(64), bias=None, v=[V[:, kt, P * h:P * h + P] for kt in range(nk)],
                    o=slice(0, P), dst=(h, P * qb)))
        att1 = []
        for h in range(8):
            for qb in range(2):
                p0 = 64 * (h % 2)
                att1.append(dict(
                    q=[QC[p0:p0 + 64, h // 2, P * qb:P * qb + P]], k=[KC[p0:p0 + 64, h // 2, :]],
                    nk=4, scale=1.0 / math.sqrt(64), bias=(h, qb), v=[VCT[:, kt, 64 * h:64 * h + 64] for kt in range(4)],
                    o=slice(p0, p0 + 64), dst=(h // 2, 256 + P * qb)))
        for h in range(4):
            for qb in range(2):
                att1.append(dict(
                    q=[QD[0:96, h, P * qb:P * qb + P]], k=[KD[0:96, h, :]],
                    nk=4, scale=1.0 / math.sqrt(96), bias=None, v=[VD[:, kt, P * h:P * h + P] for kt in range(4)],
                    o=slice(0, P), dst=(4 + h, 256 + P * qb)))
        NB_ = len(att1) - 8

        def pe_attention(pe, a, units, between=None):
            for i in range(len(units) + 2):
                if i < len(units):
                    u = units[i]
                    if i >= 2:
                        pe.wait_ge(S(f"exp{a}"), i - 1)
                    for m in range(len(u["q"])):
                        last = pe.matmul(PS[2 * (i % 2) + m][:, :P * u["nk"]], u["q"][m], u["k"][m],
                                         start=True, stop=True)
                    last.then_inc(S(f"scores{a}"), 1)
                if between is not None:
                    between(i)
                if 1 <= i <= len(units):
                    u = units[i - 1]
                    pe.wait_ge(S(f"prob{a}"), i)
                    if i >= 2:
                        pe.wait_ge(S(f"pt{a}"), i - 1)
                    for kt in range(u["nk"]):
                        last = pe.transpose(PS[4][:, P * kt:P * kt + P], PB[:, 2 * ((i - 1) % 2), P * kt:P * kt + P],
                                            ident)
                    last.then_inc(S(f"ptrans{a}"), 1)
                if i >= 2:
                    u = units[i - 2]
                    pe.wait_ge(S(f"pt{a}"), i - 1)
                    if i >= 3:
                        pe.wait_ge(S(f"o_evac{a}"), i - 2)
                    for kt in range(u["nk"]):
                        last = pe.matmul(PS[5][u["o"], :P], u["v"][kt], PT[:, i % 2, P * kt:P * kt + P],
                                         start=(kt == 0), stop=(kt == u["nk"] - 1))
                    last.then_inc(S(f"o{a}"), 1)

        def act_attention(act, a, units):
            for i in range(len(units) + 2):
                if i < len(units):
                    u = units[i]
                    act.wait_ge(S(f"negmax{a}"), i + 1)
                    if i >= 2:
                        act.wait_ge(S(f"ptrans{a}"), i - 1)
                    n = P * u["nk"]
                    for m in range(len(u["q"])):
                        src = PB[:, 2 * (i % 2), :n] if u["bias"] else PS[2 * (i % 2) + m][:, :n]
                        c = 8 + 8 * (i % 2) + m
                        last = act.activation(PB[:, 2 * (i % 2) + m, :n], src, ACT.Exp, bias=SM[:, c:c + 1],
                                              scale=1.0 if u["bias"] else u["scale"],
                                              accum_out=SM[:, c + 2:c + 3])
                    last.then_inc(S(f"exp{a}"), 1)
                if 1 <= i <= len(units):
                    u = units[i - 1]
                    act.wait_ge(S(f"ptrans{a}"), i)
                    if i >= 3:
                        act.wait_ge(S(f"o{a}"), i - 2)
                    act.activation(PT[:, (i - 1) % 2, :P * u["nk"]], PS[4][:, :P * u["nk"]], ACT.Copy)\
                       .then_inc(S(f"pt{a}"), 1)
                if i >= 2 and a == 1:
                    u = units[i - 2]
                    t, c = u["dst"]
                    act.wait_ge(S("o1"), i - 1)
                    act.activation(HH[u["o"], t, c:c + P], PS[5][u["o"], :P], ACT.Copy).then_inc(S("o_high"), 1)

        def dve_attention(dve, a, units):
            for i in range(len(units) + 2):
                if i < len(units):
                    u = units[i]
                    n = P * u["nk"]
                    dve.wait_ge(S(f"scores{a}"), i + 1)
                    if i >= 2:
                        dve.wait_ge(S(f"exp{a}"), i - 1)
                        dve.wait_ge(S(f"prob{a}"), i - 1)
                    c = 8 + 8 * (i % 2)
                    if u["bias"]:
                        if i >= 2:
                            dve.wait_ge(S(f"ptrans{a}"), i - 1)
                        dve.wait_ge(S("bias_ready"), i + 1)
                        b = PB[:, 2 * (i % 2), :]
                        dve.tensor_scalar(b[:, :CTX], PS[2 * (i % 2)][:, :CTX], u["scale"], None, ALU.mult)\
                           .then_inc(S("biased"), 1)
                        dve.scalar_tensor_tensor(b[:, CTX:], PS[2 * (i % 2)][:, CTX:], u["scale"], BT[:, i % 2, :],
                                                 ALU.mult, ALU.add).then_inc(S("biased"), 1)
                        dve.wait_ge(S("biased"), 2 * i + 2)
                        dve.tensor_reduce(SM[:, c:c + 1], b[:, :], AX, ALU.max, negate=True)\
                           .then_inc(S(f"negmax{a}"), 1)
                    else:
                        for m in range(len(u["q"])):
                            last = dve.tensor_reduce(SM[:, c + 6 + m:c + 7 + m], PS[2 * (i % 2) + m][:, :n], AX,
                                                     ALU.max, negate=True)
                        link(dve, last)
                        dve.tensor_scalar(SM[:, c:c + 2], SM[:, c + 6:c + 8], u["scale"], None, ALU.mult)\
                           .then_inc(S(f"negmax{a}"), 1)
                if 1 <= i <= len(units):
                    u = units[i - 1]
                    n = P * u["nk"]
                    b, c = 2 * ((i - 1) % 2), 8 + 8 * ((i - 1) % 2)
                    dve.wait_ge(S(f"exp{a}"), i)
                    nm = len(u["q"])
                    link(dve, dve.reciprocal(SM[:, c + 4:c + 4 + nm], SM[:, c + 2:c + 2 + nm]))
                    if nm == 2:
                        link(dve, dve.tensor_scalar(PB[:, b + 1, :n], PB[:, b + 1, :n], SM[:, c + 5:c + 6],
                                                    SM[:, 1:2], ALU.mult, ALU.mult))
                        dve.scalar_tensor_tensor(PB[:, b, :n], PB[:, b, :n], SM[:, c + 4:c + 5], PB[:, b + 1, :n],
                                                 ALU.mult, ALU.add).then_inc(S(f"prob{a}"), 1)
                    else:
                        dve.tensor_scalar(PB[:, b, :n], PB[:, b, :n], SM[:, c + 4:c + 5], None, ALU.mult)\
                           .then_inc(S(f"prob{a}"), 1)
                if i >= 2:
                    u = units[i - 2]
                    t, c = u["dst"]
                    if a == 0:
                        dve.wait_ge(S("o0"), i - 1)
                        dve.tensor_copy(OUN[:, t, c:c + P], PS[5][:, :P]).then_inc(S("o_evac0"), 1)
                    else:
                        dve.wait_ge(S("o_high"), i - 1)
                        dve.tensor_tensor(HL[u["o"], t, c:c + P], PS[5][u["o"], :P],
                                          HH[u["o"], t, c:c + P].bitcast(F32), ALU.subtract)\
                           .then_inc(S("o_evac1"), 1)

        def ropes(l):
            if l == 0:
                return [(QK[:, t, CTX:TOK], CON[:, C_R0:C_R0 + P], TAB[:, 0, :], TAB[:, 1, :]) for t in range(8)]
            r, c, s = CON[0:96, C_R1:C_R1 + 96], TAB[0:96, 2, :], TAB[0:96, 3, :]
            return [(QD[0:96, h, :], r, c, s) for h in range(4)] + [(KD[0:96, h, CTX:TOK], r, c, s) for h in range(4)]

        def pe_rope(pe, l, ready):
            for i, (x, r, c, s) in enumerate(ropes(l)):
                pe.wait_ge(*ready(i))
                if i >= 2:
                    pe.wait_ge(S(f"rot_sin{l}"), i - 1)
                pe.matmul(PS[2 + i % 2][0:x.shape[0], :SEQ], r, x, start=True, stop=True).then_inc(S(f"rot{l}"), 1)

        def dve_rope(dve, l):
            for i, (x, r, c, s) in enumerate(ropes(l)):
                n = x.shape[0]
                t1, t2 = Y[0:n, i % 2, 0:256], Y[0:n, i % 2, 256:512]
                dve.wait_ge(S(f"rot{l}"), i + 1)
                if i >= 2:
                    dve.wait_ge(S(f"roped{l}"), i - 1)
                dve.tensor_tensor(t1, PS[2 + i % 2][0:n, :SEQ], s, ALU.mult).then_inc(S(f"rot_sin{l}"), 1)
                link(dve, dve.tensor_tensor(t2, x, c, ALU.mult))
                dve.wait_ge(S(f"rot_sin{l}"), i + 1)
                dve.tensor_tensor(x, t1, t2, ALU.add).then_inc(S(f"roped{l}"), 1)

        block = ctx.enter_context(nc.Block())

        @block.sync
        def _(sp):
            sp.dma_start(CON[:, :], w["consts"]).then_inc(S("consts_in"), 16)
            rows1 = OV[0:96, 0:P]
            sp.dma_start(rows1, w["b_mod"].rearrange("l (m p) -> (l m) p", p=P)).then_inc(S("rows_in"), 16)
            sp.dma_start(OV[V_NG:V_NG + 64, P:2 * P], w["norm_g"].rearrange("l g (m p) -> (l g m) p", p=P))\
              .then_inc(S("rows_in"), 16)
            sp.dma_start(OV[V_C:V_C + 8, P:2 * P], w["c_ctx"].rearrange("(m p) -> m p", p=P)).then_inc(S("rows_in"), 16)
            sp.dma_start(OV[V_C + 8:V_C + 16, P:2 * P], w["c"][0].rearrange("(m p) -> m p", p=P))\
              .then_inc(S("rows_in"), 16)
            sp.dma_start(OV[V_GQ:V_GQ + 2, P:2 * P], w["mla_gq"][0].rearrange("(m p) -> m p", p=P))\
              .then_inc(S("rows_in"), 16)
            sp.dma_start(OV[V_GKV:V_GKV + 1, P:2 * P], w["mla_gkv"]).then_inc(S("rows_in"), 16)
            sp.dma_start(OV[V_SUB:V_SUB + 1, P:2 * P], w["diff_subln_g"]).then_inc(S("rows_in"), 16)
            sp.dma_start(OV[V_SG:V_SG + 4, P:2 * P], w["sgu_g"][0].rearrange("(m p) -> m p", p=P))\
              .then_inc(S("rows_in"), 16)

            def load(r):
                for off, shape, src in UNITS[r][2]:
                    n = int(np.prod(shape))
                    dst = raw_of(r)[:, off:off + n]
                    if len(shape) == 2:
                        dst = dst.rearrange("p (k n) -> p k n", k=shape[0])
                    sp.dma_start(dst, src).then_inc(S(f"raw{r % NRAW}"), 16)

            def expert_load(b, e, u):
                kind, j = ORDER[u // 2]
                i = u % 2
                if kind == "d":
                    src = w["moe_w2"][0][e].rearrange("(k p) n -> p k n", p=P)[:, 4 * j + 2 * i:4 * j + 2 * i + 2, :]
                    dst = RAW[:, u % NRAW, :].rearrange("p (k n) -> p k n", k=2)
                else:
                    m = w["moe_w1" if kind == "a" else "moe_w3"][0][e].rearrange("(k p) n -> p k n", p=P)
                    src = m[:, 4 * i:4 * i + 4, 512 * j:512 * j + 512]
                    dst = RAW[:, u % NRAW, :].rearrange("p (k n) -> p k n", k=4)
                sp.dma_start(dst, src).then_inc(S(f"eraw{u % NRAW}"), 16)

            def experts(b):
                g0 = b * NE * NU
                for u in range(NRAW):
                    if b == 0:
                        sem, v = release[len(UNITS) - NRAW + (u - len(UNITS)) % NRAW]
                        sp.wait_ge(S(sem), v)
                    else:
                        sp.wait_ge(S("e_low"), g0 - NRAW + u + 1)
                    expert_load(b, 0, u)
                with sp.Fori(0, NE - 1) as e:
                    for u in range(NU):
                        sp.wait_ge(S("e_low"), e * NU + (g0 + u + 1))
                        sp.sem_inc(S("loads_let"), 1)
                        n = u + NRAW
                        expert_load(b, e + n // NU, n % NU)
                for u in range(NU - NRAW):
                    sp.wait_ge(S("e_low"), g0 + (NE - 1) * NU + u + 1)
                    expert_load(b, NE - 1, u + NRAW)

            for r in range(len(UNITS)):
                if r >= NRAW:
                    sem, v = release[r - NRAW]
                    sp.wait_ge(S(sem), v)
                load(r)
            experts(0)
            sp.wait_ge(S("flag_ready"), 1)
            more = sp.value_load(SM[0:1, 60:61].bitcast(I32))
            with sp.If(more > 0):
                experts(1)
            for c in range(2):
                sp.wait_ge(S("out_ready"), 2 * c + 2)
                sp.dma_start(out[0, P * c:P * c + P, :], OUTT[:, c, :]).then_inc(S("stored"), 16)
            sp.wait_ge(S("stored"), 32)

        @block.gpsimd
        def _(pool):
            pool.dma_start(Y[:, 0:4, :].rearrange("p (t f) n -> p t (f n)", t=2),
                           w["ctx"][0].rearrange("(t p) d -> p t d", p=P)).then_inc(S("tokens_in"), 16)
            pool.dma_start(Y[:, 4:8, :].rearrange("p (t f) n -> p t (f n)", t=2),
                           w["x"][0].rearrange("(t p) d -> p t d", p=P)).then_inc(S("tokens_in"), 16)
            for i, k in enumerate(("diff_lq1", "diff_lk1", "diff_lq2", "diff_lk2")):
                pool.dma_start(OV[:, 256 + 64 * i:320 + 64 * i], bass.AP(w[k].tensor, 0, [[0, P], [1, 64]]))\
                    .then_inc(S("lambda_in"), 16)
            pool.dma_start(TAB[:, :, :].rearrange("p a b -> p (a b)"), w["angles"]).then_inc(S("angles_in"), 16)
            for n in range(4):
                pool_mod(pool, n)
            pool.wait_ge(S("x_in"), KT)
            pool.dma_start(SBB, bass.AP(w["sgu_b"].tensor, 0, [[0, P], [1, 512]])).then_inc(S("sgu_b_in"), 16)
            for n in range(4, 24):
                pool_mod(pool, n)
            pool.wait_ge(S("n4_hl"), KT)
            for i in range(NB_):
                h, qb = att1[i]["bias"]
                if i >= 2:
                    pool.wait_ge(S("biased"), 2 * i - 2)
                for r in range(2):
                    q_row = 2 * qb + r
                    base = (h * (2 * ROWS - 1) + ROWS - 1 - q_row) * REPEAT * RPB_W + WIN_W - 1
                    pool.dma_start(BT[64 * r:64 * r + 64, i % 2, :].rearrange("p (k n) -> p k n", k=4),
                                   bass.AP(w["rpb"].tensor, base, [[RPB_W - 1, GRID], [REPEAT * RPB_W, ROWS], [1, GRID]]))\
                        .then_inc(S(f"toeplitz{i % 2}"), 16)
                pool.wait_ge(S(f"toeplitz{i % 2}"), 32 * (i // 2 + 1))
                b = BT[:, i % 2, :].rearrange("p (k n) -> p k n", k=4)
                mask = CON[:, C_MASK:C_MASK + GRID].rearrange("p (o n) -> p o n", o=1).to_broadcast([P, 4, GRID])
                neg = CON[:, C_NEG:C_NEG + GRID].rearrange("p (o n) -> p o n", o=1).to_broadcast([P, 4, GRID])
                pool.tensor_tensor(b, b, mask, ALU.mult).then_inc(S("masked"), 1)
                pool.wait_ge(S("masked"), i + 1)
                pool.tensor_tensor(b, b, neg, ALU.add).then_inc(S("bias_ready"), 1)

        @block.scalar
        def _(act):
            act.wait_ge(S("consts_in"), 16)
            act.activation(IDR[:, :], ident, ACT.Copy).then_inc(S("ident_r"), 1)
            act.wait_ge(S("cols_done"), 2)
            act.activation(SC[:, :, 0], VC[:, V_C:V_C + 8], ACT.Silu)
            act.activation(SC[:, :, 1], VC[:, V_C + 8:V_C + 16], ACT.Silu).then_inc(S("silu_c"), 1)
            act.wait_ge(S("silu_c"), 1)
            act.wait_ge(S("halves_clear"), 1)
            act.activation(SCR[:, 0:4 * KT].rearrange("p (k c) -> p k c", c=4)[:, :, 0:2], SC[:, :, :], ACT.Copy)\
               .then_inc(S("silu_high"), 1)
            to = upto(act, act_split)
            to(0)
            act.wait_ge(S("lam_dots"), 1)
            act.activation(SM[:, 4:6], SM[:, 2:4], ACT.Exp).then_inc(S("lam_exp"), 1)
            act.wait_ge(S("eps"), 1)
            for s in range(8):
                to(s + 1)
                act_mod(act, s)
                act_square(act, N["n0"], s)
            act_root(act, N["n0"])
            act.wait_ge(S("affine"), 1)
            act_modulate(act, N["n0"], 0, 0, 0)
            for g, s in run("ev"):
                to(g + 1)
                if s is None:
                    act_mod(act, g)
                    continue
                for j in range(2):
                    act.wait_ge(*bank_full(g, j))
                    b = PS[j]
                    if s < 2:
                        act.activation(U[:, 2 * s + j, :], b[:, :], ACT.Gelu_apprx_tanh).then_inc(S("ev_evac"), 1)
                    elif s < 4:
                        dst = SV[:, 2 * j:2 * j + 2, 256 * (s - 2):256 * (s - 1)]
                        act.activation(dst, b[:, :].rearrange("p (t n) -> p t n", t=2), ACT.Gelu_apprx_tanh)\
                           .then_inc(S("ev_evac"), 1)
                    elif s < 8:
                        act.activation(QK[:, 2 * (s - 4) + j, :], b[:, :], ACT.Copy).then_inc(S("ev_evac"), 1)
                    else:
                        dst = V[:, 2 * j:2 * j + 2, 256 * (s - 8):256 * (s - 7)]
                        act.activation(dst, b[:, :].rearrange("p (t n) -> p t n", t=2), ACT.Copy)\
                           .then_inc(S("ev_evac"), 1)
                if s == 4:
                    act.wait_ge(S("sgu_var"), 1)
                    act.activation(SM[:, 36:40], SM[:, 32:40].rearrange("p (t c) -> p t c", c=2)[:, :, 1] if False
                                   else SM[:, 28:32], ACT.Sqrt, bias=SM[:, 0:1]).then_inc(S("sgu_std"), 1)
            for g in range(4):
                act.wait_ge(S("sgu_out"), g + 1)
                act.activation(HH[:, g, :], U[:, g, :], ACT.Copy).then_inc(S("sgu_high"), 1)
            act_attention(act, 0, att0)
            for h in range(4):
                n = N[f"sub{h}"]
                if h >= 2:
                    act.wait_ge(S("squares_used"), N[f"sub{h - 2}"]["tiles_before"] + 1)
                act_squares(act, n)
                act_root(act, n)
            for h in range(4):
                act.wait_ge(S("sub_out"), h + 1)
                act.activation(HH[:, 4 + h, :], OUN[:, h, :], ACT.Copy).then_inc(S("sub_high"), 1)
            for g, s in run("evo"):
                to(g + 1)
                for j in range(2):
                    act.wait_ge(*bank_full(g, j))
                    act.activation(Y[:, 2 * s + j, :], PS[j][:, :], ACT.Copy).then_inc(S("y_evac0"), 1)
            act_squares(act, N["n1"])
            act_root(act, N["n1"])
            act_squares(act, N["n2"])
            act_root(act, N["n2"])
            act_modulate(act, N["n2"], 0, 1, 0)
            for g, s in run("up"):
                to(g + 1)
                if s is None:
                    act_mod(act, g)
                    continue
                if s % 2 == 0:
                    p = s // 2
                    for j in range(2):
                        act.wait_ge(*bank_full(g, j))
                        if p >= 2:
                            act.wait_ge(S("g_done"), 2 * (p - 2) + j + 1)
                        act.activation(Y[:, 2 * (p % 2) + j, :], PS[(4 * p + j) % 6][:, :], ACT.Silu)\
                           .then_inc(S("silu_done"), 1)
            for k in range(FT):
                act.wait_ge(S("g_done"), k + 1)
                if k == 0:
                    act.wait_ge(*unit_used(of["up"][-1]))
                if k >= 4:
                    act.wait_ge(S("gk_used"), k - 3)
                act.activation(HH[:, k % 4, :], G[:, k, :], ACT.Copy).then_inc(S("gk_high"), 1)
                if k % 2 == 1:
                    to(of["down"][k // 2] + 1)
            act.wait_ge(S("gk_used"), FT)
            for m in range(4):
                act.activation(Y[:, m, :], PS[m][:, :], ACT.Copy).then_inc(S("ffn_evac"), 1)
            act_squares(act, N["n3"])
            act_root(act, N["n3"])
            act_squares(act, N["n4"])
            act_root(act, N["n4"])
            act_modulate(act, N["n4"], 1, 0, 0)
            for g, s in run("od"):
                to(g + 1)
                if s is None:
                    act_mod(act, g)
                    continue
                for j in range(2):
                    act.wait_ge(*bank_full(g, j))
                    b = PS[j]
                    if s < 2:
                        act.activation(QC[:, 2 * s + j, :], b[:, :SEQ], ACT.Copy).then_inc(S("od_evac"), 1)
                    elif s < 4:
                        act.activation(KC[:, 2 * (s - 2) + j, :], b[:, :], ACT.Copy).then_inc(S("od_evac"), 1)
                    elif s < 6:
                        dst = VCT[:, 2 * j:2 * j + 2, 256 * (s - 4):256 * (s - 3)]
                        act.activation(dst, b[:, :].rearrange("p (t n) -> p t n", t=2), ACT.Copy)\
                           .then_inc(S("od_evac"), 1)
                    elif s == 6:
                        act.activation(CQ[:, j, :], b[:, :SEQ], ACT.Copy).then_inc(S("od_evac"), 1)
                    elif j == 0:
                        act.activation(CKV, b[:, :], ACT.Copy).then_inc(S("od_evac"), 1)
                    else:
                        for h in range(4):
                            last = act.activation(KD[64:96, h, :], b[96:128, :], ACT.Copy)
                        last.then_inc(S("od_evac"), 1)
            for n in ("cq", "ckv"):
                act_squares(act, N[n])
                act_root(act, N[n])
            for i in range(12):
                act.wait_ge(S("mla_full"), i + 1)
                b = PS[i % 2]
                if i < 4:
                    act.activation(QD[0:96, i, :], b[0:96, :SEQ], ACT.Copy).then_inc(S("mla_evac"), 1)
                elif i < 8:
                    act.activation(KD[0:64, i - 4, :], b[0:64, :], ACT.Copy).then_inc(S("mla_evac"), 1)
                else:
                    act.activation(VD[:, i - 8, :], b[:, :], ACT.Copy).then_inc(S("mla_evac"), 1)
            act.wait_ge(*unit_used(of["odo"][0] - 1))
            act_attention(act, 1, att1)
            for g, s in run("odo"):
                to(g + 1)
                for j in range(2):
                    act.wait_ge(*bank_full(g, j))
                    act.activation(Y[:, 2 * s + j, 256:512], PS[j][:, :SEQ], ACT.Copy).then_inc(S("y_evac1"), 1)
            act_squares(act, N["n5"])
            act_root(act, N["n5"])
            act_squares(act, N["n6"])
            act_root(act, N["n6"])
            act_modulate(act, N["n6"], 1, 1, 256, full=True)
            for i in range(4):
                act.wait_ge(S("htok_full"), i + 1)
                t, f = i // 2, i % 2
                act.activation(HTH[:, t, 512 * f:512 * f + 512], PS[i][:, :], ACT.Copy).then_inc(S("htok_high"), 1)
            act.wait_ge(S("top_diff"), 1)
            act.activation(RT[:, 64:66], RT[:, 66:68], ACT.Exp).then_inc(S("top_exp"), 1)

            def experts(b):
                g0 = b * NE * NU
                for i in range(4):
                    act.wait_ge(S("pt_full"), 4 * b + i + 1)
                    act.activation(MPT[:, 2 * i:2 * i + 2, :], PS[i][:, :].rearrange("p (e n) -> p e n", e=2),
                                   ACT.Copy).then_inc(S("mpt_done"), 1)

                def xe_high(e, r):
                    act.wait_ge(S("xe_full"), e * 2 + (2 * (NE + 1) * b + r + 1))
                    act.activation(XEH[:, 4 * r:4 * r + 4, :], PS[7][:, :].rearrange("p (f n) -> p f n", f=4),
                                   ACT.Copy).then_inc(S("xe_high"), 1)

                def gt_high(e, j):
                    act.wait_ge(S("gt_full"), e * JE + (JE * NE * b + j + 1))
                    act.activation(GTH[:, j % 2, :], PS[6][:, :], ACT.Copy).then_inc(S("gt_high"), 1)

                xe_high(0, 0)
                xe_high(0, 1)
                with act.Fori(0, NE) as e:
                    for i, (kind, j) in enumerate(ORDER):
                        for u in (2 * i, 2 * i + 1):
                            act.wait_ge(S(f"eraw{u % NRAW}"), e * (16 * NU // NRAW)
                                        + (16 * (NE * NU // NRAW) * b + 16 * (u // NRAW + 1)))
                            act.wait_ge(S("e_slots"), e * NU + (g0 + u + 1))
                            act.activation(esplit(u)[0], RAW[:, u % NRAW, :], ACT.Copy).then_inc(S("e_high"), 1)
                        if i == 0:
                            continue
                        kind, j = ORDER[i - 1]
                        if kind == "a":
                            act.wait_ge(*item_used(b, e, i - 1))
                            act.wait_ge(S("ge_free"), e * JE + (JE * NE * b + j + 1))
                            act.activation(SIL, PS[2 * (j % 2)][:, :].rearrange("p (a n) -> p a n", a=2), ACT.Silu)\
                               .then_inc(S("esilu"), 1)
                            if j >= 1:
                                gt_high(e, j - 1)
                        if kind == "d" and j == JE - 2:
                            xe_high(e + 1, 0)
                            gt_high(e, JE - 1)
                            xe_high(e + 1, 1)
                    for c in range(2):
                        act.wait_ge(S("yg"), e * 2 + (2 * NE * b + c + 1))
                        act.activation(YEH[:, 512 * c:512 * c + 512],
                                       YG[:, 2 * c:2 * c + 2, :].rearrange("p a n -> p a n") if False else
                                       YG[:, 2 * c:2 * c + 2, :], ACT.Copy).then_inc(S("ye_high"), 1)

            experts(0)
            more = act.value_load(SM[0:1, 60:61].bitcast(I32))
            with act.If(more > 0):
                experts(1)
            act_squares(act, N["n7"])
            act_root(act, N["n7"])
            for i in range(4):
                act.wait_ge(S("out_full"), i + 1)
                act.activation(OUTT[:, i // 2, 512 * (i % 2):512 * (i % 2) + 512], PS[i][:, :], ACT.Copy)\
                   .then_inc(S("out_ready"), 1)

        @block.vector
        def _(dve):
            dve.memset(SCR[:, :].bitcast(F32), 0.0).then_inc(S("halves_clear"), 1)
            link(dve, dve.memset(SM[:, :], 0.0))
            dve.memset(SM[:, 0:1], EPS).then_inc(S("eps"), 1)
            dve.wait_ge(S("cols_full"), 2)
            dve.tensor_copy(BM[:, :], PS[0][:, 0:96]).then_inc(S("cols_done"), 1)
            dve.tensor_copy(VC[:, :], PS[1][:, 0:V_ALL]).then_inc(S("cols_done"), 1)
            dve.wait_ge(S("lambda_in"), 64)
            lam = OV[:, 256:512].rearrange("p (a n) -> p a n", a=4)
            for i in range(2):
                last = dve.tensor_tensor(lam[:, 2 * i, :], lam[:, 2 * i, :], lam[:, 2 * i + 1, :], ALU.mult)
            link(dve, last)
            for i in range(2):
                last = dve.tensor_reduce(SM[:, 2 + i:3 + i], lam[:, 2 * i, :], AX, ALU.add)
            last.then_inc(S("lam_dots"), 1)
            dve.wait_ge(S("lam_exp"), 1)
            link(dve, dve.tensor_tensor(SM[:, 6:7], SM[:, 5:6], SM[:, 4:5], ALU.subtract))
            link(dve, dve.tensor_scalar(SM[:, 1:2], SM[:, 6:7], -LAM_INIT, None, ALU.add))
            dve.wait_ge(S("cols_done"), 2)
            link(dve, dve.tensor_scalar(SM[:, 24:25], VC[:, V_SUB:V_SUB + 1], 1.0 - LAM_INIT, None, ALU.mult))
            for f in range(KT):
                dve.wait_ge(S("x_full"), f + 1)
                dve.tensor_copy(X[:, f, :], PS[f % 2][:, :]).then_inc(S("x_in"), 1)
            dve.wait_ge(S("direct_used"), 1)
            dve.tensor_copy(WST, PS[2][:, :]).then_inc(S("wst"), 1)
            dve.wait_ge(S("silu_high"), 1)
            scr = SCR[:, 0:4 * KT].rearrange("p (k c) -> p k c", c=4)
            dve.tensor_tensor(scr[:, :, 2:4], SC[:, :, :], scr[:, :, 0:2].bitcast(F32), ALU.subtract)\
               .then_inc(S("silu_low"), 1)
            to = upto(dve, dve_split)
            to(8)
            dve_mod_third(dve, 0)
            dve_affine(dve, 0, 0, 1.0, 8).then_inc(S("affine"), 1)
            dve_rstd(dve, N["n0"])
            dve_modulate(dve, N["n0"], 0)
            for g, s in run("ev"):
                to(g + 1)
                if s == 6:
                    dve_mod_third(dve, 1)
                if s == 4:
                    dve.wait_ge(S("ev_evac"), 8)
                    for t in range(TT):
                        last = dve.bn_stats(Y[:, 5, 8 * t:8 * t + 6], SV[:, t, :])
                    link(dve, last)
                    for t in range(TT):
                        last = dve.bn_aggr(Y[:, 5, 64 + 2 * t:66 + 2 * t], Y[:, 5, 8 * t:8 * t + 6])
                    link(dve, last)
                    dve.tensor_copy(SM[:, 28:32], Y[:, 5, 64:72].rearrange("p (t c) -> p t c", c=2)[:, :, 1])\
                       .then_inc(S("sgu_var"), 1)
                if s == 5:
                    dve.wait_ge(S("sgu_std"), 1)
                    link(dve, dve.reciprocal(SM[:, 40:44], SM[:, 36:40]))
                    for t in range(TT):
                        last = dve.tensor_scalar(SV[:, t, :], SV[:, t, :], Y[:, 5, 64 + 2 * t:65 + 2 * t],
                                                 SM[:, 40 + t:41 + t], ALU.subtract, ALU.mult)
                    last.then_inc(S("sgu_v"), 1)
            dve_mod_third(dve, 2)
            dve_affine(dve, 0, 1, 0.0, 16)
            dve_affine(dve, 0, 2, 1.0, 32)
            dve_affine(dve, 0, 3, 0.0, 40).then_inc(S("affine"), 1)
            dve.wait_ge(S("angles_in"), 16)
            dve_rope(dve, 0)
            dve.wait_ge(S("sgu_b_in"), 16)
            dve.wait_ge(*unit_used(of["ev"][-1]))
            for g in range(4):
                t1 = Y[:, 4 + g % 2, :]
                dve.wait_ge(S("sgu_full"), g + 1)
                if g >= 2:
                    dve.wait_ge(S("sgu_out"), g - 1)
                bias = SBB[:, P * g:P * g + P].rearrange("p (o n) -> p o n", o=1).to_broadcast([P, TT, P])
                dve.scalar_tensor_tensor(t1.rearrange("p (t n) -> p t n", t=TT),
                                         PS[g % 2][:, :].rearrange("p (t n) -> p t n", t=TT),
                                         VC[:, V_SG + g:V_SG + g + 1], bias, ALU.mult, ALU.add)\
                   .then_inc(S("sgu_mixed"), 1)
                dve.wait_ge(S("sgu_mixed"), g + 1)
                dve.tensor_tensor(U[:, g, :], t1, U[:, g, :], ALU.mult).then_inc(S("sgu_out"), 1)
                dve.wait_ge(S("sgu_high"), g + 1)
                dve.tensor_tensor(HL[:, g, :], U[:, g, :], HH[:, g, :].bitcast(F32), ALU.subtract)\
                   .then_inc(S("mix0"), 1)
            dve_attention(dve, 0, att0)
            for h in range(4):
                n = N[f"sub{h}"]
                dve_rstd(dve, n)
                dve.scalar_tensor_tensor(OUN[:, h, :], OUN[:, h, :], SM[:, 24:25], n["rs"], ALU.mult, ALU.mult)\
                   .then_inc(S("sub_out"), 1)
            for h in range(4):
                dve.wait_ge(S("sub_high"), h + 1)
                dve.tensor_tensor(HL[:, 4 + h, :], OUN[:, h, :], HH[:, 4 + h, :].bitcast(F32), ALU.subtract)\
                   .then_inc(S("mix0"), 1)
            to(of["evo"][-1] + 1)
            dve_rstd(dve, N["n1"])
            dve_residual(dve, N["n1"], 0, 0, 0)
            dve.wait_ge(S("n1_res"), KT)
            dve_rstd(dve, N["n2"])
            dve_modulate(dve, N["n2"], 0)
            for g, s in run("up"):
                to(g + 1)
                if s is not None and s % 2 == 1:
                    p = s // 2
                    for j in range(2):
                        dve.wait_ge(*bank_full(g, j))
                        dve.wait_ge(S("silu_done"), 2 * p + j + 1)
                        dve.tensor_tensor(G[:, 2 * p + j, :], PS[(4 * p + 2 + j) % 6][:, :],
                                          Y[:, 2 * (p % 2) + j, :], ALU.mult).then_inc(S("g_done"), 1)
                if s == 19:
                    dve_mod_third(dve, 3)
                    dve_affine(dve, 1, 0, 1.0, 8).then_inc(S("affine"), 1)
            dve.wait_ge(S("g_done"), FT)
            for k in range(FT):
                dve.wait_ge(S("gk_high"), k + 1)
                dve.tensor_tensor(HL[:, k % 4, :], G[:, k, :], HH[:, k % 4, :].bitcast(F32), ALU.subtract)\
                   .then_inc(S("gk_low"), 1)
                if k % 2 == 1:
                    to(of["down"][k // 2] + 1)
            dve.wait_ge(S("gk_used"), FT)
            for m in range(4, 8):
                dve.tensor_copy(Y[:, m, :], PS[m][:, :]).then_inc(S("ffn_evac"), 1)
            dve_rstd(dve, N["n3"])
            dve.wait_ge(S("ffn_evac"), 8)
            dve_residual(dve, N["n3"], 0, 1, 0)
            dve.wait_ge(S("n3_res"), KT)
            dve_rstd(dve, N["n4"])
            dve_modulate(dve, N["n4"], 0)
            for g, s in run("od"):
                to(g + 1)
                if s == 6:
                    dve_mod_third(dve, 4)
            for name, gain, tiles in (("cq", V_GQ, 2), ("ckv", V_GKV, 1)):
                n = N[name]
                dve_rstd(dve, n)
                for t in range(tiles):
                    last = dve.scalar_tensor_tensor(n["src"](t), n["src"](t), VC[:, gain + t:gain + t + 1],
                                                    n["rs"][:, :n["width"]], ALU.mult, ALU.mult)
                last.then_inc(S("latent"), 1)
            dve_mod_third(dve, 5)
            dve_affine(dve, 1, 1, 0.0, 16)
            dve_affine(dve, 1, 2, 1.0, 32)
            dve_affine(dve, 1, 3, 0.0, 40).then_inc(S("affine"), 1)
            dve.wait_ge(S("affine"), 4)
            dve_rope(dve, 1)
            dve_attention(dve, 1, att1)
            to(ns - 1)
            dve_rstd(dve, N["n5"])
            dve_residual(dve, N["n5"], 1, 0, 256)
            dve.wait_ge(S("n5_res"), KT)
            dve_rstd(dve, N["n6"])
            dve_modulate(dve, N["n6"], 256, full=True)
            LG, MX = RT[:, 0:16].rearrange("p (t e) -> p t e", t=2), RT[:, 16:32].rearrange("p (t e) -> p t e", t=2)
            IX = RT[:, 32:48].bitcast(U32).rearrange("p (t e) -> p t e", t=2)
            IF = RT[:, 48:64].rearrange("p (t e) -> p t e", t=2)
            EXP, DIF, G1, G2 = RT[:, 64:66], RT[:, 66:68], RT[:, 68:70], RT[:, 70:72]
            SEL = RT[:, 80:96].rearrange("p (t e) -> p t e", t=2)
            GATE = RT[:, 96:112].rearrange("p (t e) -> p t e", t=2)
            T1 = RT[:, 112:128].rearrange("p (t e) -> p t e", t=2)
            T2 = RT[:, 128:144].rearrange("p (t e) -> p t e", t=2)
            POS = RT[:, 144:160].rearrange("p (t e) -> p t e", t=2)
            CNT, GSL = RT[:, 160:168], RT[:, 176:184]
            dve.wait_ge(S("direct_used"), len(direct_at))
            link(dve, dve.tensor_copy(LG, PS[4][:, 0:16].rearrange("p (t e) -> p t e", t=2)))
            for t in range(2):
                last = dve.max(MX[:, t, :], LG[:, t, :])
            link(dve, last)
            for t in range(2):
                last = dve.max_index(IX[:, t, :], MX[:, t, :], LG[:, t, :])
            link(dve, last)
            dve.tensor_tensor(DIF, MX[:, :, 1], MX[:, :, 0], ALU.subtract).then_inc(S("top_diff"), 1)
            link(dve, dve.tensor_copy(IF, IX))
            iota8 = CON[:, C_IOTA:C_IOTA + NE]
            for t in range(2):
                dve.tensor_scalar(T1[:, t, :], iota8, IF[:, t, 0:1], None, ALU.is_equal)
                last = dve.tensor_scalar(T2[:, t, :], iota8, IF[:, t, 1:2], None, ALU.is_equal)
            link(dve, last)
            dve.tensor_tensor(SEL, T1, T2, ALU.add).then_inc(S("selected"), 1)
            for i in range(4):
                t, f = i // 2, i % 2
                dve.wait_ge(S("htok_high"), i + 1)
                dve.tensor_tensor(HTL[:, t, 512 * f:512 * f + 512], PS[i][:, :],
                                  HTH[:, t, 512 * f:512 * f + 512].bitcast(F32), ALU.subtract)\
                   .then_inc(S("htok_low"), 1)
            dve.wait_ge(S("top_exp"), 1)
            link(dve, dve.tensor_scalar(G1, EXP, 1.0, None, ALU.add))
            link(dve, dve.reciprocal(G1, G1))
            link(dve, dve.tensor_tensor(G2, G1, EXP, ALU.mult))
            for t in range(2):
                last = dve.tensor_scalar(T1[:, t, :], T1[:, t, :], G1[:, t:t + 1], None, ALU.mult)
            link(dve, last)
            for t in range(2):
                last = dve.scalar_tensor_tensor(GATE[:, t, :], T2[:, t, :], G2[:, t:t + 1], T1[:, t, :],
                                                ALU.mult, ALU.add)
            link(dve, last)
            dve.wait_ge(S("positions"), 1)
            link(dve, dve.scalar_tensor_tensor(POS, PS[5][:, 0:16].rearrange("p (t e) -> p t e", t=2), 1.0, SEL,
                                          ALU.add, ALU.mult))
            link(dve, dve.tensor_scalar(POS, POS, -1.0, None, ALU.add))
            link(dve, dve.tensor_reduce(SM[:, 56:57], PS[5][:, 16:24], AX, ALU.max))
            link(dve, dve.tensor_scalar(SM[:, 57:58], SM[:, 56:57], float(CAP), None, ALU.is_gt))
            dve.tensor_copy(SM[:, 60:61].bitcast(I32), SM[:, 57:58]).then_inc(S("flag_ready"), 1)
            link(dve, dve.memset(YACC, 0.0))

            def experts(b):
                g0 = b * NE * NU
                if b:
                    dve.tensor_scalar(POS, POS, -float(CAP), None, ALU.add).then_inc(S("later_slots"), 1)
                    dve.wait_ge(S("later_slots"), 1)
                for t in range(2):
                    for e in range(NE):
                        dve.tensor_scalar(MP[:, t, e, :], CON[:, C_IOTA:C_IOTA + P], POS[:, t, e:e + 1], None,
                                          ALU.is_equal)
                    last = dve.tensor_scalar(MP[:, t, NE, :], CON[:, C_IOTA:C_IOTA + P], 0.0, None, ALU.mult)
                last.then_inc(S("onehot"), 1)
                dve.wait_ge(S("gslot_full"), b + 1)
                dve.tensor_copy(GSL, PS[5][:, 32:40]).then_inc(S("gslot"), 1)
                dve.wait_ge(S("gslot"), b + 1)

                def xe_low(e, r):
                    dve.wait_ge(S("xe_high"), e * 2 + (2 * (NE + 1) * b + r + 1))
                    dve.tensor_tensor(XEL[:, 4 * r:4 * r + 4, :], PS[7][:, :].rearrange("p (f n) -> p f n", f=4),
                                      XEH[:, 4 * r:4 * r + 4, :].bitcast(F32), ALU.subtract)\
                       .then_inc(S("xe_low"), 1)

                def gt_low(e, j):
                    dve.wait_ge(S("gt_high"), e * JE + (JE * NE * b + j + 1))
                    dve.tensor_tensor(GTL[:, j % 2, :], PS[6][:, :], GTH[:, j % 2, :].bitcast(F32), ALU.subtract)\
                       .then_inc(S("gt_low"), 1)

                xe_low(0, 0)
                xe_low(0, 1)
                with dve.Fori(0, NE) as e:
                    for i, (kind, j) in enumerate(ORDER):
                        for u in (2 * i, 2 * i + 1):
                            dve.wait_ge(S("e_high"), e * NU + (g0 + u + 1))
                            hi, lo = esplit(u)
                            dve.tensor_tensor(lo, RAW[:, u % NRAW, :], hi.bitcast(F32), ALU.subtract)\
                               .then_inc(S("e_low"), 1)
                        if i == 0:
                            continue
                        kind, j = ORDER[i - 1]
                        if kind == "a" and j >= 1:
                            gt_low(e, j - 1)
                        if kind == "b":
                            dve.wait_ge(*item_used(b, e, i - 1))
                            dve.wait_ge(S("esilu"), e * JE + (JE * NE * b + j + 1))
                            if j >= 1:
                                dve.wait_ge(S("gt_full"), e * JE + (JE * NE * b + j))
                            dve.tensor_tensor(GE, PS[2 * (j % 2) + 1][:, :].rearrange("p (a n) -> p a n", a=2), SIL,
                                              ALU.mult).then_inc(S("ge_free"), 1)
                        if kind == "d" and j == JE - 2:
                            xe_low(e + 1, 0)
                            gt_low(e, JE - 1)
                            xe_low(e + 1, 1)
                    dve.wait_ge(*item_used(b, e, len(ORDER) - 1))
                    for c in range(2):
                        dve.tensor_scalar(YG[:, 2 * c:2 * c + 2, :],
                                          PS[4 + c][:, :].rearrange("p (a n) -> p a n", a=2),
                                          GSL[:, bass.ds(e, 1)], None, ALU.mult).then_inc(S("yg"), 1)
                    for c in range(2):
                        dve.wait_ge(S("ye_high"), e * 2 + (2 * NE * b + c + 1))
                        ysl = slice(512 * c, 512 * c + 512)
                        dve.tensor_tensor(YEL[:, ysl].rearrange("p (a n) -> p a n", a=2), YG[:, 2 * c:2 * c + 2, :],
                                          YEH[:, ysl].bitcast(F32).rearrange("p (a n) -> p a n", a=2), ALU.subtract)\
                           .then_inc(S("ye_low"), 1)
                    for r in range(4):
                        dve.wait_ge(S("comb_full"), e * 4 + (4 * NE * b + r + 1))
                        acc = YACC[:, 2 * r:2 * r + 2, :]
                        dve.tensor_tensor(acc, PS[6 + r % 2][:, :].rearrange("p (f n) -> p f n", f=2), acc, ALU.add)\
                           .then_inc(S("comb_done"), 1)

            experts(0)
            more = dve.value_load(SM[0:1, 60:61].bitcast(I32))
            with dve.If(more > 0):
                dve.wait_ge(S("comb_done"), 4 * NE)
                experts(1)
            dve.tensor_scalar(SM[:, 61:62], SM[:, 0:1], 1.0, None, ALU.mult).then_inc(S("moe_done"), 1)
            dve_rstd(dve, N["n7"])
            dve_residual(dve, N["n7"], 1, 1, 256)

        @block.tensor
        def _(pe):
            pe.wait_ge(S("consts_in"), 16)
            pe.wait_ge(S("rows_in"), 8 * 16)
            pe.transpose(PS[0][:, 0:96], OV[0:96, 0:P], CON[0:96, C_ID:C_ID + 96]).then_inc(S("cols_full"), 1)
            pe.transpose(PS[1][:, 0:V_ALL], OV[0:V_ALL, P:2 * P], CON[0:V_ALL, C_ID:C_ID + V_ALL])\
              .then_inc(S("cols_full"), 1)
            pe.wait_ge(S("tokens_in"), 32)
            pe.wait_ge(S("cols_done"), 2)
            for f in range(KT):
                if f >= 2:
                    pe.wait_ge(S("x_in"), f - 1)
                for t in range(TT):
                    c = f * P
                    src = Y[:, 2 * t:2 * t + 2, :].rearrange("p f n -> p (f n)")[:, c:c + P]
                    last = pe.transpose(PS[f % 2][:, P * t:P * t + P], src, ident)
                last.then_inc(S("x_full"), 1)
            pe.wait_ge(S("raw0"), need[0])
            for g in range(4):
                last = pe.transpose(PS[2][:, P * g:P * g + P], raw_of(0)[:, P * g:P * g + P], ident)
            last.then_inc(S("direct_used"), 1)
            pe.wait_ge(S("silu_low"), 1)
            for s in range(8):
                pe_mod(pe, s)
                pe_sum(pe, N["n0"], s)
            pe.wait_ge(*norm_root("n0"))
            pe_mod_third(pe, 0)
            for g, s in run("ev"):
                if s is None:
                    pe_mod(pe, g)
                    continue
                if s in (6, 9):
                    pe_mod_third(pe, 1 if s == 6 else 2)
                kind = "t" if s in (2, 3, 8, 9) else "f"
                free = [(S("ev_evac"), 2 * s - 1 + j) if s else None for j in range(2)]
                gemm_unit(pe, g, kind, 0, PS, free, "n0_hl" if s == 0 else None)
            pe_rope(pe, 0, lambda i: (S("ev_evac"), 9 + i))
            pe.wait_ge(S("sgu_v"), 1)
            pe.wait_ge(S("wst"), 1)
            pe.wait_ge(S("ev_evac"), 20)
            for g in range(4):
                if g >= 2:
                    pe.wait_ge(S("sgu_mixed"), g - 1)
                for t in range(TT):
                    last = pe.matmul(PS[g % 2][:, P * t:P * t + P], SV[:, t, P * g:P * g + P], WST[:, P * g:P * g + P],
                                     start=True, stop=True)
                last.then_inc(S("sgu_full"), 1)
            pe.wait_ge(S("roped0"), 8)
            pe.wait_ge(S("sgu_mixed"), 4)
            pe.wait_ge(S("mod_evac"), 3)
            pe_attention(pe, 0, att0)
            for h in range(4):
                if h >= 1:
                    pe.wait_ge(*norm_root(f"sub{h - 1}"))
                pe_sums(pe, N[f"sub{h}"])
            for g, s in run("evo"):
                free = [(S("y_evac0"), 2 * s - 1 + j) if s else None for j in range(2)]
                gemm_unit(pe, g, "f", 0, PS, free, "mix0" if s == 0 else None)
            pe_sums(pe, N["n1"])
            pe.wait_ge(*norm_root("n1"))
            pe_sums(pe, N["n2"])
            for g, s in run("up"):
                if s is None:
                    pe_mod(pe, g)
                    continue
                if s == 18:
                    pe_mod_third(pe, 3)
                free = [None, None]
                for j in range(2):
                    f = 2 * s + j - 6
                    if f >= 0:
                        free[j] = (S("g_done" if f // 2 % 2 else "silu_done"), 2 * (f // 4) + f % 2 + 1)
                gemm_unit(pe, g, "f", 0, [PS[(2 * s + j) % 6] for j in range(2)], free, "n2_hl" if s == 0 else None)
            pe.wait_ge(S("mod_evac"), 4)
            pe.wait_ge(S("g_done"), FT)
            for d in range(FT // 2):
                s = of["down"][d]
                hi, lo = SPH[:, s % NSPLIT, :], SPL[:, s % NSPLIT, :]
                pe.wait_ge(S("split_low_done"), s + 1)
                for r in range(2):
                    k = 2 * d + r
                    pe.wait_ge(S("gk_low"), k + 1)
                    for m in range(8):
                        a = slice(D * r + P * m, D * r + P * m + P)
                        last = three(pe, PS[m][:, :], hi[:, a], lo[:, a], HH[:, k % 4, :], HL[:, k % 4, :],
                                     k == 0, k == FT - 1)
                    last.then_inc(S("gk_used"), 1)
            pe.wait_ge(S("ffn_evac"), 8)
            pe_sums(pe, N["n3"])
            pe.wait_ge(*norm_root("n3"))
            pe_sums(pe, N["n4"])
            for g, s in run("od"):
                if s is None:
                    pe_mod(pe, g)
                    continue
                if s == 6:
                    pe_mod_third(pe, 4)
                kind, c0 = ("t", 0) if s in (4, 5) else ("f", 256 if s in (0, 1, 6) else 0)
                free = [(S("od_evac"), 2 * s - 1 + j) if s else None for j in range(2)]
                gemm_unit(pe, g, kind, c0, PS, free, "n4_hl" if s == 0 else None,
                          offs=(96, 128) if s == 7 else (0, 128))
            pe.wait_ge(S("mod_evac"), 5)
            pe_sums(pe, N["cq"])
            pe.wait_ge(*norm_root("cq"))
            pe_sums(pe, N["ckv"])
            pe.wait_ge(*norm_root("ckv"))
            pe_mod_third(pe, 5)
            r = latent_at
            pe.wait_ge(S(f"raw{r % NRAW}"), need[r])
            uq, ukv = raw_of(r)[:, 0:768].rearrange("p (k n) -> p k n", k=2), raw_of(r)[:, 768:1536]
            for i in range(12):
                if i == 0:
                    pe.wait_ge(S("latent"), 1)
                if i == 4:
                    pe.wait_ge(S("latent"), 2)
                if i >= 2:
                    pe.wait_ge(S("mla_evac"), i - 1)
                else:
                    pe.wait_ge(S("od_evac"), 16)
                b = PS[i % 2]
                if i < 4:
                    for k in range(2):
                        last = pe.matmul(b[0:96, :SEQ], uq[:, k, 96 * i:96 * i + 96], CQ[:, k, :],
                                         start=(k == 0), stop=(k == 1))
                elif i < 8:
                    c = 192 * (i - 4)
                    last = pe.matmul(b[0:64, :], ukv[:, c:c + 64], CKV, start=True, stop=True)
                else:
                    last = pe.matmul(b[:, :], CKV[:, P * (i - 8):P * (i - 7)],
                                     ukv.rearrange("p (h n) -> p h n", h=4)[:, :, 64:192], start=True, stop=True)
                last.then_inc(S("mla_full"), 1)
            pe_rope(pe, 1, lambda i: (S("mla_evac"), 12))
            pe.wait_ge(S("roped1"), 8)
            pe_attention(pe, 1, att1)
            for g, s in run("odo"):
                free = [(S("y_evac1"), 2 * s - 1 + j) if s else None for j in range(2)]
                if s == 0:
                    pe.wait_ge(S("o_evac1"), len(att1))
                gemm_unit(pe, g, "f", 256, PS, free)
            pe.wait_ge(S("mod_evac"), 6)
            pe_sums(pe, N["n5"])
            pe.wait_ge(*norm_root("n5"))
            pe_sums(pe, N["n6"])
            r = direct_at[-1]
            pe.wait_ge(S(f"raw{r % NRAW}"), need[r])
            rw = raw_of(r)[:, 0:64].rearrange("p (k n) -> p k n", k=KT)
            pe.wait_ge(S("n6_h"), KT)
            for t in range(2):
                for k in range(KT):
                    last = pe.matmul(PS[4][:, 8 * t:8 * t + 8], HFULL[:, k, P * t:P * t + P], rw[:, k, :],
                                     start=(k == 0), stop=(k == KT - 1))
            last.then_inc(S("direct_used"), 1)
            pe.wait_ge(S("y_evac1"), 8)
            for i in range(4):
                t, f = i // 2, i % 2
                for k in range(4):
                    last = pe.transpose(PS[i][:, P * k:P * k + P], HFULL[:, 4 * f + k, P * t:P * t + P], ident)
                last.then_inc(S("htok_full"), 1)
            pe.wait_ge(S("selected"), 1)
            SEL = RT[:, 80:96].rearrange("p (t e) -> p t e", t=2)
            GATE = RT[:, 96:112].rearrange("p (t e) -> p t e", t=2)
            pe.matmul(PS[5][:, 0:8], tri, SEL[:, 0, :], start=True, stop=True)
            pe.matmul(PS[5][:, 8:16], tri, SEL[:, 1, :], start=True, stop=False)
            pe.matmul(PS[5][:, 8:16], ones, SEL[:, 0, :], start=False, stop=True)
            pe.matmul(PS[5][:, 16:24], ones, SEL[:, 0, :], start=True, stop=False)
            pe.matmul(PS[5][:, 16:24], ones, SEL[:, 1, :], start=False, stop=True).then_inc(S("positions"), 1)
            pe.wait_ge(S("htok_low"), 4)
            pe.sem_inc(S("e_slots"), NSP_E)
            pe.wait_ge(S("ident_r"), 1)

            def experts(b):
                g0 = b * NE * NU
                pe.wait_ge(S("onehot"), b + 1)
                if b:
                    pe.wait_ge(S("comb_done"), 4 * NE * b)
                for e in range(NE):
                    for t in range(2):
                        last = pe.matmul(PS[5][:, 32 + e:33 + e], MP[:, t, e, :].bitcast(F32), GATE[:, t, e:e + 1],
                                         start=(t == 0), stop=(t == 1))
                last.then_inc(S("gslot_full"), 1)
                for i in range(4):
                    for e in range(2):
                        for t in range(2):
                            last = pe.matmul(PS[i][:, 256 * e + P * t:256 * e + P * t + P], MP[:, t, 2 * i + e, :],
                                             IDR[:, :], start=True, stop=True)
                    last.then_inc(S("pt_full"), 1)

                def dispatch(e, r):
                    for f in range(4):
                        n = 0
                        for t in range(2):
                            for half in (HTH, HTL):
                                k = P * (4 * r + f)
                                rhs = MP[:, t, e, :] if isinstance(e, int) else \
                                    MP[:, t, bass.ds(e, 1), :].rearrange("p a n -> p (a n)")
                                last = pe.matmul(PS[7][:, P * f:P * f + P], half[:, t, k:k + P], rhs,
                                                 start=(n == 0), stop=(n == 3))
                                n += 1
                    last.then_inc(S("xe_full"), 1)

                dispatch(0, 0)
                pe.wait_ge(S("xe_low"), 2 * (NE + 1) * b + 1)
                dispatch(0, 1)
                pe.wait_ge(S("mpt_done"), 4 * b + 4)
                pe.wait_ge(S("gslot"), b + 1)

                def up(e, i, xkind, j):
                    bank = PS[2 * (j % 2) + (xkind == "b")]
                    for q in range(2):
                        u = 2 * i + q
                        pe.wait_ge(S("e_low"), e * NU + (g0 + u + 1))
                        hi, lo = esplit(u)
                        for k in range(4):
                            a = slice(512 * k, 512 * k + 512)
                            kk = 4 * q + k
                            last = three(pe, bank[:, :], XEH[:, kk, :], XEL[:, kk, :], hi[:, a], lo[:, a],
                                         kk == 0, kk == KT - 1)
                        if q == 0:
                            last.then_inc(S("e_slots"), 1)
                    return last

                def turn(e, j):
                    pe.wait_ge(S("ge_free"), e * JE + (JE * NE * b + j + 2))
                    if j >= 1:
                        pe.wait_ge(S("gt_low"), e * JE + (JE * NE * b + j))
                    g = GE
                    for k in range(4):
                        src = g[:, k // 2, P * (k % 2):P * (k % 2) + P]
                        last = pe.transpose(PS[6][:, P * k:P * k + P], src, ident)
                    last.then_inc(S("gt_full"), 1)

                def down(e, i, j):
                    pe.wait_ge(S("gt_low"), e * JE + (JE * NE * b + j + 1))
                    for q in range(2):
                        u = 2 * i + q
                        pe.wait_ge(S("e_low"), e * NU + (g0 + u + 1))
                        hi, lo = esplit(u)
                        for k in range(2):
                            kk = 2 * q + k
                            gs = slice(P * kk, P * kk + P)
                            for c in range(2):
                                a = slice(D * k + 512 * c, D * k + 512 * c + 512)
                                last = three(pe, PS[4 + c][:, :], GTH[:, j % 2, gs], GTL[:, j % 2, gs], hi[:, a],
                                             lo[:, a], j == 0 and kk == 0, j == JE - 1 and kk == 3)
                        if q == 0:
                            last.then_inc(S("e_slots"), 1)
                    return last

                with pe.Fori(0, NE) as e:
                    pe.wait_ge(S("xe_low"), e * 2 + (2 * (NE + 1) * b + 2))
                    for i, (kind, j) in enumerate(ORDER):
                        if kind == "a":
                            if j >= 2:
                                pe.wait_ge(S("ge_free"), e * JE + (JE * NE * b + j))
                            up(e, i, "a", j).then_inc(S("e_slots"), 1)
                            if j >= 1:
                                turn(e, j - 1)
                        elif kind == "b":
                            up(e, i, "b", j).then_inc(S("e_slots"), 1)
                        elif j < JE - 1:
                            down(e, i, j).then_inc(S("e_slots"), 1)
                            if j == JE - 2:
                                dispatch(e + 1, 0)
                                turn(e, JE - 1)
                                pe.wait_ge(S("xe_low"), e * 2 + (2 * (NE + 1) * b + 3))
                                dispatch(e + 1, 1)
                        else:
                            down(e, i, j).then_inc(S("e_slots"), 1)
                    pe.wait_ge(S("xe_low"), e * 2 + (2 * (NE + 1) * b + 4))
                    for r in range(4):
                        pe.wait_ge(S("ye_low"), e * 2 + (2 * NE * b + r // 2 + 1))
                        if r >= 2:
                            pe.wait_ge(S("comb_done"), e * 4 + (4 * NE * b + r - 1))
                        for f in range(2):
                            k = P * (2 * r + f)
                            o = PS[6 + r % 2][:, 256 * f:256 * f + 256]
                            rhs = MPT[:, bass.ds(e, 1), :].rearrange("p a n -> p (a n)")
                            pe.matmul(o, YEH[:, k:k + P], rhs, start=True, stop=False)
                            last = pe.matmul(o, YEL[:, k:k + P], rhs, start=False, stop=True)
                        last.then_inc(S("comb_full"), 1)
                    pe.wait_ge(S("comb_done"), e * 4 + (4 * NE * b + 4))

            pe.sem_inc(S("ge_free"), 1)
            experts(0)
            more = pe.value_load(SM[0:1, 60:61].bitcast(I32))
            with pe.If(more > 0):
                experts(1)
            pe_sums(pe, N["n7"])
            for i in range(4):
                pe.wait_ge(S("n7_res"), 4 * (i % 2) + 4)
                for k in range(4):
                    src = X[:, 4 * (i % 2) + k, CTX + P * (i // 2):CTX + P * (i // 2) + P]
                    last = pe.transpose(PS[i][:, P * k:P * k + P], src, ident)
                last.then_inc(S("out_full"), 1)


_INS = ["x", "c", "ctx", "c_ctx", "w_mod", "b_mod", "norm_g", "ev_w_in", "ev_w_out", "sgu_w", "sgu_b", "sgu_g",
        "diff_lq1", "diff_lk1", "diff_lq2", "diff_lk2", "diff_subln_g", "ffn_w1", "ffn_w3", "ffn_w2",
        "od_w_in", "od_w_out", "mla_gq", "mla_w_uq", "mla_gkv", "mla_w_ukv", "router_w",
        "moe_w1", "moe_w3", "moe_w2"]


def kernel(**inputs):
    import concourse.bacc as bacc
    from concourse.bass_utils import run_bass_kernel_spmd

    nc = bacc.Bacc("TRN2", target_bir_lowering=False, num_devices=1)
    arrays = {n: np.ascontiguousarray(inputs[n]) for n in _INS}
    used = np.asarray(inputs["na_rpb"])[0, :, 8 - ROWS:8 + ROWS - 1]
    arrays["rpb"] = np.ascontiguousarray(np.tile(used, (1, 1, REPEAT)))
    arrays["consts"], arrays["angles"] = constants()
    w = {}
    for n, a in arrays.items():
        w[n] = nc.dram_tensor(f"in_{n}", a.shape, mybir.dt.from_np(a.dtype), kind="ExternalInput").ap()
    out = nc.dram_tensor("out_0", (1, SEQ, D), F32, kind="ExternalOutput").ap()
    trunk(nc, w, out)
    r = run_bass_kernel_spmd(nc, [{f"in_{n}": a for n, a in arrays.items()}], core_ids=[0])
    return r.results[0]["out_0"]
```

```python
import math

import numpy as np

import concourse.bass as bass
from concourse import mybir
from contextlib import ExitStack

F32 = mybir.dt.float32
F32R = mybir.dt.float32r
I32 = mybir.dt.int32
U32 = mybir.dt.uint32
ALU = mybir.AluOpType
ACT = mybir.ActivationFunctionType
AX = mybir.AxisListType.X

P = 128
D = 1024
KT = D // P
CTX = 256
TOK = 512
SEQ = 256
TT = TOK // P
EPS = 1e-6
GRID = 64
WIN_W = 16
RPB_W = 31
ROWS = SEQ // GRID
REPEAT = GRID + 1
OD_IN = 1952
FF = 2816
FT = FF // P
NE = 8
FFE = 3584
JE = FFE // 512
UNIT = 2048
NRAW = 6
NSPLIT = 2
NSP_E = 3
CAP = 128
LAM_INIT = 0.8 - 0.6 * math.exp(-0.3 * 0)

C_ID, C_ONE, C_R0, C_R1, C_TRI, C_IOTA, C_MASK, C_NEG = 0, 128, 256, 384, 480, 608, 736, 800
C_SEL = 864
C_ALL = 896
V_NG, V_C, V_GQ, V_GKV, V_SUB, V_SG, V_ALL = 0, 64, 80, 82, 83, 84, 88


def constants():
    c = np.zeros((P, C_ALL), np.float32)
    i = np.arange(P)
    c[:, C_ID:C_ID + P] = np.eye(P)
    c[:, C_ONE:C_ONE + P] = 1.0
    for k in range(P):
        m = k % 64
        c[k, C_R0 + (k - 32 if m >= 32 else k + 32)] = -1.0 if m >= 32 else 1.0
    for k in range(64, 96):
        m = k - 64
        c[k, C_R1 + (k - 16 if m >= 16 else k + 16)] = -1.0 if m >= 16 else 1.0
    c[:, C_TRI:C_TRI + P] = (i[:, None] < i[None, :])
    c[:, C_IOTA:C_IOTA + P] = i[None, :]
    q, k = i % GRID, np.arange(GRID)
    start = np.clip(q - WIN_W // 2, 0, GRID - WIN_W)
    inside = (k[None, :] >= start[:, None]) & (k[None, :] < start[:, None] + WIN_W)
    c[:, C_MASK:C_MASK + GRID] = inside
    c[:, C_NEG:C_NEG + GRID] = np.where(inside, 0.0, -1e30)
    for r in range(64):
        c[r, C_SEL + 2 * (r % 16) + (r // 16) % 2] = 1.0
    t = np.arange(SEQ)

    def angles(dim):
        n = dim // 4
        inv = (1.0 / (np.float32(10000.0) ** (np.arange(n, dtype=np.float32) / np.float32(n)))).astype(np.float32)
        row, col = (t // GRID).astype(np.float32), (t % GRID).astype(np.float32)
        return np.concatenate([row[:, None] * inv, col[:, None] * inv], axis=-1).astype(np.float32)

    tab = np.zeros((P, 4, SEQ), np.float32)
    a = angles(64)
    tab[:, 0], tab[:, 1] = np.cos(a).T[i % 32], np.sin(a).T[i % 32]
    a = angles(32)
    tab[:, 2] = 1.0
    tab[64:96, 2], tab[64:96, 3] = np.cos(a).T[np.arange(32) % 16], np.sin(a).T[np.arange(32) % 16]
    return c, tab.reshape(P, 4 * SEQ)


def weight_units(w):
    def cols(m, c0, n=256):
        return [(0, (KT, n), m.rearrange("(k p) n -> p k n", p=P)[:, :, c0:c0 + n])]

    def mods(l, m0, m1):
        return [("split", f"mod{l}", cols(w["w_mod"][l], 256 * m)) for m in range(m0, m1)]

    units = [("direct", "sgu", [(0, (4, P), w["sgu_w"][0].rearrange("g p q -> p g q"))])]
    units += mods(0, 0, 8)
    for s in range(10):
        units.append(("split", "ev", cols(w["ev_w_in"][0], 256 * s)))
        units += mods(0, 8 + 2 * s, min(10 + 2 * s, 24))
    units += [("split", "evo", cols(w["ev_w_out"][0], 256 * s)) for s in range(4)]
    for s in range(FT // 2):
        units += [("split", "up", cols(w["ffn_w1"][0], 256 * s)), ("split", "up", cols(w["ffn_w3"][0], 256 * s))]
        units += mods(1, s, min(s + 1, 8))
    down = w["ffn_w2"][0].rearrange("(k p) n -> p k n", p=P)
    units += [("split", "down", [(0, (2, D), down[:, 2 * s:2 * s + 2, :])]) for s in range(FT // 2)]
    od = w["od_w_in"][0]
    for s in range(8):
        units.append(("split", "od", cols(od, min(256 * s, OD_IN - 256))))
        units += mods(1, 8 + 2 * s, 10 + 2 * s)
    units.append(("latent", "latent", [(0, (2, 384), w["mla_w_uq"][0].rearrange("(k p) n -> p k n", p=P)),
                                       (768, (768,), w["mla_w_ukv"][0])]))
    units += [("split", "odo", cols(w["od_w_out"][0], 256 * s)) for s in range(4)]
    units.append(("direct", "router", [(0, (KT, NE), w["router_w"][0].rearrange("(k p) n -> p k n", p=P))]))
    return units


NORMS = ["n0", "sub0", "sub1", "sub2", "sub3", "n1", "n2", "n3", "n4", "cq", "ckv", "n5", "n6", "n7"]


def expert_order():
    order = [("a", 0), ("b", 0)]
    for j in range(1, JE):
        order += [("a", j), ("b", j), ("d", j - 1)]
    return order + [("d", JE - 1)]


ORDER = expert_order()
NU = 2 * len(ORDER)
XBANK = (7, 2)
PBANK = (0, 1, 3, 6)
CBANK = (6, 7, 2, 3)
TBANK = (4, 7)
OBANK = (5, 6)


def trunk(nc, w, out):
    ctx = ExitStack()
    with ctx:
        def sb(name, shape, dt=F32):
            return ctx.enter_context(nc.sbuf_tensor(name, shape, dt))

        sems = {}

        def S(name):
            if name not in sems:
                sems[name] = ctx.enter_context(nc.semaphore(name))
            return sems[name]

        RAW = sb("raw_weights", [P, NRAW, UNIT])
        SPH = sb("split_high", [P, NSPLIT, UNIT], F32R)
        SPL = sb("split_low", [P, NSPLIT, UNIT], F32R)
        X = sb("residual", [P, KT, TOK])
        HH = sb("h_high", [P, KT, TOK], F32R)
        HL = sb("h_low", [P, KT, TOK], F32R)
        Y = sb("y", [P, KT, TOK])
        CON = sb("constants", [P, C_ALL])
        TAB = sb("angles", [P, 4, SEQ])
        IDR = sb("ident_r", [P, P], F32R)
        BM = sb("b_mod_cols", [P, 96])
        VC = sb("vector_cols", [P, V_ALL])
        SC = sb("silu_c", [P, KT, 2])
        SCR = sb("silu_c_halves", [P, 4 * KT + P], F32R)
        MROW = sb("mod_row_buffers", [36, 512])
        MT = sb("mod_tiles", [64, 2, P])
        MOD = sb("modulation", [P, 2, 48, 2])
        VEC = sb("affine", [P, 2, 4, KT, 2])
        SM = sb("small", [P, 64])
        OVS = ExitStack()
        OV = OVS.enter_context(nc.sbuf_tensor("overlay", [P, 12288], F32))
        OVS.close()
        MP = sb("expert_onehot", [P, 2, NE + 1, CAP], F32R)
        MPT = sb("expert_onehot_t", [P, NE + 1, SEQ], F32R)
        XEH, XEL = sb("xe_high", [P, KT, CAP], F32R), sb("xe_low", [P, KT, CAP], F32R)
        GTH, GTL = sb("gt_high", [P, 2, 512], F32R), sb("gt_low", [P, 2, 512], F32R)
        YEH, YEL = sb("ye_high", [P, D], F32R), sb("ye_low", [P, D], F32R)
        PS = [ctx.enter_context(nc.psum_tensor(f"bank{i}", [P, 512], F32)) for i in range(8)]

        ident, ones = CON[:, C_ID:C_ID + P], CON[:, C_ONE:C_ONE + P]
        tri = CON[:, C_TRI:C_TRI + P]

        def ov(a, n, *shape):
            v = OV[:, a:a + n]
            if len(shape) == 2:
                return v.rearrange("p (a b) -> p a b", a=shape[0])
            return v

        SQ, TMP, HF, RS = ov(0, 1024, 2, 512), ov(1024, 1024, 2, 512), ov(2048, 1024, 2, 512), ov(3072, 512)
        QK, V, U = ov(0, 4096, 8, 512), ov(4096, 2048, 4, 512), ov(6144, 2048, 4, 512)
        SV, OUN = ov(8192, 2048, 4, 512), ov(10240, 2048, 4, 512)
        WST, SBB = Y[:, 7, :], Y[:, 6, :]
        PB = Y[:, 0:4, :]
        PT = [Y[:, 4 + 2 * b:6 + 2 * b, :].rearrange("p a (k n) -> p (a k) n", n=2 * P) for b in range(2)]
        QC, KC, VCT = ov(0, 1024, 4, 256), ov(1024, 2048, 4, 512), ov(3072, 2048, 4, 512)
        CQ, CKV = ov(5120, 512, 2, 256), ov(5632, 512)
        KD, VD, QD = ov(6144, 2048, 4, 512), ov(8192, 2048, 4, 512), ov(10240, 1024, 4, 256)
        BT = ov(11264, 512, 2, 256)
        G = ov(0, FT * 512, FT, 512)
        HFULL = Y[:, :, 256:512]
        YACC = Y[:, :, 0:256]
        HTH = HH[:, 0:4, :].rearrange("p (t f) n -> p t (f n)", t=2)
        HTL = HL[:, 0:4, :].rearrange("p (t f) n -> p t (f n)", t=2)
        YG, GE, SIL = X[:, 0:4, 0:256], X[:, 4:6, 0:256], X[:, 6:8, 0:256]
        RT = ov(10752, 512)
        OUTT = ov(4096, 2048, 2, 1024)

        UNITS = weight_units(w)
        need, count = [], [0] * NRAW
        release, ns, nd = [], 0, 0
        split_at, direct_at = [], []
        of = {}
        full_after = []
        for r, (kind, stage, parts) in enumerate(UNITS):
            count[r % NRAW] += 16 * len(parts)
            need.append(count[r % NRAW])
            if kind == "split":
                of.setdefault(stage, []).append(ns)
                full_after.append((full_after[-1] if ns else 0)
                                  + (0 if stage == "down" else 1 if stage[:3] == "mod" else 2))
                ns += 1
                split_at.append(r)
                release.append(("split_low_done", 2 * ns))
            elif kind == "latent":
                latent_at = r
                release.append(("mla_full", 12))
            else:
                nd += 1
                direct_at.append(r)
                release.append(("direct_used", nd))

        stage_of = [UNITS[r][1] for r in split_at]

        def run(stage):
            s, last, out_, i = of[stage][0], of[stage][-1], [], 0
            while s <= last or (s < ns and stage_of[s][:3] == "mod"):
                mod = stage_of[s][:3] == "mod"
                out_.append((s, None if mod else i))
                i += not mod
                s += 1
            return out_

        token_major = [of["ev"][i] for i in (2, 3, 8, 9)] + [of["od"][i] for i in (4, 5)]

        mod_index = {s: i for i, s in enumerate(of["mod0"] + of["mod1"])}

        def raw_of(r):
            return RAW[:, r % NRAW, :]

        def esplit(u):
            g = u % NSP_E
            if g < NSPLIT:
                return SPH[:, g, :], SPL[:, g, :]
            return (HH[:, 4:8, :].rearrange("p a b -> p (a b)"), HL[:, 4:8, :].rearrange("p a b -> p (a b)"))

        def item_used(b, e, i):
            return S("e_slots"), e * NU + (b * NE * NU + NSP_E + 2 * i + 2)

        def halves(c0):
            return [(0, 0, 256), (1, 256, 512)] if c0 == 0 else [(1, 0, 256)]

        def norm(name, nt, src, width, dim, ready, scratch=(SQ, RS), bank=6):
            return dict(name=name, nt=nt, src=src, width=width, dim=dim, ready=ready, sq=scratch[0], rs=scratch[1],
                        sums=PS[bank][:, :width])

        def xs(c0):
            return lambda t: X[:, t, c0:TOK]

        def ys(c0):
            return lambda t: Y[:, t, c0:TOK]

        N = {
            "n0": norm("n0", KT, xs(0), TOK, D, ("x_in", lambda t: t + 1)),
            "n1": norm("n1", KT, ys(0), TOK, D, ("y_evac0", lambda t: t + 1)),
            "n2": norm("n2", KT, xs(0), TOK, D, ("n1_res", lambda t: t + 1)),
            "n3": norm("n3", KT, ys(0), TOK, D, ("ffn_evac", lambda t: KT)),
            "n4": norm("n4", KT, xs(0), TOK, D, ("n3_res", lambda t: t + 1)),
            "n5": norm("n5", KT, ys(256), SEQ, D, ("y_evac1", lambda t: t + 1)),
            "n6": norm("n6", KT, xs(256), SEQ, D, ("n5_res", lambda t: t + 1)),
            "n7": norm("n7", KT, lambda t: YACC[:, t, :], SEQ, D, ("moe_done", lambda t: 1)),
            "cq": norm("cq", 2, lambda t: CQ[:, t, :], SEQ, 256, ("od_evac", lambda t: 13 + t),
                       (Y[:, 0:2, :], Y[:, 2, :])),
            "ckv": norm("ckv", 1, lambda t: CKV, TOK, P, ("od_evac", lambda t: 15),
                        (Y[:, 3:5, :], Y[:, 5, :]), bank=7),
        }
        for h in range(4):
            N[f"sub{h}"] = norm(f"sub{h}", 1, lambda t, h=h: OUN[:, h, :], TOK, P, ("o_evac0", lambda t: 8),
                                (SQ[:, h % 2:h % 2 + 1, :], ov(3072 + 512 * h, 512)), bank=(2, 3, 4, 7)[h])

        tiles = 0
        for i, name in enumerate(NORMS):
            N[name]["tiles_before"], N[name]["index"] = tiles, i
            tiles += N[name]["nt"]

        def norm_root(name):
            return S("norm_root"), N[name]["index"] + 1

        def act_table(act, func, column):
            act.activation(SM[:, column:column + 1], SM[:, 0:1], func)

        def act_square(act, n, t):
            act.wait_ge(S(n["ready"][0]), n["ready"][1](t))
            if t >= 2:
                act.wait_ge(S("squares_used"), n["tiles_before"] + t - 1)
            act.activation(n["sq"][:, t % 2, :n["width"]], n["src"](t), ACT.Square).then_inc(S("squares"), 1)

        def act_squares(act, n):
            for t in range(n["nt"]):
                act_square(act, n, t)

        def act_root(act, n):
            act.wait_ge(S("squares_used"), n["tiles_before"] + n["nt"])
            act.activation(n["rs"][:, :n["width"]], n["sums"], ACT.Sqrt,
                           bias=SM[:, 0:1], scale=1.0 / n["dim"]).then_inc(S("norm_root"), 1)

        def pe_sum(pe, n, t):
            pe.wait_ge(S("squares"), n["tiles_before"] + t + 1)
            pe.matmul(n["sums"], ones, n["sq"][:, t % 2, :n["width"]],
                      start=(t == 0), stop=(t == n["nt"] - 1)).then_inc(S("squares_used"), 1)

        def pe_sums(pe, n):
            for t in range(n["nt"]):
                pe_sum(pe, n, t)

        def pe_sum_pair(pe, n, s):
            if s >= 0:
                pe_sum(pe, n, 2 * s)
                pe_sum(pe, n, 2 * s + 1)

        own_steps = [0]

        def link(dve, ins):
            own_steps[0] += 1
            ins.then_inc(S("vector_step"), 1)
            dve.wait_ge(S("vector_step"), own_steps[0])

        def dve_rstd(dve, n):
            dve.wait_ge(*norm_root(n["name"]))
            r = n["rs"][:, :n["width"]]
            link(dve, dve.reciprocal(r, r))

        def mod_vectors(l, which):
            return VEC[:, l, 2 * which], MOD[:, l, 24 * which:24 * which + 8]

        def dve_modulate(dve, n, c0, full=False):
            nt, wd = n["nt"], n["width"]

            def tmp(t):
                if t >= 2:
                    dve.wait_ge(S(n["name"] + "_h"), t - 1)
                dve.tensor_tensor(TMP[:, t % 2, :wd], n["src"](t), RS[:, :wd], ALU.mult)\
                   .then_inc(S(n["name"] + "_tmp"), 1)

            tmp(0)
            tmp(1)
            for t in range(nt):
                if not full:
                    dve.wait_ge(S(n["name"] + "_hh"), t + 1)
                    dve.tensor_tensor(HL[:, t, c0:TOK], HF[:, t % 2, :wd], HH[:, t, c0:TOK].bitcast(F32),
                                      ALU.subtract).then_inc(S(n["name"] + "_hl"), 1)
                if t + 2 < nt:
                    tmp(t + 2)

        def act_modulate(act, n, l, which, c0, full=False):
            a, sh = mod_vectors(l, which)
            nt, wd = n["nt"], n["width"]
            for t in range(nt):
                act.wait_ge(S(n["name"] + "_tmp"), t + 1)
                if not full and t >= 2:
                    act.wait_ge(S(n["name"] + "_hl"), t - 1)
                dst = HFULL[:, t, :] if full else HF[:, t % 2, :wd]
                for v, a0, a1 in halves(c0):
                    last = act.activation(dst[:, a0:a1], TMP[:, t % 2, a0:a1], ACT.Identity,
                                          bias=sh[:, t, v:v + 1], scale=a[:, t, v:v + 1])
                last.then_inc(S(n["name"] + "_h"), 1)
                if not full:
                    act.wait_ge(S(n["name"] + "_h"), t + 1)
                    act.activation(HH[:, t, c0:TOK], HF[:, t % 2, :wd], ACT.Copy).then_inc(S(n["name"] + "_hh"), 1)

        def dve_residual(dve, n, l, which, c0):
            gg = VEC[:, l, 2 * which + 1]
            nt, wd = n["nt"], n["width"]

            def tmp(t):
                dve.tensor_tensor(TMP[:, t % 2, :wd], n["src"](t), RS[:, :wd], ALU.mult)\
                   .then_inc(S(n["name"] + "_tmp"), 1)

            tmp(0)
            for t in range(nt):
                if t + 1 < nt:
                    if t >= 1:
                        dve.wait_ge(S(n["name"] + "_res"), t)
                    tmp(t + 1)
                dve.wait_ge(S(n["name"] + "_tmp"), t + 1)
                for v, a0, a1 in halves(c0):
                    xt = X[:, t, c0 + a0:c0 + a1]
                    last = dve.scalar_tensor_tensor(xt, TMP[:, t % 2, a0:a1], gg[:, t, v:v + 1], xt,
                                                    ALU.mult, ALU.add)
                last.then_inc(S(n["name"] + "_res"), 1)

        def half_of(s, j, a):
            if s in of["down"]:
                return a[:, D * j:D * j + D]
            return a.rearrange("p (k n) -> p k n", k=KT)[:, :, P * j:P * j + P]

        def half_free(s, j):
            old = s - NSPLIT
            if s in of["down"] and old in of["down"]:
                return S("gk_used"), 2 * of["down"].index(old) + j + 1
            if s in of["down"] or old in of["down"] or old in token_major:
                return unit_used(old)
            return bank_full(old, j) if stage_of[old][:3] != "mod" else unit_used(old)

        def act_split(act, s, j):
            r = split_at[s]
            if j == 0:
                act.wait_ge(S(f"raw{r % NRAW}"), need[r])
            if s >= NSPLIT:
                act.wait_ge(*half_free(s, j))
            act.activation(half_of(s, j, SPH[:, s % NSPLIT, :]), half_of(s, j, raw_of(r)), ACT.Copy)\
               .then_inc(S("split_high_done"), 1)

        def dve_split(dve, s, j):
            dve.wait_ge(S("split_high_done"), 2 * s + j + 1)
            dve.tensor_tensor(half_of(s, j, SPL[:, s % NSPLIT, :]), half_of(s, j, raw_of(split_at[s])),
                              half_of(s, j, SPH[:, s % NSPLIT, :]).bitcast(F32), ALU.subtract)\
               .then_inc(S("split_low_done"), 1)

        def upto(eng, one):
            at = [0]

            def to(s, j=1):
                while at[0] <= min(2 * s + j, 2 * ns - 1):
                    one(eng, at[0] // 2, at[0] % 2)
                    at[0] += 1
            return to

        def three(pe, ps, wh, wl, xh, xl, first, last):
            pe.matmul(ps, wh, xh, start=first, stop=False)
            pe.matmul(ps, wh, xl, start=False, stop=False)
            return pe.matmul(ps, wl, xh, start=False, stop=last)

        def bank_full(s, j):
            return S("bank_full"), full_after[s] - 1 + j

        def unit_used(s):
            if s in of["down"]:
                return S("gk_used"), 2 * of["down"].index(s) + 2
            return S("bank_full"), full_after[s]

        def gemm_unit(pe, s, kind, c0, banks, free, hready=None, offs=(0, 128)):
            hi, lo = SPH[:, s % NSPLIT, :], SPL[:, s % NSPLIT, :]
            for j in range(2):
                pe.wait_ge(S("split_low_done"), 2 * s + (1 if kind == "f" and offs[j] + P <= P else 2))
                if free[j] is not None:
                    pe.wait_ge(*free[j])
                parts = 1 if kind == "f" else 2
                for q in range(parts):
                    for k in range(KT):
                        if hready is not None and j == 0 and q == 0:
                            pe.wait_ge(S(hready), k + 1)
                        if kind == "f":
                            a = slice(256 * k + offs[j], 256 * k + offs[j] + P)
                            m = three(pe, banks[j][:, :TOK - c0], hi[:, a], lo[:, a], HH[:, k, c0:TOK],
                                      HL[:, k, c0:TOK], k == 0, k == KT - 1)
                        else:
                            tt = 2 * j + q
                            a, b = slice(P * tt, P * tt + P), slice(256 * k, 256 * k + 256)
                            m = three(pe, banks[j][:, 256 * q:256 * q + 256], HH[:, k, a], HL[:, k, a],
                                      hi[:, b], lo[:, b], k == 0, k == KT - 1)
                if j == 0:
                    m.then_inc(S("bank_full"), 1)
            m.then_inc(S("bank_full"), 1)

        def pe_mod(pe, s):
            i = mod_index[s]
            if i % 2 == 0 and i >= 2:
                pe.wait_ge(S("mod_rows"), i // 2)
            pe.wait_ge(S("split_low_done"), 2 * s + 2)
            o = PS[7][:, 256 * (i % 2):256 * (i % 2) + 256]
            for k in range(KT):
                for half in (SPH, SPL):
                    last = pe.matmul(o, SCR[:, 4 * k:4 * k + P], half[:, s % NSPLIT, 256 * k:256 * k + 256],
                                     start=(k == 0 and half is SPH), stop=(k == KT - 1 and half is SPL))
            last.then_inc(S("bank_full"), 1)

        def act_mod(act, s):
            i = mod_index[s]
            if i % 2 == 0:
                return
            n = i // 2
            act.wait_ge(*unit_used(s))
            if n >= 6:
                act.wait_ge(S(f"mod_moved{n % 2}"), 64 * ((n - 4) // 2))
            elif n >= 2:
                act.wait_ge(S(f"first_moved{n % 2}"), 64 * (n // 2))
            act.activation(MROW[32 * (n % 2):32 * (n % 2) + 4, :], PS[7][0:4, :], ACT.Copy).then_inc(S("mod_rows"), 1)
            if n < 4:
                move_rows(act, n, f"first_moved{n % 2}")

        def move_rows(eng, n, moved):
            eng.wait_ge(S("mod_rows"), n + 1)
            if n >= 8 and n % 4 == 0:
                eng.wait_ge(S("mod_full"), n // 4 - 1)
            for r in range(4):
                eng.dma_start(MT[16 * r + 4 * (n % 4):16 * r + 4 * (n % 4) + 4, (n // 4) % 2, :],
                               MROW[32 * (n % 2) + r:32 * (n % 2) + r + 1, :].rearrange("r (m c) -> r m c", m=4))\
                    .then_inc(S(moved), 16)

        def pe_mod_third(pe, t):
            for b in range(2):
                if t == 0:
                    pe.wait_ge(S(f"first_moved{b}"), 64 * 2)
                else:
                    pe.wait_ge(S(f"mod_moved{b}"), 64 * 2 * t)
            pe.matmul(PS[6][:, 0:32], MT[0:64, t % 2, :], CON[0:64, C_SEL:C_SEL + 32],
                      start=True, stop=True).then_inc(S("mod_full"), 1)

        def dve_mod_third(dve, t):
            l, m0 = t // 3, 16 * (t % 3)
            dve.wait_ge(S("mod_full"), t + 1)
            dve.tensor_tensor(MOD[:, l, m0:m0 + 16, :], PS[6][:, 0:32].rearrange("p (m v) -> p m v", v=2),
                              BM[:, 48 * l + m0:48 * l + m0 + 16].rearrange("p (m o) -> p m o", o=1)
                              .to_broadcast([P, 16, 2]), ALU.add).then_inc(S("mod_evac"), 1)
            dve.wait_ge(S("mod_evac"), t + 1)

        def dve_affine(dve, l, which, plus_one, m):
            g = VC[:, V_NG + 8 * (4 * l + which):V_NG + 8 * (4 * l + which) + 8]\
                .rearrange("p (m o) -> p m o", o=1).to_broadcast([P, KT, 2])
            return dve.scalar_tensor_tensor(VEC[:, l, which], MOD[:, l, m:m + 8, :], plus_one, g, ALU.add, ALU.mult)

        att0 = []
        for h in range(4):
            for qb in range(4):
                nk = 2 if qb < 2 else 4
                att0.append(dict(
                    q=[QK[64 * m:64 * m + 64, h, P * qb:P * qb + P] for m in range(2)],
                    k=[QK[64 * m:64 * m + 64, 4 + h, 0:P * nk] for m in range(2)],
                    nk=nk, scale=1.0 / math.sqrt(64), bias=None, v=[V[:, kt, P * h:P * h + P] for kt in range(nk)],
                    o=slice(0, P), dst=(h, P * qb)))
        att1 = []
        for h in range(8):
            for qb in range(2):
                p0 = 64 * (h % 2)
                att1.append(dict(
                    q=[QC[p0:p0 + 64, h // 2, P * qb:P * qb + P]], k=[KC[p0:p0 + 64, h // 2, :]],
                    nk=4, scale=1.0 / math.sqrt(64), bias=(h, qb), v=[VCT[:, kt, 64 * h:64 * h + 64] for kt in range(4)],
                    o=slice(p0, p0 + 64), dst=(h // 2, 256 + P * qb)))
        for h in range(4):
            for qb in range(2):
                att1.append(dict(
                    q=[QD[0:96, h, P * qb:P * qb + P]], k=[KD[0:96, h, :]],
                    nk=4, scale=1.0 / math.sqrt(96), bias=None, v=[VD[:, kt, P * h:P * h + P] for kt in range(4)],
                    o=slice(0, P), dst=(4 + h, 256 + P * qb)))
        NB_ = len(att1) - 8

        def pair_out(units, p):
            u = units[2 * p]
            t, c = u["dst"]
            return PS[OBANK[p % 2]][u["o"], :2 * P], (u["o"], t, slice(c, c + 2 * P))

        def pe_attention(pe, a, units):
            def scores(i):
                u = units[i]
                if i >= 2:
                    pe.wait_ge(S(f"exp{a}"), i - 1)
                for m in range(len(u["q"])):
                    last = pe.matmul(PS[2 * (i % 2) + m][:, :P * u["nk"]], u["q"][m], u["k"][m],
                                     start=True, stop=True)
                last.then_inc(S(f"scores{a}"), 1)

            scores(0)
            scores(1)
            for i in range(1, len(units) + 2):
                if i + 1 < len(units):
                    scores(i + 1)
                if i <= len(units):
                    u = units[i - 1]
                    pe.wait_ge(S(f"prob{a}"), i)
                    if i >= 3:
                        pe.wait_ge(S(f"pt{a}"), i - 2)
                    for kt in range(u["nk"]):
                        last = pe.transpose(PS[TBANK[(i - 1) % 2]][:, P * kt:P * kt + P],
                                            PB[:, 2 * ((i - 1) % 2), P * kt:P * kt + P], ident)
                    last.then_inc(S(f"ptrans{a}"), 1)
                if i >= 3 and i % 2 == 1:
                    p = (i - 2) // 2
                    u = units[2 * p]
                    pe.wait_ge(S(f"pt{a}"), 2 * p + 2)
                    if p >= 2:
                        pe.wait_ge(S(f"o_evac{a}"), p - 1)
                    for kt in range(u["nk"]):
                        last = pe.matmul(pair_out(units, p)[0], u["v"][kt], PT[p % 2][:, kt, :],
                                         start=(kt == 0), stop=(kt == u["nk"] - 1))
                    last.then_inc(S(f"o{a}"), 1)

        def act_attention(act, a, units):
            for i in range(len(units) + 3):
                if i < len(units):
                    u = units[i]
                    act.wait_ge(S(f"negmax{a}"), i + 1)
                    if i >= 2:
                        act.wait_ge(S(f"ptrans{a}"), i - 1)
                    n = P * u["nk"]
                    for m in range(len(u["q"])):
                        src = PB[:, 2 * (i % 2), :n] if u["bias"] else PS[2 * (i % 2) + m][:, :n]
                        c = 8 + 8 * (i % 2) + m
                        last = act.activation(PB[:, 2 * (i % 2) + m, :n], src, ACT.Exp, bias=SM[:, c:c + 1],
                                              scale=1.0 if u["bias"] else u["scale"],
                                              accum_out=SM[:, c + 2:c + 3])
                    last.then_inc(S(f"exp{a}"), 1)
                if 1 <= i <= len(units):
                    u = units[i - 1]
                    p, half = (i - 1) // 2, (i - 1) % 2
                    act.wait_ge(S(f"ptrans{a}"), i)
                    if p >= 2:
                        act.wait_ge(S(f"o{a}"), p - 1)
                    act.activation(PT[p % 2][:, 0:u["nk"], P * half:P * half + P],
                                   PS[TBANK[half]][:, :P * u["nk"]].rearrange("p (k n) -> p k n", n=P), ACT.Copy)\
                       .then_inc(S(f"pt{a}"), 1)
                if i >= 4 and i % 2 == 0 and a == 1:
                    p = (i - 3) // 2
                    act.wait_ge(S("o1"), p + 1)
                    src, dst = pair_out(units, p)
                    act.activation(HH[dst], src, ACT.Copy).then_inc(S("o_high"), 1)

        def dve_attention(dve, a, units):
            lag = 3 + a
            for i in range(len(units) + lag):
                if i < len(units):
                    u = units[i]
                    n = P * u["nk"]
                    dve.wait_ge(S(f"scores{a}"), i + 1)
                    if i >= 2:
                        dve.wait_ge(S(f"exp{a}"), i - 1)
                        dve.wait_ge(S(f"prob{a}"), i - 1)
                    c = 8 + 8 * (i % 2)
                    if u["bias"]:
                        if i >= 2:
                            dve.wait_ge(S(f"ptrans{a}"), i - 1)
                        dve.wait_ge(S("bias_ready"), i + 1)
                        b = PB[:, 2 * (i % 2), :]
                        dve.tensor_scalar(b[:, :CTX], PS[2 * (i % 2)][:, :CTX], u["scale"], None, ALU.mult)\
                           .then_inc(S("biased"), 1)
                        dve.scalar_tensor_tensor(b[:, CTX:], PS[2 * (i % 2)][:, CTX:], u["scale"], BT[:, i % 2, :],
                                                 ALU.mult, ALU.add).then_inc(S("biased"), 1)
                        dve.wait_ge(S("biased"), 2 * i + 2)
                        dve.tensor_reduce(SM[:, c:c + 1], b[:, :], AX, ALU.max, negate=True)\
                           .then_inc(S(f"negmax{a}"), 1)
                    else:
                        for m in range(len(u["q"])):
                            last = dve.tensor_reduce(SM[:, c + 6 + m:c + 7 + m], PS[2 * (i % 2) + m][:, :n], AX,
                                                     ALU.max, negate=True)
                        link(dve, last)
                        dve.tensor_scalar(SM[:, c:c + 2], SM[:, c + 6:c + 8], u["scale"], None, ALU.mult)\
                           .then_inc(S(f"negmax{a}"), 1)
                if 1 <= i <= len(units):
                    u = units[i - 1]
                    n = P * u["nk"]
                    b, c = 2 * ((i - 1) % 2), 8 + 8 * ((i - 1) % 2)
                    dve.wait_ge(S(f"exp{a}"), i)
                    nm = len(u["q"])
                    link(dve, dve.reciprocal(SM[:, c + 4:c + 4 + nm], SM[:, c + 2:c + 2 + nm]))
                    if nm == 2:
                        link(dve, dve.tensor_scalar(PB[:, b + 1, :n], PB[:, b + 1, :n], SM[:, c + 5:c + 6],
                                                    SM[:, 1:2], ALU.mult, ALU.mult))
                        dve.scalar_tensor_tensor(PB[:, b, :n], PB[:, b, :n], SM[:, c + 4:c + 5], PB[:, b + 1, :n],
                                                 ALU.mult, ALU.add).then_inc(S(f"prob{a}"), 1)
                    else:
                        dve.tensor_scalar(PB[:, b, :n], PB[:, b, :n], SM[:, c + 4:c + 5], None, ALU.mult)\
                           .then_inc(S(f"prob{a}"), 1)
                if i >= lag and (i - lag) % 2 == 1:
                    p = (i - lag) // 2
                    src, dst = pair_out(units, p)
                    if a == 0:
                        dve.wait_ge(S("o0"), p + 1)
                        dve.tensor_copy(OUN[dst], src).then_inc(S("o_evac0"), 1)
                    else:
                        dve.wait_ge(S("o_high"), p + 1)
                        dve.tensor_tensor(HL[dst], src, HH[dst].bitcast(F32), ALU.subtract)\
                           .then_inc(S("o_evac1"), 1)

        def pe_sgu(pe, g):
            if g >= 2:
                pe.wait_ge(S("sgu_mixed"), g - 1)
            for t in range(TT):
                last = pe.matmul(PS[2 + g % 2][:, P * t:P * t + P], SV[:, t, P * g:P * g + P], WST[:, P * g:P * g + P],
                                 start=True, stop=True)
            last.then_inc(S("sgu_full"), 1)

        def dve_sgu(dve, g):
            t1 = Y[:, 4 + g % 2, :]
            dve.wait_ge(S("sgu_full"), g + 1)
            if g >= 2:
                dve.wait_ge(S("sgu_out"), g - 1)
            bias = SBB[:, P * g:P * g + P].rearrange("p (o n) -> p o n", o=1).to_broadcast([P, TT, P])
            dve.scalar_tensor_tensor(t1.rearrange("p (t n) -> p t n", t=TT),
                                     PS[2 + g % 2][:, :].rearrange("p (t n) -> p t n", t=TT),
                                     VC[:, V_SG + g:V_SG + g + 1], bias, ALU.mult, ALU.add)\
               .then_inc(S("sgu_mixed"), 1)
            dve.wait_ge(S("sgu_mixed"), g + 1)
            dve.tensor_tensor(U[:, g, :], t1, U[:, g, :], ALU.mult).then_inc(S("sgu_out"), 1)

        def ropes(l):
            if l == 0:
                return [(QK[:, t, CTX:TOK], CON[:, C_R0:C_R0 + P], TAB[:, 0, :], TAB[:, 1, :]) for t in range(8)]
            r, c, s = CON[0:96, C_R1:C_R1 + 96], TAB[0:96, 2, :], TAB[0:96, 3, :]
            return [(QD[0:96, h, :], r, c, s) for h in range(4)] + [(KD[0:96, h, CTX:TOK], r, c, s) for h in range(4)]

        def pe_rope(pe, l, ready, tiles=range(8)):
            for i in tiles:
                x, r, c, s = ropes(l)[i]
                pe.wait_ge(*ready(i))
                if i >= 2:
                    pe.wait_ge(S(f"rot_sin{l}"), i - 1)
                pe.matmul(PS[4 + i % 2][0:x.shape[0], :SEQ], r, x, start=True, stop=True).then_inc(S(f"rot{l}"), 1)

        def dve_rope(dve, l, tiles=range(8)):
            for i in tiles:
                x, r, c, s = ropes(l)[i]
                n = x.shape[0]
                t1, t2 = Y[0:n, i % 2, 0:256], Y[0:n, i % 2, 256:512]
                dve.wait_ge(S(f"rot{l}"), i + 1)
                if i >= 2:
                    dve.wait_ge(S(f"roped{l}"), i - 1)
                dve.tensor_tensor(t1, PS[4 + i % 2][0:n, :SEQ], s, ALU.mult).then_inc(S(f"rot_sin{l}"), 1)
                link(dve, dve.tensor_tensor(t2, x, c, ALU.mult))
                dve.wait_ge(S(f"rot_sin{l}"), i + 1)
                dve.tensor_tensor(x, t1, t2, ALU.add).then_inc(S(f"roped{l}"), 1)

        block = ctx.enter_context(nc.Block())

        @block.sync
        def _(sp):
            sp.dma_start(CON[:, :], w["consts"]).then_inc(S("consts_in"), 16)
            rows1 = OV[0:96, 0:P]
            sp.dma_start(rows1, w["b_mod"].rearrange("l (m p) -> (l m) p", p=P)).then_inc(S("rows_in"), 16)
            sp.dma_start(OV[V_NG:V_NG + 64, P:2 * P], w["norm_g"].rearrange("l g (m p) -> (l g m) p", p=P))\
              .then_inc(S("rows_in"), 16)
            sp.dma_start(OV[V_C:V_C + 8, P:2 * P], w["c_ctx"].rearrange("(m p) -> m p", p=P)).then_inc(S("rows_in"), 16)
            sp.dma_start(OV[V_C + 8:V_C + 16, P:2 * P], w["c"][0].rearrange("(m p) -> m p", p=P))\
              .then_inc(S("rows_in"), 16)
            sp.dma_start(OV[V_GQ:V_GQ + 2, P:2 * P], w["mla_gq"][0].rearrange("(m p) -> m p", p=P))\
              .then_inc(S("rows_in"), 16)
            sp.dma_start(OV[V_GKV:V_GKV + 1, P:2 * P], w["mla_gkv"]).then_inc(S("rows_in"), 16)
            sp.dma_start(OV[V_SUB:V_SUB + 1, P:2 * P], w["diff_subln_g"]).then_inc(S("rows_in"), 16)
            sp.dma_start(OV[V_SG:V_SG + 4, P:2 * P], w["sgu_g"][0].rearrange("(m p) -> m p", p=P))\
              .then_inc(S("rows_in"), 16)

            def load(r):
                for off, shape, src in UNITS[r][2]:
                    n = int(np.prod(shape))
                    dst = raw_of(r)[:, off:off + n]
                    if len(shape) == 2:
                        dst = dst.rearrange("p (k n) -> p k n", k=shape[0])
                    sp.dma_start(dst, src).then_inc(S(f"raw{r % NRAW}"), 16)

            def expert_load(b, e, u):
                kind, j = ORDER[u // 2]
                i = u % 2
                if kind == "d":
                    src = w["moe_w2"][0][e].rearrange("(k p) n -> p k n", p=P)[:, 4 * j + 2 * i:4 * j + 2 * i + 2, :]
                    dst = RAW[:, u % NRAW, :].rearrange("p (k n) -> p k n", k=2)
                else:
                    m = w["moe_w1" if kind == "a" else "moe_w3"][0][e].rearrange("(k p) n -> p k n", p=P)
                    src = m[:, 4 * i:4 * i + 4, 512 * j:512 * j + 512]
                    dst = RAW[:, u % NRAW, :].rearrange("p (k n) -> p k n", k=4)
                sp.dma_start(dst, src).then_inc(S(f"eraw{u % NRAW}"), 16)

            def experts(b):
                g0 = b * NE * NU
                for u in range(NRAW):
                    if b == 0:
                        sem, v = release[len(UNITS) - NRAW + (u - len(UNITS)) % NRAW]
                        sp.wait_ge(S(sem), v)
                    else:
                        sp.wait_ge(S("e_low"), g0 - NRAW + u + 1)
                    expert_load(b, 0, u)
                with sp.Fori(0, NE - 1) as e:
                    for u in range(NU):
                        sp.wait_ge(S("e_low"), e * NU + (g0 + u + 1))
                        sp.sem_inc(S("loads_let"), 1)
                        n = u + NRAW
                        expert_load(b, e + n // NU, n % NU)
                for u in range(NU - NRAW):
                    sp.wait_ge(S("e_low"), g0 + (NE - 1) * NU + u + 1)
                    expert_load(b, NE - 1, u + NRAW)

            for r in range(len(UNITS)):
                if r >= NRAW:
                    sem, v = release[r - NRAW]
                    sp.wait_ge(S(sem), v)
                load(r)
            sp.wait_ge(S("n4_hl"), KT)
            for i in range(NB_):
                h, qb = att1[i]["bias"]
                if i >= 2:
                    sp.wait_ge(S("biased"), 2 * i - 2)
                for r in range(2):
                    q_row = 2 * qb + r
                    base = (h * (2 * ROWS - 1) + ROWS - 1 - q_row) * REPEAT * RPB_W + WIN_W - 1
                    sp.dma_start(BT[64 * r:64 * r + 64, i % 2, :].rearrange("p (k n) -> p k n", k=4),
                                 bass.AP(w["rpb"].tensor, base, [[RPB_W - 1, GRID], [REPEAT * RPB_W, ROWS], [1, GRID]]))\
                      .then_inc(S(f"toeplitz{i % 2}"), 16)
            experts(0)
            sp.wait_ge(S("flag_ready"), 1)
            more = sp.value_load(SM[0:1, 60:61].bitcast(I32))
            with sp.If(more > 0):
                experts(1)
            for c in range(2):
                sp.wait_ge(S("out_ready"), 2 * c + 2)
                sp.dma_start(out[0, P * c:P * c + P, :], OUTT[:, c, :]).then_inc(S("stored"), 16)
            sp.wait_ge(S("stored"), 32)

        @block.gpsimd
        def _(pool):
            pool.dma_start(Y[:, 0:4, :].rearrange("p (t f) n -> p t (f n)", t=2),
                           w["ctx"][0].rearrange("(t p) d -> p t d", p=P)).then_inc(S("tokens_in"), 16)
            pool.dma_start(Y[:, 4:8, :].rearrange("p (t f) n -> p t (f n)", t=2),
                           w["x"][0].rearrange("(t p) d -> p t d", p=P)).then_inc(S("tokens_in"), 16)
            for i, k in enumerate(("diff_lq1", "diff_lk1", "diff_lq2", "diff_lk2")):
                pool.dma_start(OV[:, 256 + 64 * i:320 + 64 * i], bass.AP(w[k].tensor, 0, [[0, P], [1, 64]]))\
                    .then_inc(S("lambda_in"), 16)
            pool.dma_start(TAB[:, :, :].rearrange("p a b -> p (a b)"), w["angles"]).then_inc(S("angles_in"), 16)
            pool.wait_ge(S("x_in"), KT)
            pool.dma_start(SBB, bass.AP(w["sgu_b"].tensor, 0, [[0, P], [1, 512]])).then_inc(S("sgu_b_in"), 16)
            for n in range(4, 24):
                move_rows(pool, n, f"mod_moved{n % 2}")
            for i in range(NB_):
                pool.wait_ge(S(f"toeplitz{i % 2}"), 32 * (i // 2 + 1))
                b = BT[:, i % 2, :].rearrange("p (k n) -> p k n", k=4)
                mask = CON[:, C_MASK:C_MASK + GRID].rearrange("p (o n) -> p o n", o=1).to_broadcast([P, 4, GRID])
                neg = CON[:, C_NEG:C_NEG + GRID].rearrange("p (o n) -> p o n", o=1).to_broadcast([P, 4, GRID])
                pool.tensor_tensor(b, b, mask, ALU.mult).then_inc(S("masked"), 1)
                pool.wait_ge(S("masked"), i + 1)
                pool.tensor_tensor(b, b, neg, ALU.add).then_inc(S("bias_ready"), 1)

        @block.scalar
        def _(act):
            act.wait_ge(S("consts_in"), 16)
            act.activation(IDR[:, :], ident, ACT.Copy).then_inc(S("ident_r"), 1)
            act.wait_ge(S("cols_done"), 2)
            act.activation(SC[:, :, 0], VC[:, V_C:V_C + 8], ACT.Silu)
            act.activation(SC[:, :, 1], VC[:, V_C + 8:V_C + 16], ACT.Silu).then_inc(S("silu_c"), 1)
            act.wait_ge(S("silu_c"), 1)
            act.wait_ge(S("halves_clear"), 1)
            act.activation(SCR[:, 0:4 * KT].rearrange("p (k c) -> p k c", c=4)[:, :, 0:2], SC[:, :, :], ACT.Copy)\
               .then_inc(S("silu_high"), 1)
            to = upto(act, act_split)
            to(0)
            act.wait_ge(S("lam_dots"), 1)
            act.activation(SM[:, 4:6], SM[:, 2:4], ACT.Exp).then_inc(S("lam_exp"), 1)
            act.wait_ge(S("eps"), 1)
            for s in range(8):
                act_square(act, N["n0"], s)
                to(s + 1)
                act_mod(act, s)
            act_root(act, N["n0"])
            act.wait_ge(S("affine"), 1)
            act_modulate(act, N["n0"], 0, 0, 0)
            for g, s in run("ev"):
                to(g + 1)
                if s is None:
                    act_mod(act, g)
                    continue
                for j in range(2):
                    act.wait_ge(*bank_full(g, j))
                    b = PS[j]
                    if s < 2:
                        act.activation(U[:, 2 * s + j, :], b[:, :], ACT.Gelu_apprx_tanh).then_inc(S("ev_evac"), 1)
                    elif s < 4:
                        dst = SV[:, 2 * j:2 * j + 2, 256 * (s - 2):256 * (s - 1)]
                        act.activation(dst, b[:, :].rearrange("p (t n) -> p t n", t=2), ACT.Gelu_apprx_tanh)\
                           .then_inc(S("ev_evac"), 1)
                    elif s < 8:
                        act.activation(QK[:, 2 * (s - 4) + j, :], b[:, :], ACT.Copy).then_inc(S("ev_evac"), 1)
                    else:
                        dst = V[:, 2 * j:2 * j + 2, 256 * (s - 8):256 * (s - 7)]
                        act.activation(dst, b[:, :].rearrange("p (t n) -> p t n", t=2), ACT.Copy)\
                           .then_inc(S("ev_evac"), 1)
                    to(g + 2, j)
                if s == 4:
                    act.wait_ge(S("sgu_var"), 1)
                    act.activation(SM[:, 36:40], SM[:, 28:32], ACT.Sqrt, bias=SM[:, 0:1]).then_inc(S("sgu_std"), 1)
            act.wait_ge(*unit_used(of["ev"][-1]))
            for g in range(4):
                act.wait_ge(S("sgu_out"), g + 1)
                act.activation(HH[:, g, :], U[:, g, :], ACT.Copy).then_inc(S("sgu_high"), 1)
            act_attention(act, 0, att0)
            act_table(act, ACT.Sqrt, 48)
            for h in range(5):
                if h < 4:
                    if h >= 2:
                        act.wait_ge(S("squares_used"), N[f"sub{h - 2}"]["tiles_before"] + 1)
                    act_squares(act, N[f"sub{h}"])
                if h >= 1:
                    act_root(act, N[f"sub{h - 1}"])
            for h in range(4):
                act.wait_ge(S("sub_out"), h + 1)
                act.activation(HH[:, 4 + h, :], OUN[:, h, :], ACT.Copy).then_inc(S("sub_high"), 1)
            for g, s in run("evo"):
                to(g + 1)
                for j in range(2):
                    act.wait_ge(*bank_full(g, j))
                    act.activation(Y[:, 2 * s + j, :], PS[j][:, :], ACT.Copy).then_inc(S("y_evac0"), 1)
                    to(g + 2, j)
                for j in range(2):
                    act_square(act, N["n1"], 2 * s + j)
            act_root(act, N["n1"])
            act_squares(act, N["n2"])
            act_root(act, N["n2"])
            act_modulate(act, N["n2"], 0, 1, 0)
            for g, s in run("up"):
                to(g + 1)
                if s is None:
                    act_mod(act, g)
                    continue
                if s % 2 == 0:
                    p = s // 2
                    for j in range(2):
                        act.wait_ge(*bank_full(g, j))
                        if p >= 2:
                            act.wait_ge(S("g_done"), 2 * (p - 2) + j + 1)
                        act.activation(Y[:, 2 * (p % 2) + j, :], PS[(4 * p + j) % 6][:, :], ACT.Silu)\
                           .then_inc(S("silu_done"), 1)
                        to(g + 2, j)
                else:
                    to(g + 2)
            act_table(act, ACT.Sqrt, 49)
            for k in range(FT):
                act.wait_ge(S("g_done"), k + 1)
                if k == 0:
                    act.wait_ge(*unit_used(of["up"][-1]))
                if k >= 4:
                    act.wait_ge(S("gk_used"), k - 3)
                act.activation(HH[:, k % 4, :], G[:, k, :], ACT.Copy).then_inc(S("gk_high"), 1)
                to(of["down"][k // 2] + 1, k % 2)
            act.wait_ge(S("gk_used"), FT)
            for m in range(4):
                act.activation(Y[:, m, :], PS[m][:, :], ACT.Copy).then_inc(S("ffn_evac"), 1)
            act_squares(act, N["n3"])
            act_root(act, N["n3"])
            act_squares(act, N["n4"])
            act_root(act, N["n4"])
            act_modulate(act, N["n4"], 1, 0, 0)
            for g, s in run("od"):
                to(g + 1)
                if s is None:
                    act_mod(act, g)
                    continue
                for j in range(2):
                    act.wait_ge(*bank_full(g, j))
                    b = PS[j]
                    if s < 2:
                        act.activation(QC[:, 2 * s + j, :], b[:, :SEQ], ACT.Copy).then_inc(S("od_evac"), 1)
                    elif s < 4:
                        act.activation(KC[:, 2 * (s - 2) + j, :], b[:, :], ACT.Copy).then_inc(S("od_evac"), 1)
                    elif s < 6:
                        dst = VCT[:, 2 * j:2 * j + 2, 256 * (s - 4):256 * (s - 3)]
                        act.activation(dst, b[:, :].rearrange("p (t n) -> p t n", t=2), ACT.Copy)\
                           .then_inc(S("od_evac"), 1)
                    elif s == 6:
                        act.activation(CQ[:, j, :], b[:, :SEQ], ACT.Copy).then_inc(S("od_evac"), 1)
                    elif j == 0:
                        act.activation(CKV, b[:, :], ACT.Copy).then_inc(S("od_evac"), 1)
                    else:
                        for h in range(4):
                            last = act.activation(KD[64:96, h, :], b[96:128, :], ACT.Copy)
                        last.then_inc(S("od_evac"), 1)
                    to(g + 2, j)
            act_squares(act, N["cq"])
            act_squares(act, N["ckv"])
            act_root(act, N["cq"])
            act_root(act, N["ckv"])
            for i in range(12):
                act.wait_ge(S("mla_full"), i + 1)
                b = PS[i % 2]
                if i < 4:
                    act.activation(QD[0:96, i, :], b[0:96, :SEQ], ACT.Copy).then_inc(S("mla_evac"), 1)
                elif i < 8:
                    act.activation(KD[0:64, i - 4, :], b[0:64, :], ACT.Copy).then_inc(S("mla_evac"), 1)
                else:
                    act.activation(VD[:, i - 8, :], b[:, :], ACT.Copy).then_inc(S("mla_evac"), 1)
            act.wait_ge(*unit_used(of["odo"][0] - 1))
            act_attention(act, 1, att1)
            act_table(act, ACT.Sqrt, 50)
            for g, s in run("odo"):
                to(g + 1)
                for j in range(2):
                    act.wait_ge(*bank_full(g, j))
                    act.activation(Y[:, 2 * s + j, 256:512], PS[j][:, :SEQ], ACT.Copy).then_inc(S("y_evac1"), 1)
                    to(g + 2, j)
                for j in range(2):
                    act_square(act, N["n5"], 2 * s + j)
            act_root(act, N["n5"])
            act_squares(act, N["n6"])
            act_root(act, N["n6"])
            act_modulate(act, N["n6"], 1, 1, 256, full=True)
            act_table(act, ACT.Exp, 51)
            for i in range(4):
                f, t = i // 2, i % 2
                act.wait_ge(S("htok_full"), f + 1)
                act.activation(HTH[:, t, 512 * f:512 * f + 512], PS[2 * t + f][:, :], ACT.Copy).then_inc(S("htok_high"), 1)
            act.wait_ge(S("top_diff"), 1)
            act.activation(RT[:, 64:66], RT[:, 66:68], ACT.Exp).then_inc(S("top_exp"), 1)

            def experts(b):
                g0 = b * NE * NU
                def xe_high(e, r):
                    act.wait_ge(S("xe_full"), e * 2 + (2 * (NE + 1) * b + r + 1))
                    act.activation(XEH[:, 4 * r:4 * r + 4, :], PS[XBANK[r]][:, :].rearrange("p (f n) -> p f n", f=4),
                                   ACT.Copy).then_inc(S("xe_high"), 1)

                def gt_high(e, j):
                    act.wait_ge(S("gt_full"), e * JE + (JE * NE * b + j + 1))
                    act.activation(GTH[:, j % 2, :], PS[6][:, :], ACT.Copy).then_inc(S("gt_high"), 1)

                def ye_high(e):
                    for c in range(2):
                        act.wait_ge(S("yg"), e * 2 + (2 * (NE + 1) * b + c + 1))
                        act.activation(YEH[:, 512 * c:512 * c + 512], YG[:, 2 * c:2 * c + 2, :], ACT.Copy)\
                           .then_inc(S("ye_high"), 1)

                xe_high(0, 0)
                xe_high(0, 1)
                for i in range(4):
                    act.wait_ge(S("pt_full"), 4 * b + i + 1)
                    act.activation(MPT[:, 2 * i + 1:2 * i + 3, :], PS[PBANK[i]][:, :].rearrange("p (e n) -> p e n", e=2),
                                   ACT.Copy).then_inc(S("mpt_done"), 1)
                with act.Fori(0, NE) as e:
                    for i, (kind, j) in enumerate(ORDER):
                        for u in (2 * i, 2 * i + 1):
                            act.wait_ge(S(f"eraw{u % NRAW}"), e * (16 * NU // NRAW)
                                        + (16 * (NE * NU // NRAW) * b + 16 * (u // NRAW + 1)))
                            act.wait_ge(S("e_slots"), e * NU + (g0 + u + 1))
                            act.activation(esplit(u)[0], RAW[:, u % NRAW, :], ACT.Copy).then_inc(S("e_high"), 1)
                        if i == 0:
                            ye_high(e)
                            continue
                        kind, j = ORDER[i - 1]
                        if kind == "a":
                            act.wait_ge(*item_used(b, e, i - 1))
                            act.wait_ge(S("ge_free"), e * JE + (JE * NE * b + j + 1))
                            act.activation(SIL, PS[2 * (j % 2)][:, :].rearrange("p (a n) -> p a n", a=2), ACT.Silu)\
                               .then_inc(S("esilu"), 1)
                            if j >= 1:
                                gt_high(e, j - 1)
                        if kind == "d" and j == JE - 2:
                            xe_high(e + 1, 0)
                            gt_high(e, JE - 1)
                            xe_high(e + 1, 1)
                ye_high(NE)

            experts(0)
            more = act.value_load(SM[0:1, 60:61].bitcast(I32))
            with act.If(more > 0):
                experts(1)
            act_squares(act, N["n7"])
            act_root(act, N["n7"])
            for i in range(4):
                act.wait_ge(S("out_full"), i + 1)
                act.activation(OUTT[:, i // 2, 512 * (i % 2):512 * (i % 2) + 512], PS[i][:, :], ACT.Copy)\
                   .then_inc(S("out_ready"), 1)

        @block.vector
        def _(dve):
            dve.memset(SCR[:, :].bitcast(F32), 0.0).then_inc(S("halves_clear"), 1)
            link(dve, dve.memset(SM[:, :], 0.0))
            dve.memset(SM[:, 0:1], EPS).then_inc(S("eps"), 1)
            dve.wait_ge(S("cols_full"), 2)
            dve.tensor_copy(BM[:, :], PS[0][:, 0:96]).then_inc(S("cols_done"), 1)
            dve.tensor_copy(VC[:, :], PS[1][:, 0:V_ALL]).then_inc(S("cols_done"), 1)
            dve.wait_ge(S("lambda_in"), 64)
            lam = OV[:, 256:512].rearrange("p (a n) -> p a n", a=4)
            for i in range(2):
                last = dve.tensor_tensor(lam[:, 2 * i, :], lam[:, 2 * i, :], lam[:, 2 * i + 1, :], ALU.mult)
            link(dve, last)
            for i in range(2):
                last = dve.tensor_reduce(SM[:, 2 + i:3 + i], lam[:, 2 * i, :], AX, ALU.add)
            last.then_inc(S("lam_dots"), 1)
            dve.wait_ge(S("lam_exp"), 1)
            link(dve, dve.tensor_tensor(SM[:, 6:7], SM[:, 5:6], SM[:, 4:5], ALU.subtract))
            link(dve, dve.tensor_scalar(SM[:, 1:2], SM[:, 6:7], -LAM_INIT, None, ALU.add))
            dve.wait_ge(S("cols_done"), 2)
            link(dve, dve.tensor_scalar(SM[:, 24:25], VC[:, V_SUB:V_SUB + 1], 1.0 - LAM_INIT, None, ALU.mult))
            dve.wait_ge(S("silu_high"), 1)
            scr = SCR[:, 0:4 * KT].rearrange("p (k c) -> p k c", c=4)
            dve.tensor_tensor(scr[:, :, 2:4], SC[:, :, :], scr[:, :, 0:2].bitcast(F32), ALU.subtract)\
               .then_inc(S("silu_low"), 1)
            to = upto(dve, dve_split)
            for f in range(KT):
                dve.wait_ge(S("x_full"), f + 1)
                dve.tensor_copy(X[:, f, :], PS[f % 2][:, :]).then_inc(S("x_in"), 1)
                to(f + 1)
            dve.wait_ge(S("direct_used"), 1)
            dve.wait_ge(S("x_in"), KT)
            dve.tensor_copy(WST, PS[2][:, :]).then_inc(S("wst"), 1)
            dve_rstd(dve, N["n0"])
            dve_mod_third(dve, 0)
            dve_affine(dve, 0, 0, 1.0, 8).then_inc(S("affine"), 1)
            dve_modulate(dve, N["n0"], 0)
            for g, s in run("ev"):
                to(g + 1)
                if s == 6:
                    dve_mod_third(dve, 1)
                    dve.wait_ge(S("sgu_b_in"), 16)
                if s in (6, 7):
                    dve_sgu(dve, 2 * s - 12)
                    dve_sgu(dve, 2 * s - 11)
                if s in (8, 9):
                    dve.wait_ge(S("angles_in"), 16)
                    dve_rope(dve, 0, range(4 * s - 32, 4 * s - 28))
                if s == 4:
                    dve.wait_ge(S("ev_evac"), 8)
                    for t in range(TT):
                        last = dve.bn_stats(Y[:, 5, 8 * t:8 * t + 6], SV[:, t, :])
                    link(dve, last)
                    for t in range(TT):
                        last = dve.bn_aggr(Y[:, 5, 64 + 2 * t:66 + 2 * t], Y[:, 5, 8 * t:8 * t + 6])
                    link(dve, last)
                    dve.tensor_copy(SM[:, 28:32], Y[:, 5, 64:72].rearrange("p (t c) -> p t c", c=2)[:, :, 1])\
                       .then_inc(S("sgu_var"), 1)
                if s == 5:
                    dve.wait_ge(S("sgu_std"), 1)
                    link(dve, dve.reciprocal(SM[:, 40:44], SM[:, 36:40]))
                    for t in range(TT):
                        last = dve.tensor_scalar(SV[:, t, :], SV[:, t, :], Y[:, 5, 64 + 2 * t:65 + 2 * t],
                                                 SM[:, 40 + t:41 + t], ALU.subtract, ALU.mult)
                    last.then_inc(S("sgu_v"), 1)
            dve_mod_third(dve, 2)
            dve_affine(dve, 0, 1, 0.0, 16)
            dve_affine(dve, 0, 2, 1.0, 32)
            dve_affine(dve, 0, 3, 0.0, 40).then_inc(S("affine"), 1)
            dve.wait_ge(*unit_used(of["ev"][-1]))
            for g in range(4):
                dve.wait_ge(S("sgu_high"), g + 1)
                dve.tensor_tensor(HL[:, g, :], U[:, g, :], HH[:, g, :].bitcast(F32), ALU.subtract)\
                   .then_inc(S("mix0"), 1)
            dve_attention(dve, 0, att0)
            for h in range(5):
                if h < 4:
                    n = N[f"sub{h}"]
                    dve_rstd(dve, n)
                    dve.scalar_tensor_tensor(OUN[:, h, :], OUN[:, h, :], SM[:, 24:25], n["rs"], ALU.mult, ALU.mult)\
                       .then_inc(S("sub_out"), 1)
                if h >= 1:
                    dve.wait_ge(S("sub_high"), h)
                    dve.tensor_tensor(HL[:, 3 + h, :], OUN[:, h - 1, :], HH[:, 3 + h, :].bitcast(F32), ALU.subtract)\
                       .then_inc(S("mix0"), 1)
            to(of["evo"][-1] + 1)
            dve_rstd(dve, N["n1"])
            dve_residual(dve, N["n1"], 0, 0, 0)
            dve.wait_ge(S("n1_res"), KT)
            dve_rstd(dve, N["n2"])
            dve_modulate(dve, N["n2"], 0)
            for g, s in run("up"):
                to(g + 1)
                if s is not None and s % 2 == 1:
                    p = s // 2
                    for j in range(2):
                        dve.wait_ge(*bank_full(g, j))
                        dve.wait_ge(S("silu_done"), 2 * p + j + 1)
                        dve.tensor_tensor(G[:, 2 * p + j, :], PS[(4 * p + 2 + j) % 6][:, :],
                                          Y[:, 2 * (p % 2) + j, :], ALU.mult).then_inc(S("g_done"), 1)
                        to(g + 2, j)
                if s == 19:
                    dve_mod_third(dve, 3)
                    dve_affine(dve, 1, 0, 1.0, 8).then_inc(S("affine"), 1)
            dve.wait_ge(S("g_done"), FT)
            for k in range(FT):
                dve.wait_ge(S("gk_high"), k + 1)
                dve.tensor_tensor(HL[:, k % 4, :], G[:, k, :], HH[:, k % 4, :].bitcast(F32), ALU.subtract)\
                   .then_inc(S("gk_low"), 1)
                to(of["down"][k // 2] + 1, k % 2)
            dve.wait_ge(S("gk_used"), FT)
            for m in range(4, 8):
                dve.tensor_copy(Y[:, m, :], PS[m][:, :]).then_inc(S("ffn_evac"), 1)
            dve_rstd(dve, N["n3"])
            dve.wait_ge(S("ffn_evac"), 8)
            dve_residual(dve, N["n3"], 0, 1, 0)
            dve.wait_ge(S("n3_res"), KT)
            dve_rstd(dve, N["n4"])
            dve_modulate(dve, N["n4"], 0)
            for g, s in run("od"):
                to(g + 1)
                if s == 6:
                    dve_mod_third(dve, 4)
            for name, gain, tiles in (("cq", V_GQ, 2), ("ckv", V_GKV, 1)):
                n = N[name]
                dve_rstd(dve, n)
                for t in range(tiles):
                    last = dve.scalar_tensor_tensor(n["src"](t), n["src"](t), VC[:, gain + t:gain + t + 1],
                                                    n["rs"][:, :n["width"]], ALU.mult, ALU.mult)
                last.then_inc(S("latent"), 1)
            dve_mod_third(dve, 5)
            dve_affine(dve, 1, 1, 0.0, 16)
            dve_affine(dve, 1, 2, 1.0, 32)
            dve_affine(dve, 1, 3, 0.0, 40).then_inc(S("affine"), 1)
            dve.wait_ge(S("affine"), 4)
            dve_rope(dve, 1)
            dve_attention(dve, 1, att1)
            to(ns - 1)
            dve_rstd(dve, N["n5"])
            dve_residual(dve, N["n5"], 1, 0, 256)
            dve.wait_ge(S("n5_res"), KT)
            dve_rstd(dve, N["n6"])
            dve_modulate(dve, N["n6"], 256, full=True)
            LG, MX = RT[:, 0:16].rearrange("p (t e) -> p t e", t=2), RT[:, 16:32].rearrange("p (t e) -> p t e", t=2)
            IX = RT[:, 32:48].bitcast(U32).rearrange("p (t e) -> p t e", t=2)
            IF = RT[:, 48:64].rearrange("p (t e) -> p t e", t=2)
            EXP, DIF, G1, G2 = RT[:, 64:66], RT[:, 66:68], RT[:, 68:70], RT[:, 70:72]
            SEL = RT[:, 80:96].rearrange("p (t e) -> p t e", t=2)
            GATE = RT[:, 96:112].rearrange("p (t e) -> p t e", t=2)
            T1 = RT[:, 112:128].rearrange("p (t e) -> p t e", t=2)
            T2 = RT[:, 128:144].rearrange("p (t e) -> p t e", t=2)
            POS = RT[:, 144:160].rearrange("p (t e) -> p t e", t=2)
            GSL = RT[:, 176:185]
            dve.wait_ge(S("direct_used"), len(direct_at))
            for t in range(2):
                last = dve.tensor_copy(LG[:, t, :], PS[4 + t][:, 0:8])
            link(dve, last)
            for t in range(2):
                last = dve.max(MX[:, t, :], LG[:, t, :])
            link(dve, last)
            for t in range(2):
                last = dve.max_index(IX[:, t, :], MX[:, t, :], LG[:, t, :])
            link(dve, last)
            dve.tensor_tensor(DIF, MX[:, :, 1], MX[:, :, 0], ALU.subtract).then_inc(S("top_diff"), 1)
            link(dve, dve.tensor_copy(IF, IX))
            iota8 = CON[:, C_IOTA:C_IOTA + NE]
            for t in range(2):
                dve.tensor_scalar(T1[:, t, :], iota8, IF[:, t, 0:1], None, ALU.is_equal)
                last = dve.tensor_scalar(T2[:, t, :], iota8, IF[:, t, 1:2], None, ALU.is_equal)
            link(dve, last)
            dve.tensor_tensor(SEL, T1, T2, ALU.add).then_inc(S("selected"), 1)
            for i in range(4):
                f, t = i // 2, i % 2
                dve.wait_ge(S("htok_high"), i + 1)
                dve.tensor_tensor(HTL[:, t, 512 * f:512 * f + 512], PS[2 * t + f][:, :],
                                  HTH[:, t, 512 * f:512 * f + 512].bitcast(F32), ALU.subtract)\
                   .then_inc(S("htok_low"), 1)
            dve.wait_ge(S("top_exp"), 1)
            link(dve, dve.tensor_scalar(G1, EXP, 1.0, None, ALU.add))
            link(dve, dve.reciprocal(G1, G1))
            link(dve, dve.tensor_tensor(G2, G1, EXP, ALU.mult))
            for t in range(2):
                last = dve.tensor_scalar(T1[:, t, :], T1[:, t, :], G1[:, t:t + 1], None, ALU.mult)
            link(dve, last)
            for t in range(2):
                last = dve.scalar_tensor_tensor(GATE[:, t, :], T2[:, t, :], G2[:, t:t + 1], T1[:, t, :],
                                                ALU.mult, ALU.add)
            link(dve, last)
            dve.wait_ge(S("positions"), 1)
            link(dve, dve.scalar_tensor_tensor(POS, PS[5][:, 0:16].rearrange("p (t e) -> p t e", t=2), 1.0, SEL,
                                          ALU.add, ALU.mult))
            link(dve, dve.tensor_scalar(POS, POS, -1.0, None, ALU.add))
            link(dve, dve.tensor_reduce(SM[:, 56:57], PS[5][:, 16:24], AX, ALU.max))
            link(dve, dve.tensor_scalar(SM[:, 57:58], SM[:, 56:57], float(CAP), None, ALU.is_gt))
            dve.tensor_copy(SM[:, 60:61].bitcast(I32), SM[:, 57:58]).then_inc(S("flag_ready"), 1)

            def experts(b):
                g0 = b * NE * NU
                if b:
                    dve.tensor_scalar(POS, POS, -float(CAP), None, ALU.add).then_inc(S("later_slots"), 1)
                    dve.wait_ge(S("later_slots"), 1)
                def xe_low(e, r):
                    dve.wait_ge(S("xe_high"), e * 2 + (2 * (NE + 1) * b + r + 1))
                    dve.tensor_tensor(XEL[:, 4 * r:4 * r + 4, :], PS[XBANK[r]][:, :].rearrange("p (f n) -> p f n", f=4),
                                      XEH[:, 4 * r:4 * r + 4, :].bitcast(F32), ALU.subtract)\
                       .then_inc(S("xe_low"), 1)

                for e in range(NE):
                    for t in range(2):
                        last = dve.tensor_scalar(MP[:, t, e, :], CON[:, C_IOTA:C_IOTA + P], POS[:, t, e:e + 1], None,
                                                 ALU.is_equal)
                    if e == 0:
                        last.then_inc(S("onehot_first"), 1)
                for t in range(2):
                    last = dve.tensor_scalar(MP[:, t, NE, :], CON[:, C_IOTA:C_IOTA + P], 0.0, None, ALU.mult)
                last.then_inc(S("onehot"), 1)
                if b == 0:
                    dve.memset(GSL[:, 0:1], 0.0)
                    dve.memset(MPT[:, 0, :].bitcast(F32), 0.0)
                xe_low(0, 0)
                xe_low(0, 1)
                if b == 0:
                    link(dve, dve.memset(YACC, 0.0))
                dve.wait_ge(S("gslot_full"), b + 1)
                dve.tensor_copy(GSL[:, 1:NE + 1], PS[5][:, 32:40]).then_inc(S("gslot"), 1)
                dve.wait_ge(S("gslot"), b + 1)
                if b == 0:
                    for c in range(2):
                        dve.memset(PS[4 + c][:, :], 0.0).then_inc(S("y_clear"), 1)
                    dve.wait_ge(S("y_clear"), 2)

                def gated(e):
                    dve.wait_ge(S("e_slots"), e * NU + (g0 + NSP_E))
                    for c in range(2):
                        dve.tensor_scalar(YG[:, 2 * c:2 * c + 2, :],
                                          PS[4 + c][:, :].rearrange("p (a n) -> p a n", a=2),
                                          GSL[:, e:e + 1] if isinstance(e, int) else GSL[:, bass.ds(e, 1)], None,
                                          ALU.mult).then_inc(S("yg"), 1)
                    for c in range(2):
                        dve.wait_ge(S("ye_high"), e * 2 + (2 * (NE + 1) * b + c + 1))
                        ysl = slice(512 * c, 512 * c + 512)
                        dve.tensor_tensor(YEL[:, ysl].rearrange("p (a n) -> p a n", a=2), YG[:, 2 * c:2 * c + 2, :],
                                          YEH[:, ysl].bitcast(F32).rearrange("p (a n) -> p a n", a=2), ALU.subtract)\
                           .then_inc(S("ye_low"), 1)

                def gather(e):
                    for r in range(4):
                        dve.wait_ge(S("comb_full"), e * 4 + (4 * (NE + 1) * b + r + 1))
                        acc = YACC[:, 2 * r:2 * r + 2, :]
                        dve.tensor_tensor(acc, PS[CBANK[r]][:, :].rearrange("p (f n) -> p f n", f=2), acc, ALU.add)\
                           .then_inc(S("comb_done"), 1)

                def gt_low(e, j):
                    dve.wait_ge(S("gt_high"), e * JE + (JE * NE * b + j + 1))
                    dve.tensor_tensor(GTL[:, j % 2, :], PS[6][:, :], GTH[:, j % 2, :].bitcast(F32), ALU.subtract)\
                       .then_inc(S("gt_low"), 1)

                with dve.Fori(0, NE) as e:
                    for i, (kind, j) in enumerate(ORDER):
                        for u in (2 * i, 2 * i + 1):
                            dve.wait_ge(S("e_high"), e * NU + (g0 + u + 1))
                            hi, lo = esplit(u)
                            dve.tensor_tensor(lo, RAW[:, u % NRAW, :], hi.bitcast(F32), ALU.subtract)\
                               .then_inc(S("e_low"), 1)
                        if i == 0:
                            gated(e)
                            continue
                        if i == 1:
                            gather(e)
                        kind, j = ORDER[i - 1]
                        if kind == "a" and j >= 1:
                            gt_low(e, j - 1)
                        if kind == "b":
                            dve.wait_ge(*item_used(b, e, i - 1))
                            dve.wait_ge(S("esilu"), e * JE + (JE * NE * b + j + 1))
                            if j >= 1:
                                dve.wait_ge(S("gt_full"), e * JE + (JE * NE * b + j))
                            dve.tensor_tensor(GE, PS[2 * (j % 2) + 1][:, :].rearrange("p (a n) -> p a n", a=2), SIL,
                                              ALU.mult).then_inc(S("ge_free"), 1)
                        if kind == "d" and j == JE - 2:
                            xe_low(e + 1, 0)
                            gt_low(e, JE - 1)
                            xe_low(e + 1, 1)
                gated(NE)
                gather(NE)

            experts(0)
            more = dve.value_load(SM[0:1, 60:61].bitcast(I32))
            with dve.If(more > 0):
                dve.wait_ge(S("comb_done"), 4 * (NE + 1))
                experts(1)
            dve.tensor_scalar(SM[:, 61:62], SM[:, 0:1], 1.0, None, ALU.mult).then_inc(S("moe_done"), 1)
            dve_rstd(dve, N["n7"])
            dve_residual(dve, N["n7"], 1, 1, 256)

        @block.tensor
        def _(pe):
            pe.wait_ge(S("consts_in"), 16)
            pe.wait_ge(S("rows_in"), 8 * 16)
            pe.transpose(PS[0][:, 0:96], OV[0:96, 0:P], CON[0:96, C_ID:C_ID + 96]).then_inc(S("cols_full"), 1)
            pe.transpose(PS[1][:, 0:V_ALL], OV[0:V_ALL, P:2 * P], CON[0:V_ALL, C_ID:C_ID + V_ALL])\
              .then_inc(S("cols_full"), 1)
            pe.wait_ge(S("raw0"), need[0])
            for g in range(4):
                last = pe.transpose(PS[2][:, P * g:P * g + P], raw_of(0)[:, P * g:P * g + P], ident)
            last.then_inc(S("direct_used"), 1)
            pe.wait_ge(S("tokens_in"), 32)
            pe.wait_ge(S("cols_done"), 2)
            for f in range(KT):
                if f >= 2:
                    pe.wait_ge(S("x_in"), f - 1)
                for t in range(TT):
                    src = Y[:, 2 * t:2 * t + 2, :].rearrange("p f n -> p (f n)")[:, f * P:f * P + P]
                    last = pe.transpose(PS[f % 2][:, P * t:P * t + P], src, ident)
                last.then_inc(S("x_full"), 1)
                if f == 0:
                    pe.wait_ge(S("silu_low"), 1)
                pe_mod(pe, f)
                if f >= 1:
                    pe_sum(pe, N["n0"], f - 1)
            pe_sum(pe, N["n0"], KT - 1)
            pe.wait_ge(*norm_root("n0"))
            pe_mod_third(pe, 0)
            for g, s in run("ev"):
                if s is None:
                    pe_mod(pe, g)
                    continue
                if s in (6, 9):
                    pe_mod_third(pe, 1 if s == 6 else 2)
                if s in (6, 7):
                    if s == 6:
                        pe.wait_ge(S("sgu_v"), 1)
                        pe.wait_ge(S("wst"), 1)
                    pe_sgu(pe, 2 * s - 12)
                    pe_sgu(pe, 2 * s - 11)
                if s in (8, 9):
                    pe_rope(pe, 0, lambda i: (S("ev_evac"), 9 + i), range(4 * s - 32, 4 * s - 28))
                kind = "t" if s in (2, 3, 8, 9) else "f"
                free = [(S("ev_evac"), 2 * s - 1 + j) if s else None for j in range(2)]
                gemm_unit(pe, g, kind, 0, PS, free, "n0_hl" if s == 0 else None)
            pe.wait_ge(S("ev_evac"), 20)
            pe.wait_ge(S("roped0"), 8)
            pe.wait_ge(S("mod_evac"), 3)
            pe.wait_ge(S("mod_rows"), 12)
            pe_attention(pe, 0, att0)
            for h in range(4):
                pe_sums(pe, N[f"sub{h}"])
            for g, s in run("evo"):
                free = [(S("y_evac0"), 2 * s - 1 + j) if s else None for j in range(2)]
                gemm_unit(pe, g, "f", 0, PS, free, "mix0" if s == 0 else None)
                pe_sum_pair(pe, N["n1"], s - 1)
            pe_sum_pair(pe, N["n1"], 3)
            pe.wait_ge(*norm_root("n1"))
            pe_sums(pe, N["n2"])
            for g, s in run("up"):
                if s is None:
                    pe_mod(pe, g)
                    continue
                if s == 18:
                    pe_mod_third(pe, 3)
                free = [None, None]
                for j in range(2):
                    f = 2 * s + j - 6
                    if f >= 0:
                        free[j] = (S("g_done" if f // 2 % 2 else "silu_done"), 2 * (f // 4) + f % 2 + 1)
                gemm_unit(pe, g, "f", 0, [PS[(2 * s + j) % 6] for j in range(2)], free, "n2_hl" if s == 0 else None)
            pe.wait_ge(S("mod_evac"), 4)
            pe.wait_ge(S("g_done"), FT)
            for d in range(FT // 2):
                s = of["down"][d]
                hi, lo = SPH[:, s % NSPLIT, :], SPL[:, s % NSPLIT, :]
                for r in range(2):
                    k = 2 * d + r
                    pe.wait_ge(S("split_low_done"), 2 * s + r + 1)
                    pe.wait_ge(S("gk_low"), k + 1)
                    for m in range(8):
                        a = slice(D * r + P * m, D * r + P * m + P)
                        last = three(pe, PS[m][:, :], hi[:, a], lo[:, a], HH[:, k % 4, :], HL[:, k % 4, :],
                                     k == 0, k == FT - 1)
                    last.then_inc(S("gk_used"), 1)
            pe.wait_ge(S("ffn_evac"), 8)
            pe_sums(pe, N["n3"])
            pe.wait_ge(*norm_root("n3"))
            pe_sums(pe, N["n4"])
            for g, s in run("od"):
                if s is None:
                    pe_mod(pe, g)
                    continue
                if s == 6:
                    pe_mod_third(pe, 4)
                kind, c0 = ("t", 0) if s in (4, 5) else ("f", 256 if s in (0, 1, 6) else 0)
                free = [(S("od_evac"), 2 * s - 1 + j) if s else None for j in range(2)]
                gemm_unit(pe, g, kind, c0, PS, free, "n4_hl" if s == 0 else None,
                          offs=(96, 128) if s == 7 else (0, 128))
            pe.wait_ge(S("mod_evac"), 5)
            pe_sums(pe, N["cq"])
            pe.wait_ge(S("mod_rows"), 24)
            pe_sums(pe, N["ckv"])
            pe.wait_ge(*norm_root("ckv"))
            pe_mod_third(pe, 5)
            r = latent_at
            pe.wait_ge(S(f"raw{r % NRAW}"), need[r])
            uq, ukv = raw_of(r)[:, 0:768].rearrange("p (k n) -> p k n", k=2), raw_of(r)[:, 768:1536]
            for i in range(12):
                if i == 0:
                    pe.wait_ge(S("latent"), 1)
                if i == 4:
                    pe.wait_ge(S("latent"), 2)
                if i >= 2:
                    pe.wait_ge(S("mla_evac"), i - 1)
                else:
                    pe.wait_ge(S("od_evac"), 16)
                b = PS[i % 2]
                if i < 4:
                    for k in range(2):
                        last = pe.matmul(b[0:96, :SEQ], uq[:, k, 96 * i:96 * i + 96], CQ[:, k, :],
                                         start=(k == 0), stop=(k == 1))
                elif i < 8:
                    c = 192 * (i - 4)
                    last = pe.matmul(b[0:64, :], ukv[:, c:c + 64], CKV, start=True, stop=True)
                else:
                    last = pe.matmul(b[:, :], CKV[:, P * (i - 8):P * (i - 7)],
                                     ukv.rearrange("p (h n) -> p h n", h=4)[:, :, 64:192], start=True, stop=True)
                last.then_inc(S("mla_full"), 1)
            pe_rope(pe, 1, lambda i: (S("mla_evac"), 12))
            pe.wait_ge(S("roped1"), 8)
            pe.wait_ge(S("mod_evac"), 6)
            pe_attention(pe, 1, att1)
            for g, s in run("odo"):
                free = [(S("y_evac1"), 2 * s - 1 + j) if s else None for j in range(2)]
                if s == 0:
                    pe.wait_ge(S("o_evac1"), len(att1) // 2)
                gemm_unit(pe, g, "f", 256, PS, free)
                pe_sum_pair(pe, N["n5"], s - 1)
            pe_sum_pair(pe, N["n5"], 3)
            pe.wait_ge(*norm_root("n5"))
            pe_sums(pe, N["n6"])
            r = direct_at[-1]
            pe.wait_ge(S(f"raw{r % NRAW}"), need[r])
            rw = raw_of(r)[:, 0:64].rearrange("p (k n) -> p k n", k=KT)
            pe.wait_ge(S("y_evac1"), 8)
            for k in range(KT):
                pe.wait_ge(S("n6_h"), k + 1)
                for t in range(2):
                    last = pe.matmul(PS[4 + t][:, 0:8], HFULL[:, k, P * t:P * t + P], rw[:, k, :],
                                     start=(k == 0), stop=(k == KT - 1))
                if k == KT - 1:
                    last.then_inc(S("direct_used"), 1)
                for t in range(2):
                    last = pe.transpose(PS[2 * t + k // 4][:, P * (k % 4):P * (k % 4) + P],
                                        HFULL[:, k, P * t:P * t + P], ident)
                if k % 4 == 3:
                    last.then_inc(S("htok_full"), 1)
            pe.wait_ge(S("selected"), 1)
            SEL = RT[:, 80:96].rearrange("p (t e) -> p t e", t=2)
            GATE = RT[:, 96:112].rearrange("p (t e) -> p t e", t=2)
            pe.matmul(PS[5][:, 0:8], tri, SEL[:, 0, :], start=True, stop=True)
            pe.matmul(PS[5][:, 8:16], tri, SEL[:, 1, :], start=True, stop=False)
            pe.matmul(PS[5][:, 8:16], ones, SEL[:, 0, :], start=False, stop=True)
            pe.matmul(PS[5][:, 16:24], ones, SEL[:, 0, :], start=True, stop=False)
            pe.matmul(PS[5][:, 16:24], ones, SEL[:, 1, :], start=False, stop=True).then_inc(S("positions"), 1)
            pe.wait_ge(S("htok_low"), 4)
            pe.sem_inc(S("e_slots"), NSP_E)
            pe.wait_ge(S("ident_r"), 1)

            def experts(b):
                g0 = b * NE * NU
                def slot_gates():
                    for e in range(NE):
                        for t in range(2):
                            last = pe.matmul(PS[5][:, 32 + e:33 + e], MP[:, t, e, :].bitcast(F32), GATE[:, t, e:e + 1],
                                             start=(t == 0), stop=(t == 1))
                    last.then_inc(S("gslot_full"), 1)

                def turn_onehots():
                    for i in range(4):
                        for e in range(2):
                            for t in range(2):
                                last = pe.matmul(PS[PBANK[i]][:, 256 * e + P * t:256 * e + P * t + P],
                                                 MP[:, t, 2 * i + e, :], IDR[:, :], start=True, stop=True)
                        last.then_inc(S("pt_full"), 1)

                def dispatch(e, r):
                    for f in range(4):
                        n = 0
                        for t in range(2):
                            for half in (HTH, HTL):
                                k = P * (4 * r + f)
                                rhs = MP[:, t, e, :] if isinstance(e, int) else \
                                    MP[:, t, bass.ds(e, 1), :].rearrange("p a n -> p (a n)")
                                last = pe.matmul(PS[XBANK[r]][:, P * f:P * f + P], half[:, t, k:k + P], rhs,
                                                 start=(n == 0), stop=(n == 3))
                                n += 1
                    last.then_inc(S("xe_full"), 1)

                if b:
                    pe.wait_ge(S("comb_done"), 4 * (NE + 1) * b)
                pe.wait_ge(S("onehot_first"), b + 1)
                dispatch(0, 0)
                dispatch(0, 1)
                pe.wait_ge(S("onehot"), b + 1)
                turn_onehots()
                slot_gates()
                pe.wait_ge(S("mpt_done"), 4 * b + 4)
                if b == 0:
                    pe.wait_ge(S("y_clear"), 2)
                pe.wait_ge(S("gslot"), b + 1)

                def up(e, i, xkind, j):
                    bank = PS[2 * (j % 2) + (xkind == "b")]
                    for q in range(2):
                        u = 2 * i + q
                        pe.wait_ge(S("e_low"), e * NU + (g0 + u + 1))
                        hi, lo = esplit(u)
                        for k in range(4):
                            a = slice(512 * k, 512 * k + 512)
                            kk = 4 * q + k
                            last = three(pe, bank[:, :], XEH[:, kk, :], XEL[:, kk, :], hi[:, a], lo[:, a],
                                         kk == 0, kk == KT - 1)
                        if q == 0:
                            last.then_inc(S("e_slots"), 1)
                    return last

                def turn(e, j):
                    pe.wait_ge(S("ge_free"), e * JE + (JE * NE * b + j + 2))
                    if j >= 1:
                        pe.wait_ge(S("gt_low"), e * JE + (JE * NE * b + j))
                    g = GE
                    for k in range(4):
                        src = g[:, k // 2, P * (k % 2):P * (k % 2) + P]
                        last = pe.transpose(PS[6][:, P * k:P * k + P], src, ident)
                    last.then_inc(S("gt_full"), 1)

                def down(e, i, j):
                    pe.wait_ge(S("gt_low"), e * JE + (JE * NE * b + j + 1))
                    for q in range(2):
                        u = 2 * i + q
                        pe.wait_ge(S("e_low"), e * NU + (g0 + u + 1))
                        hi, lo = esplit(u)
                        for k in range(2):
                            kk = 2 * q + k
                            gs = slice(P * kk, P * kk + P)
                            for c in range(2):
                                a = slice(D * k + 512 * c, D * k + 512 * c + 512)
                                last = three(pe, PS[4 + c][:, :], GTH[:, j % 2, gs], GTL[:, j % 2, gs], hi[:, a],
                                             lo[:, a], j == 0 and kk == 0, j == JE - 1 and kk == 3)
                        if q == 0:
                            last.then_inc(S("e_slots"), 1)
                    return last

                def combine(e):
                    for r in range(4):
                        pe.wait_ge(S("ye_low"), e * 2 + (2 * (NE + 1) * b + r // 2 + 1))
                        for f in range(2):
                            k = P * (2 * r + f)
                            o = PS[CBANK[r]][:, 256 * f:256 * f + 256]
                            rhs = MPT[:, e, :] if isinstance(e, int) else \
                                MPT[:, bass.ds(e, 1), :].rearrange("p a n -> p (a n)")
                            pe.matmul(o, YEH[:, k:k + P], rhs, start=True, stop=False)
                            last = pe.matmul(o, YEL[:, k:k + P], rhs, start=False, stop=True)
                        last.then_inc(S("comb_full"), 1)

                with pe.Fori(0, NE) as e:
                    pe.wait_ge(S("xe_low"), e * 2 + (2 * (NE + 1) * b + 2))
                    for i, (kind, j) in enumerate(ORDER):
                        if kind == "a":
                            if j >= 2:
                                pe.wait_ge(S("ge_free"), e * JE + (JE * NE * b + j))
                            if j == 1:
                                pe.wait_ge(S("comb_done"), e * 4 + (4 * (NE + 1) * b + 4))
                            up(e, i, "a", j).then_inc(S("e_slots"), 1)
                            if j == 0:
                                combine(e)
                            if j >= 1:
                                turn(e, j - 1)
                        elif kind == "b":
                            up(e, i, "b", j).then_inc(S("e_slots"), 1)
                        elif j < JE - 1:
                            down(e, i, j).then_inc(S("e_slots"), 1)
                            if j == JE - 2:
                                dispatch(e + 1, 0)
                                turn(e, JE - 1)
                                dispatch(e + 1, 1)
                        else:
                            down(e, i, j).then_inc(S("e_slots"), 1)
                combine(NE)

            pe.sem_inc(S("ge_free"), 1)
            experts(0)
            more = pe.value_load(SM[0:1, 60:61].bitcast(I32))
            with pe.If(more > 0):
                experts(1)
            pe_sums(pe, N["n7"])
            for i in range(4):
                pe.wait_ge(S("n7_res"), 4 * (i % 2) + 4)
                for k in range(4):
                    src = X[:, 4 * (i % 2) + k, CTX + P * (i // 2):CTX + P * (i // 2) + P]
                    last = pe.transpose(PS[i][:, P * k:P * k + P], src, ident)
                last.then_inc(S("out_full"), 1)


_INS = ["x", "c", "ctx", "c_ctx", "w_mod", "b_mod", "norm_g", "ev_w_in", "ev_w_out", "sgu_w", "sgu_b", "sgu_g",
        "diff_lq1", "diff_lk1", "diff_lq2", "diff_lk2", "diff_subln_g", "ffn_w1", "ffn_w3", "ffn_w2",
        "od_w_in", "od_w_out", "mla_gq", "mla_w_uq", "mla_gkv", "mla_w_ukv", "router_w",
        "moe_w1", "moe_w3", "moe_w2"]


def kernel(**inputs):
    import concourse.bacc as bacc
    from concourse.bass_utils import run_bass_kernel_spmd

    nc = bacc.Bacc("TRN2", target_bir_lowering=False, num_devices=1)
    arrays = {n: np.ascontiguousarray(inputs[n]) for n in _INS}
    used = np.asarray(inputs["na_rpb"])[0, :, 8 - ROWS:8 + ROWS - 1]
    arrays["rpb"] = np.ascontiguousarray(np.tile(used, (1, 1, REPEAT)))
    arrays["consts"], arrays["angles"] = constants()
    w = {}
    for n, a in arrays.items():
        w[n] = nc.dram_tensor(f"in_{n}", a.shape, mybir.dt.from_np(a.dtype), kind="ExternalInput").ap()
    out = nc.dram_tensor("out_0", (1, SEQ, D), F32, kind="ExternalOutput").ap()
    trunk(nc, w, out)
    r = run_bass_kernel_spmd(nc, [{f"in_{n}": a for n, a in arrays.items()}], core_ids=[0])
    return r.results[0]["out_0"]
```
